# Optimizing a Trainium2 kernel written in Bass

```python
import jax
import jax.numpy as jnp
from jax import lax
import numpy as np

D_MODEL = 1024
BATCH = 1
SEQ = 512
DEPTH = 2

MEM_LEN = 256
EPS = 1e-6
N_EVEN = (DEPTH + 1) // 2
N_ODD = DEPTH // 2

HEAD_DIM = 64
SWA_Q_HEADS = (D_MODEL // 2) // HEAD_DIM
SWA_KV_HEADS = SWA_Q_HEADS // 4
WINDOW = 128
SWA_Q_COLS = SWA_Q_HEADS * HEAD_DIM
SWA_KV_COLS = SWA_KV_HEADS * HEAD_DIM
SWA_COLS = SWA_Q_COLS + 2 * SWA_KV_COLS

RWKV_HEADS = (D_MODEL // 2) // HEAD_DIM
RWKV_WIDTH = RWKV_HEADS * HEAD_DIM
RWKV_DECAY_RANK = 64
RWKV_A_RANK = 64
RWKV_GATE_RANK = 128
RWKV_COLS = 3 * RWKV_WIDTH + RWKV_DECAY_RANK + RWKV_A_RANK + RWKV_GATE_RANK
RWKV_LN_EPS = 64e-5
EVEN_IN_COLS = SWA_COLS + RWKV_COLS
EVEN_MIX_WIDTH = SWA_Q_COLS + RWKV_WIDTH

GLA_HEADS = 4
GLA_KEY_WIDTH = D_MODEL // 2
GLA_VAL_WIDTH = D_MODEL
GLA_DK = GLA_KEY_WIDTH // GLA_HEADS
GLA_DV = GLA_VAL_WIDTH // GLA_HEADS
GLA_GATE_RANK = 16
GLA_GATE_NORM = 16.0
GLA_CHUNK = 64
ODD_IN_COLS = 2 * GLA_KEY_WIDTH + 2 * GLA_VAL_WIDTH + GLA_GATE_RANK

XA_HEADS = 4
XA_HEAD_DIM = 128
XA_WIDTH = XA_HEADS * XA_HEAD_DIM

MOE_GROUPS = 4
MOE_EXPERTS_PER_GROUP = 8
MOE_EXPERTS = MOE_GROUPS * MOE_EXPERTS_PER_GROUP
MOE_TOPK = 2
MOE_FF = 512
MOE_BLOCK = 128

kernel_name = 'hybrid_swa_rwkv7_gla_hmoe_trunk'

def rmsnorm(x, g, eps=EPS):
    xf = x.astype(jnp.float32)
    y = xf * lax.rsqrt(jnp.mean(xf * xf, axis=-1, keepdims=True) + eps)
    return (y * g.astype(jnp.float32)).astype(x.dtype)

def swa_with_sinks(q, k, v, sinks):
    B, S, HQ, Dh = q.shape
    HKV = k.shape[2]
    G = HQ // HKV
    W = WINDOW
    nb = S // W
    qb = q.astype(jnp.float32).reshape(B, nb, W, HKV, G, Dh)

    def band(t):
        tp = jnp.pad(t.astype(jnp.float32), ((0, 0), (W, 0), (0, 0), (0, 0))).reshape(B, nb + 1, W, HKV, Dh)
        return jnp.concatenate([tp[:, :-1], tp[:, 1:]], axis=2)

    kb, vb = band(k), band(v)
    s = jnp.einsum('bnqhgd,bnkhd->bnhgqk', qb, kb) * (Dh ** -0.5)
    qpos = jnp.arange(W)[:, None] + W
    kpos = jnp.arange(2 * W)[None, :]
    rel = qpos - kpos
    gkey = jnp.arange(nb)[:, None, None] * W + kpos[None] - W
    valid = (rel >= 0)[None] & (rel < W)[None] & (gkey >= 0)
    s = jnp.where(valid[None, :, None, None], s, -jnp.inf)
    sink = sinks.astype(jnp.float32).reshape(1, 1, HKV, G, 1, 1)
    m = jnp.maximum(jnp.max(s, axis=-1, keepdims=True), sink)
    pr = jnp.exp(s - m)
    den = jnp.sum(pr, axis=-1, keepdims=True) + jnp.exp(sink - m)
    o = jnp.einsum('bnhgqk,bnkhd->bnqhgd', pr / den, vb)
    return o.reshape(B, S, HQ * Dh)

def rwkv7_scan(r, decay, k, v, a_vec, b_vec):
    B, S, H, N = r.shape

    def step(state, inp):
        r_t, w_t, k_t, v_t, a_t, b_t = inp
        sa = jnp.einsum('bhvk,bhk->bhv', state, a_t)
        state = state * w_t[:, :, None, :] + sa[..., None] * b_t[:, :, None, :] + v_t[..., None] * k_t[:, :, None, :]
        y = jnp.einsum('bhvk,bhk->bhv', state, r_t)
        return state, y

    xs = tuple(jnp.moveaxis(t, 1, 0) for t in (r, decay, k, v, a_vec, b_vec))
    _, ys = lax.scan(step, jnp.zeros((B, H, N, N), jnp.float32), xs)
    return jnp.moveaxis(ys, 0, 1)

def rwkv7_time_mix(p, mu, w0, w2, a0, a2, g2, k_k, k_a, r_k, lnx_w, lnx_b):
    B, S, _ = p.shape
    C = RWKV_WIDTH
    p = p.astype(jnp.float32)
    p_prev = jnp.pad(p, ((0, 0), (1, 0), (0, 0)))[:, :-1]
    p = p + (p_prev - p) * mu
    r = p[..., :C]
    k = p[..., C:2 * C]
    v = p[..., 2 * C:3 * C]
    o = 3 * C
    xw = p[..., o:o + RWKV_DECAY_RANK]
    o += RWKV_DECAY_RANK
    xa = p[..., o:o + RWKV_A_RANK]
    o += RWKV_A_RANK
    xg = p[..., o:]
    w = -jax.nn.softplus(-(w0 + jnp.tanh(xw) @ w2)) - 0.5
    decay = jnp.exp(-jnp.exp(w))
    a = jax.nn.sigmoid(a0 + xa @ a2)
    g = jax.nn.sigmoid(xg) @ g2
    kk = (k * k_k).reshape(B, S, RWKV_HEADS, HEAD_DIM)
    kk = kk / jnp.maximum(jnp.sqrt(jnp.sum(kk * kk, axis=-1, keepdims=True)), 1e-12)
    k = k * (1.0 + (a - 1.0) * k_a)

    def heads(t):
        return t.reshape(B, S, RWKV_HEADS, HEAD_DIM)

    r, k, v, decay, a = heads(r), heads(k), heads(v), heads(decay), heads(a)
    y = rwkv7_scan(r, decay, k, v, -kk, kk * a)
    mean = jnp.mean(y, axis=-1, keepdims=True)
    var = jnp.mean(jnp.square(y - mean), axis=-1, keepdims=True)
    y = ((y - mean) * lax.rsqrt(var + RWKV_LN_EPS)).reshape(B, S, C) * lnx_w + lnx_b
    bonus = jnp.sum(r * k * r_k, axis=-1, keepdims=True) * v
    y = y + bonus.reshape(B, S, C)
    return y * g

def even_mixer(h, w_in, sinks, mu, w0, w2, a0, a2, g2, k_k, k_a, r_k, lnx_w, lnx_b, w_out):
    B, S, _ = h.shape
    p = h @ w_in
    q = p[..., :SWA_Q_COLS].reshape(B, S, SWA_Q_HEADS, HEAD_DIM)
    k = p[..., SWA_Q_COLS:SWA_Q_COLS + SWA_KV_COLS].reshape(B, S, SWA_KV_HEADS, HEAD_DIM)
    v = p[..., SWA_Q_COLS + SWA_KV_COLS:SWA_COLS].reshape(B, S, SWA_KV_HEADS, HEAD_DIM)
    o_a = swa_with_sinks(q, k, v, sinks).astype(h.dtype)
    o_b = rwkv7_time_mix(p[..., SWA_COLS:], mu, w0, w2, a0, a2, g2, k_k, k_a, r_k, lnx_w, lnx_b).astype(h.dtype)
    return jnp.concatenate([o_a, o_b], axis=-1) @ w_out

def gla_chunked(q, k, v, gk):
    B, S, _ = q.shape
    H, C = GLA_HEADS, GLA_CHUNK
    nc = S // C

    def chunks(t, d):
        return t.reshape(B, nc, C, H, d).transpose(1, 0, 3, 2, 4)

    qc, kc, gc = chunks(q, GLA_DK), chunks(k, GLA_DK), chunks(gk, GLA_DK)
    vc = chunks(v, GLA_DV)
    causal = jnp.tril(jnp.ones((C, C), dtype=bool))

    def step(state, inp):
        qi, ki, vi, gi = inp
        b = jnp.cumsum(gi, axis=2)
        o_inter = jnp.einsum('bhcd,bhde->bhce', qi * jnp.exp(b), state)
        diff = b[:, :, :, None, :] - b[:, :, None, :, :]
        diff = jnp.where(causal[:, :, None], diff, -jnp.inf)
        att = jnp.einsum('bhid,bhjd,bhijd->bhij', qi, ki, jnp.exp(diff))
        o_intra = jnp.einsum('bhij,bhje->bhie', att, vi)
        b_last = b[:, :, -1:, :]
        state = state * jnp.exp(b_last)[:, :, 0, :, None] + jnp.einsum('bhcd,bhce->bhde', ki * jnp.exp(b_last - b), vi)
        return state, o_inter + o_intra

    _, oc = lax.scan(step, jnp.zeros((B, H, GLA_DK, GLA_DV), jnp.float32), (qc, kc, vc, gc))
    return oc.transpose(1, 0, 3, 2, 4).reshape(B, S, H, GLA_DV)

def odd_mixer(h, w_in, gate_up, gate_b, onorm, w_out):
    B, S, _ = h.shape
    KW, VW, R = GLA_KEY_WIDTH, GLA_VAL_WIDTH, GLA_GATE_RANK
    p = h @ w_in
    q = p[..., :KW].astype(jnp.float32) * (GLA_DK ** -0.5)
    k = p[..., KW:2 * KW].astype(jnp.float32)
    v = p[..., 2 * KW:2 * KW + VW].astype(jnp.float32)
    gd = p[..., 2 * KW + VW:2 * KW + VW + R]
    og = p[..., 2 * KW + VW + R:].astype(jnp.float32)
    gk = jax.nn.log_sigmoid((gd @ gate_up + gate_b).astype(jnp.float32)) / GLA_GATE_NORM
    o = gla_chunked(q, k, v, gk)
    o = rmsnorm(o, onorm).reshape(B, S, VW) * jax.nn.silu(og)
    return o.astype(h.dtype) @ w_out

def memory_kv(mem, mem_norm, wk, wv):
    B, M, _ = mem.shape
    m = rmsnorm(mem, mem_norm)
    mk = (m @ wk).reshape(B, M, XA_HEADS, XA_HEAD_DIM)
    mv = (m @ wv).reshape(B, M, XA_HEADS, XA_HEAD_DIM)
    return mk, mv

def cross_attention(h, mk, mv, wq, wo):
    B, S, _ = h.shape
    q = (h @ wq).reshape(B, S, XA_HEADS, XA_HEAD_DIM).astype(jnp.float32)
    s = jnp.einsum('bshd,bmhd->bhsm', q, mk.astype(jnp.float32)) * (XA_HEAD_DIM ** -0.5)
    pr = jax.nn.softmax(s, axis=-1)
    o = jnp.einsum('bhsm,bmhd->bshd', pr, mv.astype(jnp.float32)).reshape(B, S, XA_WIDTH)
    return o.astype(h.dtype) @ wo

def hierarchical_moe(h, w_group, b_group, w_expert, b_expert, w1, w3, w2):
    B, S, D = h.shape
    T = B * S
    hf = h.reshape(T, D)
    g_logits = (hf @ w_group).astype(jnp.float32) + b_group.astype(jnp.float32)
    g_prob = jax.nn.softmax(g_logits, axis=-1)
    _, g_top = lax.top_k(g_logits, 1)
    p_group = jnp.take_along_axis(g_prob, g_top, axis=-1)
    e_logits = ((hf @ w_expert).astype(jnp.float32) + b_expert.astype(jnp.float32)).reshape(T, MOE_GROUPS, MOE_EXPERTS_PER_GROUP)
    idx = jnp.broadcast_to(g_top[:, :, None], (T, 1, MOE_EXPERTS_PER_GROUP))
    e_in = jnp.take_along_axis(e_logits, idx, axis=1)[:, 0]
    e_prob = jax.nn.softmax(e_in, axis=-1)
    top_p, top_i = lax.top_k(e_prob, MOE_TOPK)
    gate = p_group * top_p / jnp.sum(top_p, axis=-1, keepdims=True)
    expert = g_top * MOE_EXPERTS_PER_GROUP + top_i

    A = T * MOE_TOPK
    P = A + MOE_EXPERTS * MOE_BLOCK
    NB = P // MOE_BLOCK
    e_flat = expert.reshape(A)
    order = jnp.argsort(e_flat)
    e_s = e_flat[order]
    tok_s = (order // MOE_TOPK).astype(jnp.int32)
    w_s = gate.reshape(A)[order]
    counts = jnp.bincount(e_flat, length=MOE_EXPERTS)
    starts = jnp.cumsum(counts) - counts
    padded = (counts + MOE_BLOCK - 1) // MOE_BLOCK * MOE_BLOCK
    pends = jnp.cumsum(padded)
    pstarts = pends - padded
    dest = pstarts[e_s] + jnp.arange(A) - starts[e_s]
    buf_tok = jnp.zeros((P,), jnp.int32).at[dest].set(tok_s)
    buf_w = jnp.zeros((P,), jnp.float32).at[dest].set(w_s)
    block_e = jnp.minimum(jnp.searchsorted(pends, jnp.arange(NB) * MOE_BLOCK, side='right'), MOE_EXPERTS - 1)
    xb = hf[buf_tok].reshape(NB, MOE_BLOCK, D)

    def expert_block(args):
        xe, e = args
        return (jax.nn.silu(xe @ w1[e]) * (xe @ w3[e])) @ w2[e]

    yb = lax.map(expert_block, (xb, block_e)).reshape(P, D)
    y = jnp.zeros((T, D), jnp.float32).at[buf_tok].add(yb.astype(jnp.float32) * buf_w[:, None])
    return y.astype(h.dtype).reshape(B, S, D)

def setup_inputs(seed: int = 0) -> dict:
    key = jax.random.key(seed)
    ks = iter(jax.random.split(key, 64))
    D = D_MODEL

    def nrm(shape, scale):
        return jax.random.normal(next(ks), shape, jnp.float32) * scale

    def unif(shape, lo, hi):
        return jax.random.uniform(next(ks), shape, jnp.float32, lo, hi)

    def gain(shape):
        return 1.0 + nrm(shape, 0.02)

    return {
        'x': nrm((BATCH, SEQ, D), 1.0),
        'mem': nrm((BATCH, MEM_LEN, D), 1.0),
        'norm_mix': gain((DEPTH, D)),
        'norm_xattn': gain((DEPTH, D)),
        'norm_moe': gain((DEPTH, D)),
        'norm_final': gain((D,)),
        'ev_w_in': nrm((N_EVEN, D, EVEN_IN_COLS), D ** -0.5),
        'ev_sinks': nrm((N_EVEN, SWA_Q_HEADS), 0.5),
        'ev_mu': unif((N_EVEN, RWKV_COLS), 0.0, 1.0),
        'ev_w0': unif((N_EVEN, RWKV_WIDTH), -4.0, 0.0),
        'ev_w2': nrm((N_EVEN, RWKV_DECAY_RANK, RWKV_WIDTH), 0.1),
        'ev_a0': nrm((N_EVEN, RWKV_WIDTH), 0.1),
        'ev_a2': nrm((N_EVEN, RWKV_A_RANK, RWKV_WIDTH), 0.1),
        'ev_g2': nrm((N_EVEN, RWKV_GATE_RANK, RWKV_WIDTH), RWKV_GATE_RANK ** -0.5),
        'ev_k_k': 0.85 + nrm((N_EVEN, RWKV_WIDTH), 0.02),
        'ev_k_a': gain((N_EVEN, RWKV_WIDTH)),
        'ev_r_k': nrm((N_EVEN, RWKV_HEADS, HEAD_DIM), 0.1),
        'ev_lnx_w': gain((N_EVEN, RWKV_WIDTH)),
        'ev_lnx_b': nrm((N_EVEN, RWKV_WIDTH), 0.02),
        'ev_w_out': nrm((N_EVEN, EVEN_MIX_WIDTH, D), EVEN_MIX_WIDTH ** -0.5),
        'od_w_in': nrm((N_ODD, D, ODD_IN_COLS), D ** -0.5),
        'od_gate_up': nrm((N_ODD, GLA_GATE_RANK, GLA_KEY_WIDTH), GLA_GATE_RANK ** -0.5),
        'od_gate_b': nrm((N_ODD, GLA_KEY_WIDTH), 0.1),
        'od_onorm': gain((N_ODD, GLA_DV)),
        'od_w_out': nrm((N_ODD, GLA_VAL_WIDTH, D), GLA_VAL_WIDTH ** -0.5),
        'mem_norm': gain((D,)),
        'mem_wk': nrm((D, XA_WIDTH), D ** -0.5),
        'mem_wv': nrm((D, XA_WIDTH), D ** -0.5),
        'xa_wq': nrm((DEPTH, D, XA_WIDTH), D ** -0.5),
        'xa_wo': nrm((DEPTH, XA_WIDTH, D), XA_WIDTH ** -0.5),
        'moe_w_group': nrm((DEPTH, D, MOE_GROUPS), D ** -0.5),
        'moe_b_group': nrm((DEPTH, MOE_GROUPS), 0.01),
        'moe_w_expert': nrm((DEPTH, D, MOE_EXPERTS), D ** -0.5),
        'moe_b_expert': nrm((DEPTH, MOE_EXPERTS), 0.01),
        'moe_w1': nrm((DEPTH, MOE_EXPERTS, D, MOE_FF), D ** -0.5),
        'moe_w3': nrm((DEPTH, MOE_EXPERTS, D, MOE_FF), D ** -0.5),
        'moe_w2': nrm((DEPTH, MOE_EXPERTS, MOE_FF, D), MOE_FF ** -0.5),
    }

def reference(x, mem, norm_mix, norm_xattn, norm_moe, norm_final,
              ev_w_in, ev_sinks, ev_mu, ev_w0, ev_w2, ev_a0, ev_a2, ev_g2, ev_k_k, ev_k_a, ev_r_k,
              ev_lnx_w, ev_lnx_b, ev_w_out,
              od_w_in, od_gate_up, od_gate_b, od_onorm, od_w_out,
              mem_norm, mem_wk, mem_wv, xa_wq, xa_wo,
              moe_w_group, moe_b_group, moe_w_expert, moe_b_expert, moe_w1, moe_w3, moe_w2):
    mk, mv = memory_kv(mem, mem_norm, mem_wk, mem_wv)
    for layer in range(DEPTH):
        i = layer // 2
        h = rmsnorm(x, norm_mix[layer])
        if layer % 2 == 0:
            mix = even_mixer(h, ev_w_in[i], ev_sinks[i], ev_mu[i], ev_w0[i], ev_w2[i], ev_a0[i], ev_a2[i],
                             ev_g2[i], ev_k_k[i], ev_k_a[i], ev_r_k[i], ev_lnx_w[i], ev_lnx_b[i], ev_w_out[i])
        else:
            mix = odd_mixer(h, od_w_in[i], od_gate_up[i], od_gate_b[i], od_onorm[i], od_w_out[i])
        x = x + mix
        x = x + cross_attention(rmsnorm(x, norm_xattn[layer]), mk, mv, xa_wq[layer], xa_wo[layer])
        x = x + hierarchical_moe(rmsnorm(x, norm_moe[layer]), moe_w_group[layer], moe_b_group[layer],
                                 moe_w_expert[layer], moe_b_expert[layer], moe_w1[layer], moe_w3[layer], moe_w2[layer])
    return rmsnorm(x, norm_final)


_drawn_inputs = setup_inputs


def setup_inputs(seed=0):
    import zlib

    import numpy as np

    out = dict(_drawn_inputs(seed))
    spreads = {}
    factors = {'norm_xattn': 6.423,
     'norm_final': 7.305,
     'ev_sinks': 3.141,
     'ev_k_k': 3.892,
     'od_onorm': 2.845,
     'mem_norm': 3.427,
     'moe_b_expert': 6.77}
    for name, (base, spread) in spreads.items():
        noise = np.random.default_rng([zlib.crc32(name.encode()), seed]).standard_normal(out[name].shape)
        drawn = base * np.exp(spread * noise) if base else spread * noise
        out[name] = jnp.asarray(drawn.astype(out[name].dtype))
    for name, factor in factors.items():
        out[name] = (out[name] * factor).astype(out[name].dtype)
    return out
```

```python
from contextlib import ExitStack

import concourse.bass as bass
from concourse import mybir
from concourse.alu_op_type import AluOpType as ALU

F32 = mybir.dt.float32
I32 = mybir.dt.int32
U32 = mybir.dt.uint32
ACT = mybir.ActivationFunctionType
AX = mybir.AxisListType

P = 128
SEQ, D, MEM = 512, 1024, 256
KD = D // P
TT = SEQ // P
MT = MEM // P
HD = 64
CH = 128
NCH = SEQ // CH
LEVELS = 7
EPS = 1e-6
GN_EPS = 64e-5
DECAY = 0.6065306597126334
GATE_NORM = 16.0
NEG = -1e30
NG, NE, NX = 4, 8, 32
NR = NG + NX
BLK = 64
NBLK = 52
NROW = 3072
FF = 512

PARAMS = {}
NPAR = 0
for _name, _n in (("norm_mix", 16), ("norm_xattn", 16), ("norm_moe", 16), ("norm_final", 8), ("mem_norm", 8),
                  ("ev_mu", 14), ("ev_w0", 4), ("ev_a0", 4), ("ev_k_k", 4), ("ev_k_a", 4), ("ev_r_k", 4),
                  ("ev_lnx_w", 4), ("ev_lnx_b", 4), ("od_gate_b", 4), ("od_onorm", 2)):
    PARAMS[_name] = (NPAR, _n)
    NPAR += _n

LOADS = [("ev_q", 2), ("ev_kvx", 0), ("ev_r", 1), ("ev_k", 2), ("ev_v", 0), ("ev_o0", 1), ("ev_o1", 2),
         ("xk", 0), ("xv", 1), ("xq0", 2), ("xo0", 0),
         ("od_q", 0), ("od_k", 1), ("od_v0", 2), ("od_v1", 0), ("od_gd", 1), ("od_og0", 2), ("od_og1", 0),
         ("od_o0", 1), ("od_o1", 2), ("xq1", 0), ("xo1", 1)]
LAYER0_LOADS = 11
DMAS_OF = {"ev_q": 16, "ev_kvx": 2, "ev_o0": 3, "ev_o1": 3}


DONE = {"ev_q": ("proj_done", 4), "ev_kvx": ("proj_done", 8), "ev_r": ("proj_done", 12), "ev_k": ("proj_done", 16),
        "ev_v": ("proj_done", 20), "ev_o0": ("res_done", 8), "ev_o1": ("res_done", 8),
        "xk": ("proj_done", 32), "xv": ("proj_done", 34), "xq0": ("proj_done", 38), "xo0": ("res_done", 16),
        "od_q": ("proj_done", 42), "od_k": ("proj_done", 46), "od_v0": ("proj_done", 50), "od_v1": ("proj_done", 54),
        "od_gd": ("proj_done", 55), "od_og0": ("proj_done", 63), "od_og1": ("proj_done", 67),
        "od_o0": ("res_done", 24), "od_o1": ("res_done", 24), "xq1": ("proj_done", 71), "xo1": ("res_done", 32)}
PLAN_V = 5


def use_of(name):
    slot, loaded, former = dict(LOADS)[name], 0, None
    for n, sl in LOADS:
        if sl == slot:
            loaded += 16 * DMAS_OF.get(n, 1)
            if n == name:
                return slot, loaded, former
            former = DONE[n]


class Steps:

    def __init__(self, eng, sem):
        self.eng, self.sem, self.n, self.base = eng, sem, 0, 0

    def did(self, ins):
        ins.then_inc(self.sem, 1)
        self.n += 1

    def settle(self):
        self.eng.wait_ge(self.sem, self.base + self.n)

    def then(self, ins):
        self.did(ins)
        self.settle()

    def enter(self, i, per):
        self.outer, self.per = self.base + self.n, per
        self.base, self.n = i * per + self.outer, 0

    def leave(self, trips):
        assert self.n == self.per, (self.n, self.per)
        self.base, self.n = 0, self.outer + trips * self.per


def trunk(nc, a, hrows, yrows, out):
    with ExitStack() as ctx:
        KB = 1024
        cursor = [16512]

        def sb(name, shape, dt=F32, at=None):
            size = 4
            for n in shape[1:]:
                size *= n
            if at is None:
                at = cursor[0]
                cursor[0] += -(-size // 32) * 32
            return nc.alloc_sbuf_tensor_at(name, shape, dt, offset=at, align_bytes=4)

        XT = sb("XT", [P, KD, SEQ])
        HT_AT = cursor[0]
        HT = sb("HT", [P, KD, SEQ])
        RING = cursor[0]
        W = [sb(f"W{i}", [P, 4096]) for i in range(6)]
        W8 = [w[:, :].rearrange("p (k n) -> p k n", k=8) for w in W]
        W4 = [w[:, :].rearrange("p (k n) -> p k n", k=4) for w in W]
        WORK = cursor[0]
        cursor[0] += 72 * KB
        ident = sb("ident", [P, P])
        ones = sb("ones", [P, P])
        pair = sb("pair", [P, P])
        tri = sb("tri", [P, 2, P])
        level = sb("level", [P, LEVELS, P])
        par = sb("par", [P, NPAR])
        omu = sb("omu", [P, 14])
        oka = sb("oka", [P, 4])
        nwa = sb("nwa", [P, 8])
        bc = sb("bc", [P, 80])
        cst = sb("cst", [P, 2])
        small = sb("small", [P, 10, 8])
        assert cursor[0] <= nc.sbuf_usable_end, cursor[0]
        rs = sb("rs", [P, SEQ], at=WORK + 62 * KB)

        def col(name, k):
            c = PARAMS[name][0] + k
            return par[:, c:c + 1]

        xin = sb("xin", [P, TT, D], at=HT_AT)
        prow = sb("prow", [NPAR, P], at=WORK)
        brow = sb("brow", [1, 80], at=WORK + KB)
        Rt = sb("Rt", [P, 4, SEQ], at=WORK)
        Kt = sb("Kt", [P, 4, SEQ], at=WORK + 8 * KB)
        Vt = sb("Vt", [P, 4, SEQ], at=WORK + 16 * KB)
        KKt = sb("KKt", [P, 4, SEQ], at=WORK + 24 * KB)
        At = sb("At", [P, 4, SEQ], at=WORK + 32 * KB)
        SGt = sb("SGt", [P, 4, SEQ], at=WORK + 40 * KB)
        SO = sb("SO", [P, 4, SEQ], at=WORK + 48 * KB)
        X2 = sb("X2", [P, 2, SEQ], at=WORK + 56 * KB)
        shf = sb("shf", [P, 2, SEQ], at=WORK + 60 * KB)
        lora = sb("lora", [P, 2, SEQ], at=WORK + 64 * KB)
        S3 = RING + 48 * KB
        sqT = sb("sqT", [P, 4, SEQ], at=S3)
        skT = sb("skT", [P, 5 * P], at=S3 + 8 * KB)
        sv = sb("sv", [P, 5, P], at=S3 + 8 * KB + 2560)
        smask = sb("smask", [P, 2, 2 * P], at=S3 + 14 * KB)
        sp = sb("sp", [P, 8, 2 * P], at=S3 + 16 * KB)
        spT = sb("spT", [P, 16 * P], at=S3 + 24 * KB)
        AR = sb("AR", [P, 4, 2, CH], at=S3)
        BT = sb("BT", [P, 4, CH], at=S3 + 4 * KB)
        KT = sb("KT", [P, 4, CH], at=S3 + 6 * KB)
        TOK = sb("TOK", [P, 4, 512], at=S3 + 8 * KB)
        MA = sb("MA", [P, 4, 2, 2, CH], at=S3 + 16 * KB)
        MK = sb("MK", [P, 4, 2, 2, CH], at=S3 + 24 * KB)
        XI = [sb(f"XI{r}", [P, 4, CH], at=S3 + (32 + 8 * r) * KB) for r in range(2)]
        XJ = [sb(f"XJ{r}", [P, 4, CH], at=S3 + (34 + 8 * r) * KB) for r in range(2)]
        TL = [sb(f"TL{r}", [P, 4, CH], at=S3 + (36 + 8 * r) * KB) for r in range(2)]
        UL = [sb(f"UL{r}", [P, 4, CH], at=S3 + (38 + 8 * r) * KB) for r in range(2)]
        AKV = sb("AKV", [P, 512], at=HT_AT)
        WT = sb("WT", [P, 4, CH], at=HT_AT + 2 * KB)
        Us = sb("Us", [P, 4, 2, HD], at=HT_AT + 4 * KB)
        CS = sb("CS", [P, 4, CH], at=HT_AT + 6 * KB)
        Dp = sb("Dp", [P, 4, CH], at=WORK + 60 * KB)
        Em = sb("Em", [P, 4, CH], at=WORK + 62 * KB)
        St = sb("St", [P, 4, HD], at=WORK + 64 * KB)
        Sn = sb("Sn", [P, 4, HD], at=WORK + 65 * KB)
        VC = sb("VC", [P, 4, CH], at=WORK + 68 * KB)
        Ep = sb("Ep", [P, 4, CH], at=WORK + 70 * KB)
        Epp = Dp
        mid = small[:, 0, 0:4]
        pc = small[:, 1, 0:4]
        fc = small[:, 2, 0:4]
        smx = small[:, 3, :]
        snm = small[:, 4, :]
        ses = small[:, 5, :]
        sden = small[:, 6, :]
        srec = small[:, 7, :]
        gq = sb("gq", [P, 4, SEQ], at=WORK)
        gk = sb("gk", [P, 4, SEQ], at=WORK + 8 * KB)
        gv = sb("gv", [P, TT, D], at=WORK + 16 * KB)
        gl = sb("gl", [P, 4, SEQ], at=WORK + 32 * KB)
        og = sb("og", [P, KD, SEQ], at=WORK + 40 * KB)
        gup = sb("gup", [16, SEQ], at=WORK + 56 * KB)
        gdT = sb("gdT", [16, SEQ], at=WORK + 58 * KB)
        gz = sb("gz", [P, 4, SEQ], at=S3)
        ge = sb("ge", [P, 4, SEQ], at=S3 + 8 * KB)
        gqc = sb("gqc", [P, 4, CH], at=S3 + 16 * KB)
        gkc = sb("gkc", [P, 4, CH], at=S3 + 18 * KB)
        gkt = sb("gkt", [P, 512], at=S3 + 20 * KB)
        gat = sb("gat", [P, 4, CH], at=S3 + 22 * KB)
        gvc = sb("gvc", [P, D], at=S3 + 24 * KB)
        gcs = sb("gcs", [P, 4, CH], at=S3 + 28 * KB)
        gep = sb("gep", [P, 4, CH], at=S3 + 30 * KB)
        gem = sb("gem", [P, 4, CH], at=S3 + 32 * KB)
        gst = sb("gst", [P, 4, 256], at=S3 + 34 * KB)
        gsn = sb("gsn", [P, 4, 256], at=S3 + 38 * KB)
        gsq = sb("gsq", [P, KD, SEQ], at=WORK)
        grs = sb("grs", [P, 4, SEQ], at=WORK + 16 * KB)
        ogs = sb("ogs", [P, KD, SEQ], at=S3)
        mkT = sb("mkT", [P, 4, MEM], at=WORK + 64 * KB)
        mv = sb("mv", [P, MT, 512], at=WORK + 68 * KB)
        memin = sb("memin", [P, MT, D], at=WORK)
        memT = sb("memT", [P, KD, MEM], at=WORK + 8 * KB)
        memN = sb("memN", [P, KD, MEM], at=WORK + 16 * KB)
        xq = sb("xq", [P, 4, SEQ], at=WORK + 24 * KB)
        xo = sb("xo", [P, 4, SEQ], at=WORK + 32 * KB)
        xp = sb("xp", [P, 2, 4, MEM], at=WORK + 40 * KB)
        xpT = HT
        wr = sb("wr", [P, KD, NR], at=WORK)
        hk = sb("hk", [P, TT, D], at=WORK + 4 * KB)
        lg = sb("lg", [P, TT, NR], at=WORK + 20 * KB)
        M0 = WORK + 20 * KB + 1024
        glp = sb("glp", [P, TT, 8], at=M0)
        g8 = sb("g8", [P, TT, 8], at=M0 + 128)
        gi8 = sb("gi8", [P, TT, 8], U32, at=M0 + 256)
        ein = sb("ein", [P, TT, 8], at=M0 + 384)
        e8 = sb("e8", [P, TT, 8], at=M0 + 512)
        ei8 = sb("ei8", [P, TT, 8], U32, at=M0 + 640)
        gidx = sb("gidx", [P, TT], at=M0 + 768)
        ogh = sb("ogh", [P, TT, 4], at=M0 + 784)
        gex = sb("gex", [P, TT, 4], at=M0 + 848)
        pg = sb("pg", [P, TT], at=M0 + 912)
        dv = sb("dv", [P, TT], at=M0 + 928)
        ee = sb("ee", [P, TT], at=M0 + 944)
        gate = sb("gate", [P, TT, 2], at=M0 + 960)
        eid = sb("eid", [P, TT, 2], at=M0 + 992)
        M1 = M0 + 1024
        oh = sb("oh", [P, TT, 2, NX], at=M1)
        msk = sb("msk", [P, TT, NX], at=M1 + 1024)
        rk = sb("rk", [P, TT, NX], at=M1 + 1536)
        cn = sb("cn", [P, NX], at=M1 + 2048)
        nb = sb("nb", [P, NX], at=M1 + 2176)
        pend = sb("pend", [P, NX], at=M1 + 2304)
        pst = sb("pst", [P, NX], at=M1 + 2432)
        selr = sb("selr", [P, 8], at=M1 + 2560)
        selp = sb("selp", [P, 8], at=M1 + 2592)
        rq = sb("rq", [P, 8], at=M1 + 2624)
        blk = sb("blk", [P, 8], at=M1 + 2656)
        brk = sb("brk", [P, 8], at=M1 + 2688)
        sloti = sb("sloti", [P, 8], I32, at=M1 + 2720)
        nit = sb("nit", [P, 2], I32, at=M1 + 2752)
        nitf = sb("nitf", [P, 2], at=M1 + 2760)
        bei = sb("bei", [P, NBLK], I32, at=M1 + 2816)
        bef = sb("bef", [P, NBLK], at=M1 + 3072)
        idx = sb("idx", [BLK, NBLK], I32, at=M1 + 3328)
        io = sb("io", [P, 64], at=M1 + 3584)
        M2 = M1 + 3840
        io64 = sb("io64", [P, 8], at=M2)
        tokid = sb("tokid", [P, TT], at=M2 + 32)
        rhot = sb("rhot", [P, 8, BLK], at=M2 + 64)
        bhot = sb("bhot", [P, 8, NBLK], at=M2 + 64 + 2048)
        cmp = sb("cmp", [P, NBLK * NX], at=M2 + 64 + 4096)
        M3 = WORK + 38 * KB
        assert M2 + 64 + 4096 + 4 * NBLK * NX <= M3
        xg = [sb(f"xg{b}", [BLK, D], at=M3 + 4 * KB * b) for b in range(2)]
        xgT = [sb(f"xgT{b}", [P, KD, BLK], at=M3 + 8 * KB + 2 * KB * b) for b in range(2)]
        hs = [sb(f"hs{b}", [P, FF], at=M3 + 12 * KB + 2 * KB * b) for b in range(2)]
        sl = [sb(f"sl{b}", [P, 4, BLK], at=M3 + 16 * KB + KB * b) for b in range(2)]
        act_ = [sb(f"act{b}", [P, 4, BLK], at=M3 + 18 * KB + KB * b) for b in range(2)]
        ysb = [sb(f"ysb{b}", [P, FF], at=M3 + 20 * KB + 2 * KB * b) for b in range(2)]
        idc = [sb(f"idc{b}", [BLK, 1], I32, at=M1 + 3072 + 208 + 8 * b) for b in range(2)]
        yg = [sb(f"yg{n}", [P, D], at=S3 + 4 * KB * n) for n in range(8)]
        osb = sb("osb", [P, TT, D], at=WORK)

        ps = ctx.enter_context(nc.psum_tensor("ps", [P, 8, 512], F32))

        s = {n: ctx.enter_context(nc.semaphore(n)) for n in (
            "v_step", "a_step", "g_step",
            "consts", "par_in", "par_turned", "par_ready", "x_in", "x_turned", "lora_in",
            "xt_ready", "sq_ready", "sum_ready", "rstd_ready", "h_ready", "proj_done", "proj_taken", "res_done",
            "sm_scored", "sm_max", "sm_exp", "sm_norm", "sm_turned", "sm_pt", "sm_pv", "sm_out", 
            "shifted", "pre_v", "pre_a", "pre_p", "post_v", "post_a", "post_p",
            "ck_cs", "ck_exp", "ck_el", "ck_vc", "ck_turned", "ck_tok", "ck_mat", "ck_masked", "ck_y", "ck_y_in", "ck_s",
            "iv_tl", "iv_u", "iv_ul", "iv_v", "iv_x", "gst_read", "akv_done", "akv_in", "wt_done", "wt_in", "u_done", "u_in",
            "mem_in", "mem_turned", "gup_in",
            "wr_in", "plan_v", "plan_a", "plan_p", "plan_g", "h_turned", "h_taken", "h_stored",
            "xg_turned", "xgT_in", "hh_done", "hs_in", "hs_turned", "sl_in", "act_in", "y_done", "y_in",
            "gb_step", "zeros", "y_zeroed", "go", "y_back", "y_sum", "y_turned",
            "f_turned", "f_taken", "out_stored")}
        w_loaded = [ctx.enter_context(nc.semaphore(f"w_loaded{i}")) for i in range(3)]
        w13_in, w2_in, xg_in, y_stored = ([ctx.enter_context(nc.semaphore(f"{n}{b}")) for b in range(2)]
                                          for n in ("w13_in", "w2_in", "xg_in", "y_stored"))
        block = ctx.enter_context(nc.Block())

        @block.sync
        def _(sp):
            sources = {
                "ev_kvx": [(W8[0][:, :, 0:256], a["ev_w_in"][0][:, 512:768]), (W8[0][:, :, 256:512], a["ev_w_in"][0][:, 2304:2560])],
                "ev_r": [(W8[1], a["ev_w_in"][0][:, 768:1280])],
                "ev_k": [(W8[2], a["ev_w_in"][0][:, 1280:1792])],
                "ev_v": [(W8[0], a["ev_w_in"][0][:, 1792:2304])],
                "xk": [(W8[0], a["mem_wk"])], "xv": [(W8[1], a["mem_wv"])],
                "xq0": [(W8[2], a["xa_wq"][0])], "xq1": [(W8[0], a["xa_wq"][1])],
                "xo0": [(W4[0], a["xa_wo"][0])], "xo1": [(W4[1], a["xa_wo"][1])],
                "od_q": [(W8[0], a["od_w_in"][0][:, 0:512])], "od_k": [(W8[1], a["od_w_in"][0][:, 512:1024])],
                "od_v0": [(W8[2], a["od_w_in"][0][:, 1024:1536])], "od_v1": [(W8[0], a["od_w_in"][0][:, 1536:2048])],
                "od_gd": [(W8[1][:, :, 0:16], a["od_w_in"][0][:, 2048:2064])],
                "od_og0": [(W8[2], a["od_w_in"][0][:, 2064:2576])], "od_og1": [(W8[0], a["od_w_in"][0][:, 2576:3088])],
                "od_o0": [(W8[1], a["od_w_out"][0][:, 0:512])], "od_o1": [(W8[2], a["od_w_out"][0][:, 512:1024])],
            }
            sources["ev_q"] = [(W8[2].rearrange("p k (j g d) -> p k j g d", j=4, g=2)[:, k, :, g, :],
                                a["ev_w_in"][0][k * P:k * P + P, 256 * g:256 * g + 256].rearrange("p (j d) -> p j d", j=4))
                               for k in range(KD) for g in range(2)]
            for h, name in enumerate(("ev_o0", "ev_o1")):
                w = a["ev_w_out"][0][:, 512 * h:512 * h + 512]
                dst = W8[dict(LOADS)[name]]
                sources[name] = [(dst[0:64, 0:4, :], w[0:256, :].rearrange("(j d) n -> d j n", d=HD)),
                                 (dst[64:128, 0:4, :], w[256:512, :].rearrange("(j d) n -> d j n", d=HD)),
                                 (dst[:, 4:8, :], w[512:1024, :].rearrange("(k p) n -> p k n", p=P))]

            def load(name):
                slot, _, former = use_of(name)
                if former:
                    sp.wait_ge(s[former[0]], former[1])
                for dst, src in sources[name]:
                    if len(dst.shape) == 3 and len(src.shape) == 2:
                        src = src.rearrange("(k p) n -> p k n", p=P)
                    sp.dma_start(dst, src).then_inc(w_loaded[slot], 16)

            def experts(L, before):
                sp.wait_ge(s["plan_v"], PLAN_V * (L + 1))
                trips = sp.value_load(nit[0:1, 0:1], min_val=1, max_val=NROW // BLK // 2)
                sp.wait_ge(s["hh_done"], before + (L + 2))
                sp.sem_inc(s["go"], 1)
                with sp.Fori(0, trips) as i:
                    for b in range(2):
                        n = i * 2 + b
                        e = sp.value_load(bei[0:1, bass.ds(n, 1)], min_val=0, max_val=NX - 1)
                        w1, w3, w2 = (a[k][L][bass.ds(e, 1)][0].rearrange("(k p) n -> p k n", p=P) for k in ("moe_w1", "moe_w3", "moe_w2"))
                        sp.wait_ge(s["hh_done"], n + (before + L + 1))
                        sp.dma_start(W8[3 * b], w1).then_inc(w13_in[b], 16)
                        sp.dma_start(W8[3 * b + 1], w3).then_inc(w13_in[b], 16)
                        sp.wait_ge(s["y_done"], n + (before + L + 1))
                        sp.dma_start(W4[3 * b + 2], w2).then_inc(w2_in[b], 16)
                return trips

            for i, (name, _) in enumerate(LOADS[:LAYER0_LOADS]):
                if i == 3:
                    sp.wait_ge(s["zeros"], 1)
                    for q in range(NROW // (4 * P)):
                        sp.dma_start(yrows[q * 4 * P:(q + 1) * 4 * P, :].rearrange("(p r) d -> p (r d)", p=P), W[5][:, :]).then_inc(s["y_zeroed"], 16)
                load(name)
            before = experts(0, 0) * 2
            sp.wait_ge(s["y_done"], before + 2)
            for name, _ in LOADS[LAYER0_LOADS:]:
                load(name)
            experts(1, before)
            dst = out[0].rearrange("(t p) d -> t p d", p=P)
            for t in range(TT):
                sp.wait_ge(s["f_taken"], t + 1)
                sp.dma_start(dst[t], osb[:, t, :]).then_inc(s["out_stored"], 16)
            sp.wait_ge(s["out_stored"], 16 * TT)

        @block.gpsimd
        def _(pool):
            st = Steps(pool, s["g_step"])
            g = nc.gpsimd
            st.then(g.memset(ident[:, :], 0.0))
            st.then(g.affine_select(out=ident[:, :], in_=ident[:, :], compare_op=ALU.not_equal, fill=1.0, base=0,
                                    pattern=[[-1, P]], channel_multiplier=1))
            st.then(g.memset(ones[:, :], 1.0))
            st.then(g.memset(cst[:, 0:1], EPS))
            st.then(g.memset(cst[:, 1:2], GN_EPS))
            st.then(g.memset(pair[:, :], 0.0))
            for r in range(2):
                st.then(g.memset(pair[64 * r:64 * r + 64, 64 * r:64 * r + 64], 1.0))
            for v in range(2):
                st.then(g.memset(tri[:, v, :], 1.0))
                st.then(g.affine_select(out=tri[:, v, :], in_=tri[:, v, :], compare_op=ALU.is_ge, fill=0.0, base=v - 1,
                                        pattern=[[1, P]], channel_multiplier=-1))
            st.then(g.memset(level[:, :, :], 0.0))
            for l in range(LEVELS):
                h = 1 << l
                half = level[:, l, :].rearrange("p (b h w) -> p b h w", h=2, w=h)[:, :, 1, :]
                st.then(g.memset(half, 1.0))
                st.then(g.affine_select(out=half, in_=half, compare_op=ALU.is_ge, fill=0.0, base=0,
                                        pattern=[[-2 * h, P // (2 * h)], [0, h]], channel_multiplier=1))
                st.then(g.affine_select(out=half, in_=half, compare_op=ALU.is_ge, fill=0.0, base=h - 1,
                                        pattern=[[2 * h, P // (2 * h)], [0, h]], channel_multiplier=-1))
            st.then(g.memset(smask[:, :, :], 0.0))
            st.then(g.affine_select(out=smask[:, 1, 0:P], in_=smask[:, 1, 0:P], compare_op=ALU.is_ge, fill=NEG, base=-1,
                                    pattern=[[1, P]], channel_multiplier=-1))
            for v in range(2):
                st.then(g.affine_select(out=smask[:, v, P:2 * P], in_=smask[:, v, P:2 * P], compare_op=ALU.is_ge, fill=NEG,
                                        base=0, pattern=[[-1, P]], channel_multiplier=1))
            st.then(g.memset(smask[:, 0, 0:P], NEG))
            st.then(g.memset(skT[:, 0:P], 0.0))
            g.memset(sv[:, 0, :], 0.0).then_inc(s["consts"], 1)

            def even():
                with pool.Fori(0, NCH) as c:
                    pool.wait_ge(s["pre_v"], 2)
                    pool.wait_ge(s["ck_turned"], c * 4 + 1)
                    g.tensor_copy(VC[:, :, :], Vt[:, :, bass.ds(c * CH, CH)]).then_inc(s["ck_vc"], 1)

            def odd():
                with pool.Fori(0, NCH) as c:
                    pool.wait_ge(s["proj_taken"], DONE["od_v1"][1])
                    pool.wait_ge(s["ck_s"], c + NCH)
                    g.tensor_copy(gvc[:, :], gv[:, bass.ds(c, 1), :].rearrange("p a d -> p (a d)")).then_inc(s["ck_vc"], 1)

            def moe(L, before):
                pool.wait_ge(s["h_ready"], 8 * (4 + 3 * L))
                st.then(g.iota(io[:, :], pattern=[[1, 64]], base=0, channel_multiplier=0, allow_small_or_imprecise_dtypes=True))
                st.then(g.iota(io64[:, :], pattern=[[64, 8]], base=0, channel_multiplier=0, allow_small_or_imprecise_dtypes=True))
                g.iota(tokid[:, :], pattern=[[P, TT]], base=0, channel_multiplier=1,
                       allow_small_or_imprecise_dtypes=True).then_inc(s["plan_g"], 1)
                pool.wait_ge(s["plan_v"], PLAN_V * (L + 1))
                pool.wait_ge(s["h_stored"], 16 * TT * (L + 1))
                trips = pool.value_load(nit[0:1, 0:1], min_val=1, max_val=NROW // BLK // 2)

                def gather(column, b):
                    st2.then(g.tensor_copy(idc[b][:, :], column))
                    pool.sem_inc(s["go"], 1)
                    g.indirect_dma_start(out=xg[b][:, :], out_offset=None, in_=hrows[:, :],
                                         in_offset=bass.IndirectOffsetOnAxis(ap=idc[b][:, :], axis=0)).then_inc(xg_in[b], 16)

                st2 = Steps(pool, s["gb_step"])
                st2.base = before + L
                gather(idx[:, 0:1], 0)
                with pool.Fori(0, trips) as i:
                    st2.enter(i, 2)
                    for b in (1, 0):
                        n = i * 2 + (2 - b)
                        pool.wait_ge(s["xg_turned"], n + (before + L))
                        gather(idx[:, bass.ds(n, 1)], b)
                for b in range(2):
                    pool.wait_ge(y_stored[b], (trips * 2 + before) * 16 + 1)
                pool.wait_ge(xg_in[0], (trips + 1) * 16 + (before * 8 + 16 * L))
                pool.sem_inc(s["go"], 1)
                for n in range(8):
                    g.indirect_dma_start(out=yg[n][:, :], out_offset=None, in_=yrows[:, :],
                                         in_offset=bass.IndirectOffsetOnAxis(ap=sloti[:, n:n + 1], axis=0)).then_inc(s["y_back"], 16)
                return trips

            even()
            before = moe(0, 0) * 2
            odd()
            moe(1, before)

        @block.scalar
        def _(act):
            st = Steps(act, s["a_step"])
            sc = nc.scalar
            n = {"proj": 0, "norm": 0, "xt": 8}

            for sem in (s["ck_y_in"], y_stored[0], y_stored[1]):
                act.sem_inc(sem, 1)
            act.dma_start(xin[:, :, :], a["x"][0].rearrange("(t p) d -> p t d", p=P)).then_inc(s["x_in"], 16)
            for name, (c0, k) in PARAMS.items():
                src = a[name]
                while len(src.shape) > 1:
                    src = src.rearrange({2: "a b -> (a b)", 3: "a b c -> (a b c)"}[len(src.shape)])
                act.dma_start(prow[c0:c0 + k, :], src.rearrange("(r p) -> r p", p=P)).then_inc(s["par_in"], 16)
            act.dma_start(brow[0:1, 0:8], a["ev_sinks"]).then_inc(s["par_in"], 16)
            for L in range(2):
                o = 8 + NR * L
                act.dma_start(brow[0:1, o:o + NG], a["moe_b_group"][L:L + 1, :]).then_inc(s["par_in"], 16)
                act.dma_start(brow[0:1, o + NG:o + NR], a["moe_b_expert"][L:L + 1, :]).then_inc(s["par_in"], 16)
            act.dma_start(lora[0:64, 0, :], a["ev_w2"][0]).then_inc(s["lora_in"], 16)
            act.dma_start(lora[64:128, 0, :], a["ev_a2"][0]).then_inc(s["lora_in"], 16)
            act.dma_start(lora[:, 1, :], a["ev_g2"][0]).then_inc(s["lora_in"], 16)

            def norm(src, dst, width):
                for q in range(4):
                    sc.activation(dst[:, 2 * q:2 * q + 2, :], src[:, 2 * q:2 * q + 2, :], ACT.Square).then_inc(s["sq_ready"], 1)
                act.wait_ge(s["h_ready"], 8 * n["norm"])
                n["norm"] += 1
                act.wait_ge(s["sum_ready"], n["norm"])
                st.then(sc.activation(rs[:, 0:width], ps[:, 7, 0:width], ACT.Ln, bias=cst[:, 0:1], scale=1.0 / D))
                sc.activation(rs[:, 0:width], rs[:, 0:width], ACT.Exp, scale=-0.5).then_inc(s["rstd_ready"], 1)

            def take(dst, src=None, last=True, func=ACT.Copy, **k):
                act.wait_ge(s["proj_done"], n["proj"] + 1)
                if src is None:
                    src = ps[:, n["proj"] % 2, :]
                ins = sc.activation(dst, src, func, **k)
                if last:
                    ins.then_inc(s["proj_taken"], 1)
                    n["proj"] += 1

            def even():
                act.wait_ge(s["xt_ready"], 8)
                norm(XT, HT, SEQ)
                act.wait_ge(s["consts"], 1)
                for j in range(4):
                    take(sqT[:, j, :])
                take(skT[:, P:5 * P])
                take(sv[:, 1:5, :].rearrange("p t n -> p (t n)"))

                def swa_exp(b):
                    act.wait_ge(s["sm_max"], b + 1)
                    for h in range(8):
                        sc.activation(sp[:, h, :], sp[:, h, :], ACT.Exp, bias=snm[:, h:h + 1], accum_out=sden[:, h:h + 1])
                    sc.activation(ses, ses, ACT.Exp).then_inc(s["sm_exp"], 1)

                def swa_pt(b):
                    act.wait_ge(s["sm_turned"], b + 1)
                    sc.activation(spT[:, :].rearrange("p (b n) -> p b n", b=4), ps[:, 4:8, :], ACT.Copy).then_inc(s["sm_pt"], 1)

                def swa_out(b):
                    act.wait_ge(s["sm_pv"], b + 1)
                    sc.activation(SO[:, :, b * P:b * P + P], ps[:, 2, :].rearrange("p (j q) -> p j q", j=4), ACT.Copy).then_inc(s["sm_out"], 1)

                tiles = [X2[:, 0, :], X2[:, 1, :]] + [t[:, j, :] for t in (Rt, Kt, Vt) for j in range(4)]
                mus = [12, 13] + list(range(12))
                for i, (dst, mu) in enumerate(zip(tiles, mus)):
                    take(dst, func=ACT.Copy, scale=omu[:, mu:mu + 1], last=False)
                    if i >= 2:
                        act.wait_ge(s["shifted"], i - 1)
                    take(shf[:, i % 2, :], func=ACT.Copy, scale=col("ev_mu", mu))
                    if i >= 4 and (i - 4) % 3 == 0:
                        swa_pt((i - 4) // 3)
                    if i >= 5 and (i - 5) % 3 == 0:
                        swa_out((i - 5) // 3)
                    if i >= 2 and (i - 2) % 3 == 0 and (i - 2) // 3 < 4:
                        swa_exp((i - 2) // 3)
                swa_out(3)

                act.wait_ge(s["shifted"], 14)
                sc.activation(X2[0:64, 0, :], X2[0:64, 0, :], ACT.Tanh).then_inc(s["pre_a"], 1)
                for j in range(8):
                    act.wait_ge(s["proj_done"], n["proj"] + 1)
                    dst = (SGt, At)[j // 4][:, j % 4, :]
                    sc.activation(dst, ps[:, n["proj"] % 2, :], ACT.Exp, bias=nwa[:, j:j + 1], scale=-1.0).then_inc(s["proj_taken"], 1)
                    n["proj"] += 1
                for j in range(4):
                    sc.activation(HT[:, j, :], Kt[:, j, :], ACT.Square, scale=col("ev_k_k", j)).then_inc(s["pre_a"], 1)
                act.wait_ge(s["pre_v"], 1)
                sc.activation(KKt[:, :, :], KKt[:, :, :], ACT.Sqrt).then_inc(s["pre_a"], 1)

                act.wait_ge(s["y_zeroed"], 16 * (NROW // (4 * P)))
                with act.Fori(0, NCH) as c:
                    act.wait_ge(s["ck_cs"], c + 1)
                    sc.activation(Ep[:, :, :], CS[:, :, :], ACT.Exp, scale=-DECAY)
                    sc.activation(Em[:, :, :], CS[:, :, :], ACT.Exp, scale=DECAY)
                    sc.activation(Epp[:, :, :], Dp[:, :, :], ACT.Exp, scale=-DECAY)
                    sc.activation(pc, mid, ACT.Exp, scale=-DECAY).then_inc(s["ck_exp"], 1)
                    for k in range(4):
                        act.wait_ge(s["ck_turned"], c * 4 + (k + 2))
                        sc.activation(TOK[:, k, :], ps[:, k, :], ACT.Copy).then_inc(s["ck_tok"], 1)
                    act.wait_ge(s["akv_done"], c + 1)
                    sc.activation(AKV[:, :], ps[:, 3, :], ACT.Copy).then_inc(s["akv_in"], 1)
                    for l in range(LEVELS):
                        for r in range(2):
                            k = 2 * l + r
                            act.wait_ge(s["iv_u"], c * (2 * LEVELS) + (k + 1))
                            sc.activation((XI if l == 0 else UL)[r][:, :, :].rearrange("p j t -> p (j t)"), ps[:, r, :],
                                          ACT.Copy).then_inc(s["iv_ul"], 1)
                    act.wait_ge(s["wt_done"], c + 1)
                    sc.activation(WT[:, :, :].rearrange("p j t -> p (j t)"), ps[:, 7, :], ACT.Copy).then_inc(s["wt_in"], 1)
                    act.wait_ge(s["u_done"], c + 1)
                    sc.activation(Us[:, :, :, :].rearrange("p j r v -> p r j v"),
                                  ps[:, 0:2, 0:256].rearrange("p r (j v) -> p r j v", j=4), ACT.Copy).then_inc(s["u_in"], 1)
                    act.wait_ge(s["ck_y"], c + 1)
                    sc.activation(HT[:, 4:8, bass.ds(c * CH, CH)], ps[:, 4, :].rearrange("p (j t) -> p j t", j=4),
                                  ACT.Copy).then_inc(s["ck_y_in"], 1)

                sc.activation(X2[:, 1, :], X2[:, 1, :], ACT.Exp, scale=-1.0).then_inc(s["post_a"], 1)
                act.wait_ge(s["post_v"], 4)
                sc.activation(KKt[:, :, :], HT[:, 4:8, :], ACT.Square).then_inc(s["post_a"], 1)
                act.wait_ge(s["post_p"], 4)
                st.then(sc.activation(At[:, :, :], ps[:, 4:8, :], ACT.Ln, bias=cst[:, 1:2], scale=1.0 / HD))
                sc.activation(At[:, :, :], At[:, :, :], ACT.Exp, scale=-0.5).then_inc(s["post_a"], 1)
                n["xt"] += 8

            def cross(L):
                act.wait_ge(s["xt_ready"], n["xt"])
                if L == 0:
                    act.dma_start(memin[:, :, :], a["mem"][0].rearrange("(t p) d -> p t d", p=P)).then_inc(s["mem_in"], 16)
                norm(XT, HT, SEQ)
                if L == 0:
                    act.wait_ge(s["mem_turned"], 4)
                    for q in range(4):
                        st.then(sc.activation(memT[:, 2 * q:2 * q + 2, :], ps[:, q, :].rearrange("p (k t) -> p k t", k=2), ACT.Copy))
                    norm(memT, memN, MEM)
                    for j in range(4):
                        take(mkT[:, j, :], ps[:, n["proj"] % 2, 0:MEM])
                    for t in range(MT):
                        take(mv[:, t, :])
                for h in range(4):
                    take(xq[:, h, :])
                off = 4 * (L + 1)
                for t in range(TT):
                    act.wait_ge(s["sm_max"], off + t + 1)
                    for h in range(4):
                        ins = sc.activation(xp[:, t % 2, h, :], ps[:, 4 + h // 2, MEM * (h % 2):MEM * (h % 2) + MEM], ACT.Exp,
                                            bias=snm[:, h:h + 1], scale=P ** -0.5, accum_out=sden[:, h:h + 1])
                    ins.then_inc(s["sm_exp"], 1)
                    act.wait_ge(s["sm_turned"], off + t + 1)
                    sc.activation(xpT[:, :, t * P:t * P + P], ps[:, 2:4, :].rearrange("p b (c q) -> p (b c) q", c=4), ACT.Copy).then_inc(s["sm_pt"], 1)
                for h in range(4):
                    act.wait_ge(s["sm_pv"], 4 + 4 * L + h + 1)
                    sc.activation(xo[:, h, :], ps[:, 4 + h, :], ACT.Copy).then_inc(s["sm_out"], 1)
                n["xt"] += 8

            def odd():
                act.wait_ge(s["xt_ready"], n["xt"])
                act.dma_start(gup[:, :], a["od_gate_up"][0]).then_inc(s["gup_in"], 16)
                norm(XT, HT, SEQ)
                for t in (gq, gk):
                    for j in range(4):
                        take(t[:, j, :])
                for h in range(2):
                    for t in range(TT):
                        take(gv[:, t, 512 * h:512 * h + 512])
                take(gdT[:, :], ps[0:16, n["proj"] % 2, :])
                for j in range(4):
                    take(gl[:, j, :], func=ACT.Identity, bias=col("od_gate_b", j))
                act.wait_ge(s["proj_taken"], n["proj"])
                st.then(sc.activation(ge[:, :, :], gl[:, :, :], ACT.Abs))
                st.then(sc.activation(ge[:, :, :], ge[:, :, :], ACT.Exp, scale=-1.0))
                sc.activation(ge[:, :, :], ge[:, :, :], ACT.Ln, bias=1.0).then_inc(s["pre_a"], 1)
                for j in range(KD):
                    take(og[:, j, :])
                with act.Fori(0, NCH) as c:
                    act.wait_ge(s["ck_cs"], c + (NCH + 1))
                    sc.activation(gep[:, :, :], gcs[:, :, :], ACT.Exp, scale=1.0 / GATE_NORM)
                    sc.activation(gem[:, :, :], gcs[:, :, :], ACT.Exp, scale=-1.0 / GATE_NORM)
                    sc.activation(pc, mid, ACT.Exp, scale=1.0 / GATE_NORM).then_inc(s["ck_exp"], 1)
                    act.wait_ge(s["ck_turned"], c + (4 * NCH + 2))
                    sc.activation(gkt[:, :], ps[:, 0, :], ACT.Copy).then_inc(s["ck_tok"], 1)
                    act.wait_ge(s["ck_y"], c + (NCH + 1))
                    sc.activation(HT[:, :, bass.ds(c * CH, CH)], ps[:, 2:4, :].rearrange("p b (k t) -> p (b k) t", k=4),
                                  ACT.Copy).then_inc(s["ck_y_in"], 1)
                act.wait_ge(s["ck_y_in"], 2 * NCH + 1)
                act.wait_ge(s["ck_s"], 2 * NCH)
                sc.activation(ogs[:, :, :], og[:, :, :], ACT.Exp, scale=-1.0).then_inc(s["post_a"], 1)
                sc.activation(gsq[:, :, :], HT[:, :, :], ACT.Square).then_inc(s["post_a"], 1)
                act.wait_ge(s["post_p"], 5)
                st.then(sc.activation(grs[:, :, :], ps[:, 4:8, :], ACT.Ln, bias=cst[:, 0:1], scale=1.0 / 256))
                sc.activation(grs[:, :, :], grs[:, :, :], ACT.Exp, scale=-0.5).then_inc(s["post_a"], 1)
                n["xt"] += 8

            def moe(L, before):
                act.wait_ge(s["xt_ready"], n["xt"])
                for o, k, w in ((0, NG, a["moe_w_group"]), (NG, NX, a["moe_w_expert"])):
                    act.dma_start(wr[:, :, o:o + k], w[L].rearrange("(k p) n -> p k n", p=P)).then_inc(s["wr_in"], 16)
                norm(XT, HT, SEQ)
                for t in range(TT):
                    act.wait_ge(s["h_turned"], TT * L + t + 1)
                    sc.activation(hk[:, t, :].rearrange("p (b n) -> p b n", b=2), ps[:, 2 * (t % 2):2 * (t % 2) + 2, :], ACT.Copy).then_inc(s["h_taken"], 1)
                    act.wait_ge(s["h_taken"], TT * L + t + 1)
                    act.dma_start(hrows[t * P:t * P + P, :], hk[:, t, :]).then_inc(s["h_stored"], 16)
                act.wait_ge(s["plan_v"], PLAN_V * L + 1)
                sc.activation(gex[:, :, :], gex[:, :, :], ACT.Exp).then_inc(s["plan_a"], 1)
                act.wait_ge(s["plan_v"], PLAN_V * L + 2)
                sc.activation(ee[:, :], dv[:, :], ACT.Exp).then_inc(s["plan_a"], 1)

                act.wait_ge(s["plan_v"], PLAN_V * (L + 1))
                trips = act.value_load(nit[0:1, 0:1], min_val=1, max_val=NROW // BLK // 2)
                with act.Fori(0, trips) as i:
                    for b in range(2):
                        k = i * 2 + (before + b)
                        act.wait_ge(s["hh_done"], k + (L + 3))
                        sc.activation(hs[b][:, :], ps[:, 2 + b, :], ACT.Copy).then_inc(s["hs_in"], 1)
                        act.wait_ge(s["hs_turned"], k + 1)
                        sc.activation(sl[b][:, :, :], ps[:, 4 + b, :].rearrange("p (f c) -> p f c", f=4)[:, :, 0:BLK], ACT.Silu).then_inc(s["sl_in"], 1)
                        act.wait_ge(s["y_done"], k + (L + 3))
                        act.wait_ge(y_stored[b], i * 32 + (before * 16 + 1))
                        sc.activation(ysb[b][:, :], ps[:, 6 + b, :], ACT.Copy).then_inc(s["y_in"], 1)
                        act.wait_ge(s["y_in"], k + 1)
                        for h in range(2):
                            act.dma_start(yrows[bass.ds((i * 2 + b) * BLK, BLK), 512 * h:512 * h + 512],
                                          ysb[b][64 * h:64 * h + 64, :]).then_inc(y_stored[b], 16)
                n["xt"] += 8
                return trips

            even()
            cross(0)
            before = moe(0, 0) * 2
            odd()
            cross(1)
            moe(1, before)
            act.wait_ge(s["xt_ready"], n["xt"])
            norm(XT, HT, SEQ)
            for t in range(TT):
                act.wait_ge(s["f_turned"], t + 1)
                sc.activation(osb[:, t, :].rearrange("p (b n) -> p b n", b=2), ps[:, 2 * (t % 2):2 * (t % 2) + 2, :], ACT.Copy).then_inc(s["f_taken"], 1)

        @block.tensor
        def _(pe):
            te = nc.tensor
            n = {"proj": 0, "norm": 0, "h": 0, "xt": 8}

            def mm(o, l, r, first=True, last=True):
                return te.matmul(o, l, r, start=first, stop=last)

            for name in ("ck_turned", "hh_done", "y_done", "xg_turned"):
                pe.sem_inc(s[name], 1)
            pe.wait_ge(s["consts"], 1)
            pe.wait_ge(s["par_in"], 16 * (len(PARAMS) + 5))
            te.transpose(ps[:, 7, 0:NPAR], prow[:, :], ident[0:NPAR, 0:NPAR]).then_inc(s["par_turned"], 1)
            mm(ps[:, 6, 0:80], ones[0:1, :], brow[0:1, :]).then_inc(s["par_turned"], 1)
            pe.wait_ge(s["x_in"], 16)
            for k in range(KD):
                if k == 6:
                    pe.wait_ge(s["par_ready"], 1)
                for t in range(TT):
                    ins = te.transpose(ps[:, k, t * P:t * P + P], xin[:, t, k * P:k * P + P], ident[:, :])
                ins.then_inc(s["x_turned"], 1)

            def norm(dst, width):
                for q in range(4):
                    pe.wait_ge(s["sq_ready"], 4 * n["norm"] + q + 1)
                    for k in (2 * q, 2 * q + 1):
                        ins = mm(ps[:, 7, 0:width], ones[:, :], dst[:, k, :], k == 0, k == KD - 1)
                ins.then_inc(s["sum_ready"], 1)
                n["norm"] += 1

            def project(o, pairs, free=None):
                if n["proj"] >= 2:
                    pe.wait_ge(s["proj_taken"], n["proj"] - 1)
                for k, (l, r) in enumerate(pairs):
                    ins = mm(o, l, r, k == 0, k == len(pairs) - 1)
                n["proj"] += 1
                ins.then_inc(s["proj_done"], 1)

            def bank():
                return ps[:, n["proj"] % 2, :]

            def weights(name):
                slot, loaded, _ = use_of(name)
                pe.wait_ge(w_loaded[slot], loaded)
                return slot

            def residual(tiles_of, count):
                for mt in range(KD):
                    if mt >= 2:
                        pe.wait_ge(s["xt_ready"], n["xt"] + mt - 1)
                    pairs = tiles_of(mt)
                    for k, (l, r) in enumerate(pairs):
                        ins = mm(ps[:, 2 + mt % 2, :], l, r, k == 0, k == len(pairs) - 1)
                    ins.then_inc(s["res_done"], 1)
                n["xt"] += 8

            def even():
                norm(HT, SEQ)
                pe.wait_ge(s["h_ready"], 8)
                slot = weights("ev_q")
                for j in range(4):
                    project(bank(), [(W8[slot][:, k, P * j:P * j + P], HT[:, k, :]) for k in range(KD)])
                slot = weights("ev_kvx")
                project(bank(), [(W8[slot][:, k, 0:P], HT[:, k, :]) for k in range(KD)])
                pe.wait_ge(s["proj_taken"], n["proj"] - 1)
                for t in range(TT):
                    for k in range(KD):
                        ins = mm(ps[:, n["proj"] % 2, t * P:t * P + P], HT[:, k, t * P:t * P + P], W8[slot][:, k, P:2 * P],
                                 k == 0, k == KD - 1)
                n["proj"] += 1
                ins.then_inc(s["proj_done"], 1)

                def scores(b):
                    pe.wait_ge(s["proj_taken"], 5 if b == 0 else 6)
                    if b:
                        pe.wait_ge(s["sm_pt"], b)
                    for j in range(4):
                        for g in range(2):
                            r = slice(64 * g, 64 * g + 64)
                            ins = mm(ps[:, 4 + 2 * g + j // 2, 256 * (j % 2):256 * (j % 2) + 256],
                                     sqT[r, j, b * P:b * P + P], skT[r, b * P:b * P + 2 * P])
                    ins.then_inc(s["sm_scored"], 1)

                def turn(b):
                    pe.wait_ge(s["sm_norm"], b + 1)
                    for i in range(16):
                        ins = te.transpose(ps[:, 4 + i // 4, P * (i % 4):P * (i % 4) + P], sp[:, i // 2, P * (i % 2):P * (i % 2) + P], ident[:, :])
                    ins.then_inc(s["sm_turned"], 1)

                def pv(b):
                    pe.wait_ge(s["sm_pt"], b + 1)
                    if b:
                        pe.wait_ge(s["sm_out"], b)
                    for j in range(4):
                        for g in range(2):
                            for half in range(2):
                                i = 2 * (4 * g + j) + half
                                ins = mm(ps[64 * g:64 * g + 64, 2, j * P:j * P + P], sv[:, b + half, 64 * g:64 * g + 64],
                                         spT[:, P * i:P * i + P], half == 0, half == 1)
                    ins.then_inc(s["sm_pv"], 1)

                i = 0
                for name, off, k_tiles in (("ev_kvx", 256, 2), ("ev_r", 0, 4), ("ev_k", 0, 4), ("ev_v", 0, 4)):
                    slot = weights(name)
                    for j in range(k_tiles):
                        o = off + j * P
                        project(bank(), [(W8[slot][:, k, o:o + P], HT[:, k, :]) for k in range(KD)])
                        if i >= 4 and (i - 4) % 3 == 0:
                            turn((i - 4) // 3)
                        if i >= 5 and (i - 5) % 3 == 0:
                            pv((i - 5) // 3)
                        if i >= 2 and (i - 2) % 3 == 0 and (i - 2) // 3 < 4:
                            scores((i - 2) // 3)
                        i += 1
                pv(3)

                pe.wait_ge(s["lora_in"], 48)
                pe.wait_ge(s["pre_a"], 1)
                for r in range(2):
                    q = slice(64 * r, 64 * r + 64)
                    for j in range(4):
                        project(bank(), [(lora[q, 0, j * P:j * P + P], X2[q, 0, :])])
                for j in range(4):
                    pe.wait_ge(s["pre_a"], 2 + j)
                    mm(ps[:, 4 + j, :], pair[:, :], HT[:, j, :]).then_inc(s["pre_p"], 1)

                with pe.Fori(0, NCH) as c:
                    pe.wait_ge(s["ck_el"], c + 1)
                    pe.wait_ge(s["ck_vc"], c + 1)
                    pe.wait_ge(s["ck_y_in"], c + 1)
                    for k, src in enumerate((AR[:, :, 0, :], BT[:, :, :], KT[:, :, :], VC[:, :, :])):
                        for j in range(4):
                            ins = te.transpose(ps[:, k, j * P:j * P + P], src[:, j, :], ident[:, :])
                        ins.then_inc(s["ck_turned"], 1)
                    for x, lt in enumerate((BT, KT)):
                        for q in range(2):
                            for r in range(2):
                                if x:
                                    pe.wait_ge(s["ck_masked"], c * 8 + (2 * q + r + 1))
                                rr = slice(64 * r, 64 * r + 64)
                                for j in (2 * q, 2 * q + 1):
                                    ins = mm(ps[:, 4 + 2 * q + r, 256 * (j % 2):256 * (j % 2) + 256], lt[rr, j, :],
                                             AR[rr, j, :, :].rearrange("p x t -> p (x t)"))
                                ins.then_inc(s["ck_mat"], 1)
                    pe.wait_ge(s["ck_masked"], c * 8 + 8)
                    pe.wait_ge(s["ck_tok"], c * 4 + 4)
                    for j in range(4):
                        for r in range(2):
                            h = 64 * (2 * j + r)
                            ins = mm(ps[:, 3, h:h + 64], MK[:, j, r, 0, :], TOK[:, 3, h:h + 64])
                    ins.then_inc(s["akv_done"], 1)
                    for l in range(LEVELS):
                        for r in range(2):
                            k = 2 * l + r
                            pe.wait_ge(s["iv_tl"], c * (2 * LEVELS) + (k + 1))
                            if l == 1:
                                pe.wait_ge(s["iv_ul"], c * (2 * LEVELS) + (r + 1))
                            if l > 1:
                                pe.wait_ge(s["iv_x"], c * (2 * LEVELS - 2) + (k - 3))
                            for j in range(4):
                                o = ps[:, r, j * P:j * P + P]
                                if l == 0:
                                    ins = te.transpose(o, XJ[r][:, j, :], ident[:, :])
                                else:
                                    ins = mm(o, TL[r][:, j, :], XI[r][:, j, :])
                            ins.then_inc(s["iv_u"], 1)
                        if l == 0:
                            continue
                        for r in range(2):
                            k = 2 * l + r
                            pe.wait_ge(s["iv_ul"], c * (2 * LEVELS) + (k + 1))
                            for j in range(4):
                                if l < LEVELS - 1:
                                    mm(ps[:, 5 + r, j * P:j * P + P], XJ[r][:, j, :], UL[r][:, j, :])
                                ins = mm(ps[:, (2, 4)[r], j * P:j * P + P], UL[r][:, j, :], XJ[r][:, j, :])
                            ins.then_inc(s["iv_v"], 1)
                    for r in range(2):
                        pe.wait_ge(s["iv_x"], c * (2 * LEVELS - 2) + (2 * LEVELS - 3 + r))
                        for j in range(4):
                            h = 64 * (2 * j + r)
                            ins = mm(ps[64 * r:64 * r + 64, 7, j * P:j * P + P], TOK[:, 0, h:h + 64], XJ[r][:, j, :])
                    ins.then_inc(s["wt_done"], 1)
                    pe.wait_ge(s["akv_in"], c + 1)
                    pe.wait_ge(s["wt_in"], c + 1)
                    for j in range(4):
                        for r in range(2):
                            h, rr = 64 * (2 * j + r), slice(64 * r, 64 * r + 64)
                            o = ps[:, r, j * HD:j * HD + HD]
                            mm(o, XJ[r][:, j, :], AKV[:, h:h + 64], True, False)
                            ins = mm(o, WT[rr, j, :], Sn[rr, j, :], False, True)
                    ins.then_inc(s["u_done"], 1)
                    pe.wait_ge(s["u_in"], c + 1)
                    for j in range(4):
                        for r in range(2):
                            h, rr = 64 * (2 * j + r), slice(64 * r, 64 * r + 64)
                            o = ps[rr, 4, j * P:j * P + P]
                            mm(o, Us[:, j, r, :], MA[:, j, r, 1, :], True, False)
                            mm(o, TOK[:, 3, h:h + 64], MK[:, j, r, 1, :], False, False)
                            ins = mm(o, Sn[rr, j, :], AR[rr, j, 1, :], False, True)
                    ins.then_inc(s["ck_y"], 1)
                    for j in range(4):
                        for r in range(2):
                            h, rr = 64 * (2 * j + r), slice(64 * r, 64 * r + 64)
                            o = ps[rr, 5, j * HD:j * HD + HD]
                            mm(o, TOK[:, 1, h:h + 64], Us[:, j, r, :], True, False)
                            ins = mm(o, TOK[:, 2, h:h + 64], TOK[:, 3, h:h + 64], False, True)
                    ins.then_inc(s["ck_s"], 1)

                pe.wait_ge(s["post_v"], 1)
                pe.wait_ge(s["ck_y_in"], NCH + 1)
                for j in range(4):
                    ins = mm(ps[:, j, :], lora[:, 1, j * P:j * P + P], X2[:, 1, :])
                ins.then_inc(s["post_p"], 1)
                pe.wait_ge(s["post_v"], 2)
                for j in range(4):
                    ins = mm(ps[:, 4 + j, :], pair[:, :], KKt[:, j, :])
                ins.then_inc(s["post_p"], 1)
                pe.wait_ge(s["post_v"], 3)
                for j in range(4):
                    ins = mm(ps[:, 4 + j, :], pair[:, :], HT[:, 4 + j, :])
                ins.then_inc(s["post_p"], 1)
                pe.wait_ge(s["post_a"], 2)
                for j in range(4):
                    ins = mm(ps[:, 4 + j, :], pair[:, :], KKt[:, j, :])
                ins.then_inc(s["post_p"], 1)

                pe.wait_ge(s["post_v"], 5)
                slots = [weights("ev_o0"), weights("ev_o1")]
                residual(lambda mt: [(W8[slots[mt // 4]][:, k, P * (mt % 4):P * (mt % 4) + P],
                                      (SO if k < 4 else HT)[:, k, :]) for k in range(KD)], KD)

            def cross(L):
                norm(HT, SEQ)
                if L == 0:
                    pe.wait_ge(s["mem_in"], 16)
                    for q in range(4):
                        for k in (2 * q, 2 * q + 1):
                            for t in range(MT):
                                o = 256 * (k % 2) + t * P
                                ins = te.transpose(ps[:, q, o:o + P], memin[:, t, k * P:k * P + P], ident[:, :])
                        ins.then_inc(s["mem_turned"], 1)
                    norm(memN, MEM)
                    pe.wait_ge(s["h_ready"], 8 * n["norm"])
                    slot = weights("xk")
                    for j in range(4):
                        project(ps[:, n["proj"] % 2, 0:MEM], [(W8[slot][:, k, P * j:P * j + P], memN[:, k, :]) for k in range(KD)])
                    slot = weights("xv")
                    for t in range(MT):
                        project(bank(), [(memN[:, k, t * P:t * P + P], W8[slot][:, k, :]) for k in range(KD)])
                pe.wait_ge(s["h_ready"], 8 * n["norm"])
                slot = weights(f"xq{L}")
                for h in range(4):
                    project(bank(), [(W8[slot][:, k, P * h:P * h + P], HT[:, k, :]) for k in range(KD)])
                off = 4 * (L + 1)
                pe.wait_ge(s["proj_taken"], n["proj"])
                for t in range(TT):
                    if t:
                        pe.wait_ge(s["sm_exp"], off + t)
                    for h in range(4):
                        ins = mm(ps[:, 4 + h // 2, MEM * (h % 2):MEM * (h % 2) + MEM], xq[:, h, t * P:t * P + P], mkT[:, h, :])
                    ins.then_inc(s["sm_scored"], 1)
                    pe.wait_ge(s["sm_norm"], off + t + 1)
                    if t:
                        pe.wait_ge(s["sm_pt"], off + t)
                    for i in range(8):
                        ins = te.transpose(ps[:, 2 + i // 4, P * (i % 4):P * (i % 4) + P], xp[:, t % 2, i // 2, P * (i % 2):P * (i % 2) + P], ident[:, :])
                    ins.then_inc(s["sm_turned"], 1)
                pe.wait_ge(s["sm_pt"], off + TT)
                for h in range(4):
                    for t in range(MT):
                        ins = mm(ps[:, 4 + h, :], mv[:, t, P * h:P * h + P], xpT[:, 2 * h + t, :], t == 0, t == 1)
                    ins.then_inc(s["sm_pv"], 1)
                slot = weights(f"xo{L}")
                pe.wait_ge(s["sm_out"], off + TT)
                residual(lambda mt: [(W4[slot][:, k, P * mt:P * mt + P], xo[:, k, :]) for k in range(4)], 4)

            def odd():
                norm(HT, SEQ)
                pe.wait_ge(s["h_ready"], 8 * n["norm"])
                for name in ("od_q", "od_k"):
                    slot = weights(name)
                    for j in range(4):
                        project(bank(), [(W8[slot][:, k, P * j:P * j + P], HT[:, k, :]) for k in range(KD)])
                for name in ("od_v0", "od_v1"):
                    slot = weights(name)
                    for t in range(TT):
                        project(bank(), [(HT[:, k, t * P:t * P + P], W8[slot][:, k, :]) for k in range(KD)])
                slot = weights("od_gd")
                project(ps[0:16, n["proj"] % 2, :], [(W8[slot][:, k, 0:16], HT[:, k, :]) for k in range(KD)])
                pe.wait_ge(s["gup_in"], 16)
                pe.wait_ge(s["proj_taken"], n["proj"])
                for j in range(4):
                    project(bank(), [(gup[:, P * j:P * j + P], gdT[:, :])])
                for name in ("od_og0", "od_og1"):
                    slot = weights(name)
                    for j in range(4):
                        project(bank(), [(W8[slot][:, k, P * j:P * j + P], HT[:, k, :]) for k in range(KD)])
                pe.wait_ge(s["proj_taken"], n["proj"])
                with pe.Fori(0, NCH) as c:
                    pe.wait_ge(s["ck_el"], c + (NCH + 1))
                    pe.wait_ge(s["ck_vc"], c + (NCH + 1))
                    pe.wait_ge(s["ck_y_in"], c + (NCH + 1))
                    for h in range(4):
                        ins = te.transpose(ps[:, 0, h * P:h * P + P], gkc[:, h, :], ident[:, :])
                    ins.then_inc(s["ck_turned"], 1)
                    for h in range(4):
                        ins = mm(ps[:, 1, h * P:h * P + P], gkc[:, h, :], gqc[:, h, :])
                    ins.then_inc(s["ck_mat"], 1)
                    pe.wait_ge(s["ck_masked"], c + (8 * NCH + 1))
                    for e in range(KD):
                        o = ps[:, 2 + e // 4, P * (e % 4):P * (e % 4) + P]
                        mm(o, gvc[:, e * P:e * P + P], gat[:, e // 2, :], True, False)
                        ins = mm(o, gsn[:, e // 2, P * (e % 2):P * (e % 2) + P], gqc[:, e // 2, :], False, True)
                    ins.then_inc(s["ck_y"], 1)
                    pe.wait_ge(s["ck_tok"], c + (4 * NCH + 1))
                    for h in range(4):
                        ins = mm(ps[:, 4 + h // 2, 256 * (h % 2):256 * (h % 2) + 256], gkt[:, h * P:h * P + P], gvc[:, 256 * h:256 * h + 256])
                    ins.then_inc(s["ck_s"], 1)
                pe.wait_ge(s["post_a"], 5)
                pe.wait_ge(s["gst_read"], 1)
                for h in range(4):
                    for t in range(2):
                        ins = mm(ps[:, 4 + h, :], ones[:, :], gsq[:, 2 * h + t, :], t == 0, t == 1)
                ins.then_inc(s["post_p"], 1)
                pe.wait_ge(s["post_v"], 6)
                slots = [weights("od_o0"), weights("od_o1")]
                residual(lambda mt: [(W8[slots[mt // 4]][:, k, P * (mt % 4):P * (mt % 4) + P], HT[:, k, :]) for k in range(KD)], KD)

            def moe(L, before):
                norm(HT, SEQ)
                pe.wait_ge(s["h_ready"], 8 * n["norm"])
                pe.wait_ge(s["wr_in"], 32 * (L + 1))
                for t in range(TT):
                    for k in range(KD):
                        ins = mm(ps[:, 4, 64 * t:64 * t + NR], HT[:, k, t * P:t * P + P], wr[:, k, :], k == 0, k == KD - 1)
                ins.then_inc(s["plan_p"], 1)
                for t in range(TT):
                    if t >= 2:
                        pe.wait_ge(s["h_taken"], TT * L + t - 1)
                    for k in range(KD):
                        ins = te.transpose(ps[:, 2 * (t % 2) + k // 4, P * (k % 4):P * (k % 4) + P], HT[:, k, t * P:t * P + P], ident[:, :])
                    ins.then_inc(s["h_turned"], 1)
                pe.wait_ge(s["plan_v"], PLAN_V * L + 3)
                for t in range(TT):
                    for u in range(t + 1):
                        mm(ps[:, 5, NX * t:NX * t + NX], (tri[:, 0, :] if u == t else ones[:, :]), msk[:, u, :], u == 0, u == t)
                for u in range(TT):
                    ins = mm(ps[:, 5, P:P + NX], ones[:, :], msk[:, u, :], u == 0, u == TT - 1)
                ins.then_inc(s["plan_p"], 1)
                pe.wait_ge(s["plan_v"], PLAN_V * L + 4)
                for i in range(8):
                    ins = mm(ps[0:BLK, 6, 0:NBLK], rhot[:, i, :], bhot[:, i, :], i == 0, i == 7)
                ins.then_inc(s["plan_p"], 1)
                pe.wait_ge(s["plan_p"], 3 * (L + 1))
                pe.sem_inc(s["hh_done"], 1)
                pe.sem_inc(s["y_done"], 1)
                pe.wait_ge(s["plan_v"], PLAN_V * (L + 1))
                trips = pe.value_load(nit[0:1, 0:1], min_val=1, max_val=NROW // BLK // 2)

                def turn_rows(b, arrived):
                    pe.wait_ge(xg_in[b], arrived)
                    pe.sem_inc(s["go"], 1)
                    for k in range(KD):
                        ins = te.transpose(ps[:, b, BLK * k:BLK * k + BLK], xg[b][:, k * P:k * P + P], ident[0:BLK, 0:BLK])
                    ins.then_inc(s["xg_turned"], 1)

                turn_rows(0, before * 8 + 16 * (L + 1))
                with pe.Fori(0, trips) as i:
                    for b in range(2):
                        k0 = i * 2 + (before + b)
                        pe.wait_ge(s["xgT_in"], k0 + (L + 1))
                        pe.wait_ge(w13_in[b], (i + 1) * 32 + before * 16)
                        for k in range(KD):
                            mm(ps[0:64, 2 + b, :], xgT[b][:, k, :], W8[3 * b][:, k, :], k == 0, k == KD - 1)
                            ins = mm(ps[64:128, 2 + b, :], xgT[b][:, k, :], W8[3 * b + 1][:, k, :], k == 0, k == KD - 1)
                        ins.then_inc(s["hh_done"], 1)
                        turn_rows(1 - b, (i * 16 + (before * 8 + 16)) if b == 0 else (i * 16 + (before * 8 + 16 * L + 32)))
                        pe.wait_ge(s["hs_in"], k0 + 1)
                        for f in range(4):
                            ins = te.transpose(ps[:, 4 + b, f * P:f * P + P], hs[b][:, f * P:f * P + P], ident[:, :])
                        ins.then_inc(s["hs_turned"], 1)
                        pe.wait_ge(s["act_in"], k0 + 1)
                        pe.wait_ge(w2_in[b], (i + 1) * 16 + before * 8)
                        for f in range(4):
                            for h in range(2):
                                ins = mm(ps[64 * h:64 * h + 64, 6 + b, :], act_[b][:, f, :], W4[3 * b + 2][:, f, 512 * h:512 * h + 512],
                                         f == 0, f == 3)
                        ins.then_inc(s["y_done"], 1)
                return trips

            def moe_back(L):
                for k in range(KD):
                    pe.wait_ge(s["y_sum"], TT * (L + 1))
                    for t in range(TT):
                        ins = te.transpose(ps[:, k, t * P:t * P + P], yg[2 * t][:, k * P:k * P + P], ident[:, :])
                    ins.then_inc(s["y_turned"], 1)
                n["xt"] += 8

            even()
            cross(0)
            before = moe(0, 0) * 2
            moe_back(0)
            odd()
            cross(1)
            moe(1, before)
            moe_back(1)
            norm(HT, SEQ)
            pe.wait_ge(s["h_ready"], 8 * n["norm"])
            for t in range(TT):
                if t >= 2:
                    pe.wait_ge(s["f_taken"], t - 1)
                for k in range(KD):
                    ins = te.transpose(ps[:, 2 * (t % 2) + k // 4, P * (k % 4):P * (k % 4) + P], HT[:, k, t * P:t * P + P], ident[:, :])
                ins.then_inc(s["f_turned"], 1)

        @block.vector
        def _(dve):
            st = Steps(dve, s["v_step"])
            ve = nc.vector
            n = {"norm": 0, "xt": 8}

            def bcast(ap, shape):
                return ap.broadcast_to(shape)

            ve.memset(W[5][:, :], 0.0).then_inc(s["zeros"], 1)
            dve.wait_ge(s["par_turned"], 2)
            st.then(ve.tensor_copy(par[:, :], ps[:, 7, 0:NPAR]))
            st.then(ve.tensor_copy(bc[:, :], ps[:, 6, 0:80]))
            ve.tensor_scalar(omu[:, :], par[:, PARAMS["ev_mu"][0]:PARAMS["ev_mu"][0] + 14], -1.0, 1.0, ALU.mult, ALU.add)
            ve.tensor_scalar(oka[:, :], par[:, PARAMS["ev_k_a"][0]:PARAMS["ev_k_a"][0] + 4], -1.0, 1.0, ALU.mult, ALU.add)
            ve.tensor_scalar(nwa[:, :], par[:, PARAMS["ev_w0"][0]:PARAMS["ev_w0"][0] + 8], -1.0, None, ALU.mult).then_inc(s["par_ready"], 1)
            for k in range(KD):
                dve.wait_ge(s["x_turned"], k + 1)
                ve.tensor_copy(XT[:, k, :], ps[:, k, :]).then_inc(s["xt_ready"], 1)

            def norm(src, dst, width, gain, first):
                n["norm"] += 1
                dve.wait_ge(s["rstd_ready"], n["norm"])
                for k in range(KD):
                    ve.scalar_tensor_tensor(dst[:, k, :], src[:, k, :], col(gain, first + k), rs[:, 0:width], ALU.mult, ALU.mult).then_inc(s["h_ready"], 1)

            def residual():
                for mt in range(KD):
                    dve.wait_ge(s["res_done"], n["res"] + mt + 1)
                    ve.tensor_tensor(XT[:, mt, :], ps[:, 2 + mt % 2, :], XT[:, mt, :], ALU.add).then_inc(s["xt_ready"], 1)
                n["res"] += 8

            n["res"] = 0

            def even():
                norm(XT, HT, SEQ, "norm_mix", 0)
                dve.wait_ge(s["par_ready"], 1)

                def softmax(b):
                    dve.wait_ge(s["sm_scored"], b + 1)
                    dve.wait_ge(s["sm_turned"], b)
                    st.then(ve.scalar_tensor_tensor(sp[:, :, :], ps[:, 4:8, :].rearrange("p b (h k) -> p (b h) k", h=2), HD ** -0.5,
                                                    bcast(smask[:, min(b, 1), :].unsqueeze(1), [P, 8, 2 * P]), ALU.mult, ALU.add))
                    st.then(ve.tensor_reduce(smx, sp[:, :, :], AX.X, ALU.max))
                    st.then(ve.tensor_tensor(smx, smx, bc[:, 0:8], ALU.max))
                    ve.tensor_scalar(snm, smx, -1.0, None, ALU.mult)
                    ve.tensor_tensor(ses, bc[:, 0:8], smx, ALU.subtract).then_inc(s["sm_max"], 1)
                    dve.wait_ge(s["sm_exp"], b + 1)
                    st.then(ve.tensor_tensor(sden, sden, ses, ALU.add))
                    st.then(ve.reciprocal(srec, sden))
                    ve.tensor_tensor(sp[:, :, :], sp[:, :, :], bcast(srec.unsqueeze(2), [P, 8, 2 * P]), ALU.mult).then_inc(s["sm_norm"], 1)

                tiles = [X2[:, 0, :], X2[:, 1, :]] + [t[:, j, :] for t in (Rt, Kt, Vt) for j in range(4)]
                for i, dst in enumerate(tiles):
                    dve.wait_ge(s["proj_taken"], 6 + i + 1)
                    ve.tensor_tensor(dst[:, 1:SEQ], dst[:, 1:SEQ], shf[:, i % 2, 0:SEQ - 1], ALU.add).then_inc(s["shifted"], 1)
                    if i >= 2 and (i - 2) % 3 == 0 and (i - 2) // 3 < 4:
                        softmax((i - 2) // 3)

                dve.wait_ge(s["proj_taken"], 28)
                for t in (SGt, At):
                    st.then(ve.tensor_scalar(t[:, :, :], t[:, :, :], 1.0, None, ALU.add))
                    st.then(ve.reciprocal(t[:, :, :], t[:, :, :]))
                dve.wait_ge(s["pre_p"], 4)
                ve.tensor_scalar(KKt[:, :, :], ps[:, 4:8, :], 1e-24, None, ALU.max).then_inc(s["pre_v"], 1)
                dve.wait_ge(s["pre_a"], 6)
                st.then(ve.reciprocal(KKt[:, :, :], KKt[:, :, :]))
                for j in range(4):
                    ins = ve.scalar_tensor_tensor(KKt[:, j, :], Kt[:, j, :], col("ev_k_k", j), KKt[:, j, :], ALU.mult, ALU.mult)
                st.then(ins)
                tmp = HT[:, 0:4, :]
                for j in range(4):
                    ins = ve.tensor_scalar(tmp[:, j, :], At[:, j, :], col("ev_k_a", j), oka[:, j:j + 1], ALU.mult, ALU.add)
                st.then(ins)
                st.then(ve.tensor_tensor(Kt[:, :, :], Kt[:, :, :], tmp, ALU.mult))
                st.then(ve.tensor_tensor(At[:, :, :], At[:, :, :], KKt[:, :, :], ALU.mult))
                ve.memset(St[:, :, :], 0.0).then_inc(s["pre_v"], 1)
                dve.wait_ge(s["pre_v"], 2)

                dve.wait_ge(s["y_zeroed"], 16 * (NROW // (4 * P)))
                with dve.Fori(0, NCH) as c:
                    st.enter(c, 9 + 2 + 2 * (LEVELS - 1))
                    t = bass.ds(c * CH, CH)
                    for j in range(4):
                        ins = ve.tensor_tensor_scan(CS[:, j, :], ones[:, :], SGt[:, j, t], 0.0, ALU.mult, ALU.add)
                    st.then(ins)
                    st.then(ve.tensor_copy(mid.unsqueeze(2), CS[:, :, CH // 2 - 1:CH // 2]))
                    st.then(ve.tensor_tensor(CS[:, :, :], CS[:, :, :], bcast(mid.unsqueeze(2), [P, 4, CH]), ALU.subtract))
                    ve.tensor_tensor(Dp[:, :, :], CS[:, :, :], SGt[:, :, t], ALU.subtract).then_inc(s["ck_cs"], 1)
                    dve.wait_ge(s["ck_exp"], c + 1)
                    ve.tensor_tensor(AR[:, :, 1, :], Rt[:, :, t], Ep[:, :, :], ALU.mult)
                    ve.scalar_tensor_tensor(AR[:, :, 0, :], KKt[:, :, t], -1.0, Epp[:, :, :], ALU.mult, ALU.mult)
                    ve.tensor_tensor(BT[:, :, :], At[:, :, t], Em[:, :, :], ALU.mult)
                    ve.tensor_tensor(Sn[:, :, :], St[:, :, :], bcast(pc.unsqueeze(2), [P, 4, HD]), ALU.mult)
                    ve.tensor_tensor(KT[:, :, :], Kt[:, :, t], Em[:, :, :], ALU.mult).then_inc(s["ck_el"], 1)
                    for x, dst in enumerate((MA, MK)):
                        for q in range(2):
                            for r in range(2):
                                k = 4 * x + 2 * q + r
                                dve.wait_ge(s["ck_mat"], c * 8 + (k + 1))
                                ve.tensor_tensor(dst[:, 2 * q:2 * q + 2, r, :, :].rearrange("p j x t -> p j (x t)"),
                                                 ps[:, 4 + 2 * q + r, :].rearrange("p (j n) -> p j n", j=2),
                                                 bcast(tri[:, :, :].rearrange("p x t -> p (x t)").unsqueeze(1), [P, 2, 2 * CH]),
                                                 ALU.mult).then_inc(s["ck_masked"], 1)
                    dve.wait_ge(s["ck_masked"], c * 8 + 8)

                    def masked(r, l):
                        return ve.tensor_tensor(TL[r][:, :, :] if l else XJ[r][:, :, :], MA[:, :, r, 0, :],
                                                bcast(level[:, l, :].unsqueeze(1), [P, 4, CH]), ALU.mult)

                    for r in range(2):
                        st.then(masked(r, 0))
                        ve.tensor_tensor(XJ[r][:, :, :], XJ[r][:, :, :], bcast(ident[:, :].unsqueeze(1), [P, 4, CH]), ALU.add).then_inc(s["iv_tl"], 1)
                    for r in range(2):
                        masked(r, 1).then_inc(s["iv_tl"], 1)
                    for l in range(1, LEVELS):
                        if l + 1 < LEVELS:
                            for r in range(2):
                                dve.wait_ge(s["iv_u"], c * (2 * LEVELS) + (2 * l + r + 1))
                                masked(r, l + 1).then_inc(s["iv_tl"], 1)
                        for r in range(2):
                            dve.wait_ge(s["iv_v"], c * (2 * LEVELS - 2) + (2 * l + r - 1))
                            if l == 1:
                                dve.wait_ge(s["iv_tl"], c * (2 * LEVELS) + (r + 1))
                                dve.wait_ge(s["iv_ul"], c * (2 * LEVELS) + (r + 1))
                            else:
                                dve.wait_ge(s["iv_x"], c * (2 * LEVELS - 2) + (2 * l + r - 3))
                            if l + 1 < LEVELS:
                                st.then(ve.tensor_tensor(XI[r][:, :, :], ps[:, 5 + r, :].rearrange("p (j t) -> p j t", j=4), XI[r][:, :, :], ALU.add))
                            ve.tensor_tensor(XJ[r][:, :, :], ps[:, (2, 4)[r], :].rearrange("p (j t) -> p j t", j=4), XJ[r][:, :, :], ALU.add).then_inc(s["iv_x"], 1)
                    st.then(ve.tensor_copy(fc.unsqueeze(2), Ep[:, :, CH - 1:CH]))
                    dve.wait_ge(s["ck_s"], c + 1)
                    st.then(ve.tensor_tensor(Sn[:, :, :], ps[:, 5, 0:4 * HD].rearrange("p (j v) -> p j v", j=4), Sn[:, :, :], ALU.add))
                    st.then(ve.tensor_tensor(St[:, :, :], Sn[:, :, :], bcast(fc.unsqueeze(2), [P, 4, HD]), ALU.mult))
                    while st.n < st.per:
                        st.then(ve.tensor_copy(mid, fc))
                    st.leave(NCH)

                dve.wait_ge(s["post_a"], 1)
                st.then(ve.tensor_scalar(X2[:, 1, :], X2[:, 1, :], 1.0, None, ALU.add))
                ve.reciprocal(X2[:, 1, :], X2[:, 1, :]).then_inc(s["post_v"], 1)
                for j in range(4):
                    ins = ve.scalar_tensor_tensor(KKt[:, j, :], Rt[:, j, :], col("ev_r_k", j), Kt[:, j, :], ALU.mult, ALU.mult)
                ins.then_inc(s["post_v"], 1)
                dve.wait_ge(s["post_p"], 2)
                ve.tensor_tensor(Vt[:, :, :], ps[:, 4:8, :], Vt[:, :, :], ALU.mult).then_inc(s["post_v"], 1)
                dve.wait_ge(s["post_p"], 3)
                ve.scalar_tensor_tensor(HT[:, 4:8, :], ps[:, 4:8, :], -1.0 / HD, HT[:, 4:8, :], ALU.mult, ALU.add).then_inc(s["post_v"], 1)
                dve.wait_ge(s["post_a"], 3)
                st.then(ve.tensor_tensor(HT[:, 4:8, :], HT[:, 4:8, :], At[:, :, :], ALU.mult))
                for j in range(4):
                    ins = ve.tensor_scalar(HT[:, 4 + j, :], HT[:, 4 + j, :], col("ev_lnx_w", j), col("ev_lnx_b", j), ALU.mult, ALU.add)
                st.then(ins)
                st.then(ve.tensor_tensor(HT[:, 4:8, :], HT[:, 4:8, :], Vt[:, :, :], ALU.add))
                ve.tensor_tensor(HT[:, 4:8, :], ps[:, 0:4, :], HT[:, 4:8, :], ALU.mult).then_inc(s["post_v"], 1)
                residual()

            def cross(L):
                norm(XT, HT, SEQ, "norm_xattn", 8 * L)
                if L == 0:
                    norm(memT, memN, MEM, "mem_norm", 0)
                off = 4 * (L + 1)
                for t in range(TT):
                    dve.wait_ge(s["sm_scored"], off + t + 1)
                    st.then(ve.tensor_reduce(smx[:, 0:4], ps[:, 4:6, :].rearrange("p b (h k) -> p (b h) k", h=2), AX.X, ALU.max))
                    ve.tensor_scalar(snm[:, 0:4], smx[:, 0:4], -(P ** -0.5), None, ALU.mult).then_inc(s["sm_max"], 1)
                    dve.wait_ge(s["sm_exp"], off + t + 1)
                    st.then(ve.reciprocal(srec[:, 0:4], sden[:, 0:4]))
                    ve.tensor_tensor(xp[:, t % 2, :, :], xp[:, t % 2, :, :], bcast(srec[:, 0:4].unsqueeze(2), [P, 4, MEM]), ALU.mult).then_inc(s["sm_norm"], 1)
                residual()

            def odd():
                norm(XT, HT, SEQ, "norm_mix", 8)
                dve.wait_ge(s["proj_taken"], 59)
                st.then(ve.tensor_scalar(gz[:, :, :], gl[:, :, :], 0.0, None, ALU.min))
                dve.wait_ge(s["pre_a"], 7)
                st.then(ve.tensor_tensor(gl[:, :, :], gz[:, :, :], ge[:, :, :], ALU.subtract))
                st.then(ve.memset(gst[:, :, :], 0.0))
                with dve.Fori(0, NCH) as c:
                    st.enter(c, 5)
                    t = bass.ds(c * CH, CH)
                    for j in range(4):
                        ins = ve.tensor_tensor_scan(gcs[:, j, :], ones[:, :], gl[:, j, t], 0.0, ALU.mult, ALU.add)
                    st.then(ins)
                    st.then(ve.tensor_copy(mid.unsqueeze(2), gcs[:, :, CH // 2 - 1:CH // 2]))
                    ve.tensor_tensor(gcs[:, :, :], gcs[:, :, :], bcast(mid.unsqueeze(2), [P, 4, CH]), ALU.subtract).then_inc(s["ck_cs"], 1)
                    dve.wait_ge(s["ck_exp"], c + (NCH + 1))
                    ve.scalar_tensor_tensor(gqc[:, :, :], gq[:, :, t], P ** -0.5, gep[:, :, :], ALU.mult, ALU.mult)
                    ve.tensor_tensor(gsn[:, :, :], gst[:, :, :], bcast(pc.unsqueeze(2), [P, 4, 256]), ALU.mult)
                    st.then(ve.tensor_copy(fc.unsqueeze(2), gep[:, :, CH - 1:CH]))
                    ve.tensor_tensor(gkc[:, :, :], gk[:, :, t], gem[:, :, :], ALU.mult).then_inc(s["ck_el"], 1)
                    dve.wait_ge(s["ck_mat"], c + (8 * NCH + 1))
                    ve.tensor_tensor(gat[:, :, :], ps[:, 1, :].rearrange("p (h t) -> p h t", h=4),
                                     bcast(tri[:, 1, :].unsqueeze(1), [P, 4, CH]), ALU.mult).then_inc(s["ck_masked"], 1)
                    dve.wait_ge(s["ck_s"], c + (NCH + 1))
                    st.then(ve.tensor_tensor(gsn[:, :, :], ps[:, 4:6, :].rearrange("p b (h v) -> p (b h) v", h=2), gsn[:, :, :], ALU.add))
                    st.then(ve.tensor_tensor(gst[:, :, :], gsn[:, :, :], bcast(fc.unsqueeze(2), [P, 4, 256]), ALU.mult))
                    st.leave(NCH)
                dve.sem_inc(s["gst_read"], 1)
                dve.wait_ge(s["post_a"], 4)
                st.then(ve.tensor_scalar(ogs[:, :, :], ogs[:, :, :], 1.0, None, ALU.add))
                st.then(ve.reciprocal(ogs[:, :, :], ogs[:, :, :]))
                st.then(ve.tensor_tensor(og[:, :, :], og[:, :, :], ogs[:, :, :], ALU.mult))
                dve.wait_ge(s["post_a"], 6)
                for k in range(KD):
                    ins = ve.scalar_tensor_tensor(HT[:, k, :], HT[:, k, :], col("od_onorm", k % 2), grs[:, k // 2, :], ALU.mult, ALU.mult)
                st.then(ins)
                ve.tensor_tensor(HT[:, :, :], HT[:, :, :], og[:, :, :], ALU.mult).then_inc(s["post_v"], 1)
                residual()

            def moe(L, before):
                norm(XT, HT, SEQ, "norm_moe", 8 * L)
                done = {"plan": PLAN_V * L}
                dve.wait_ge(s["plan_g"], L + 1)
                dve.wait_ge(s["plan_p"], 3 * L + 1)
                o = 8 + NR * L
                st.then(ve.memset(glp[:, :, :], NEG))
                st.then(ve.tensor_tensor(lg[:, :, :], ps[:, 4, 0:256].rearrange("p (t n) -> p t n", t=TT)[:, :, 0:NR],
                                         bcast(bc[:, o:o + NR].unsqueeze(1), [P, TT, NR]), ALU.add))
                st.then(ve.tensor_copy(glp[:, :, 0:NG], lg[:, :, 0:NG]))
                for t in range(TT):
                    ins = ve.max(g8[:, t, :], glp[:, t, :])
                st.then(ins)
                for t in range(TT):
                    ins = ve.max_index(gi8[:, t, :], g8[:, t, :], glp[:, t, :])
                st.then(ins)
                ve.tensor_tensor(gex[:, :, :], lg[:, :, 0:NG], bcast(g8[:, :, 0:1], [P, TT, NG]), ALU.subtract).then_inc(s["plan_v"], 1)
                st.then(ve.tensor_copy(gidx[:, :].unsqueeze(2), gi8[:, :, 0:1]))
                st.then(ve.tensor_tensor(ogh[:, :, :], bcast(io[:, 0:NG].unsqueeze(1), [P, TT, NG]),
                                         bcast(gidx[:, :].unsqueeze(2), [P, TT, NG]), ALU.is_equal))
                prod = cmp[:, 0:TT * NX].rearrange("p (t e g) -> p t e g", t=TT, e=NE)
                for g in range(NG):
                    ins = ve.tensor_tensor(prod[:, :, :, g], lg[:, :, NG + NE * g:NG + NE * g + NE], bcast(ogh[:, :, g:g + 1], [P, TT, NE]), ALU.mult)
                st.then(ins)
                st.then(ve.tensor_reduce(ein[:, :, :], prod, AX.X, ALU.add))
                for t in range(TT):
                    ins = ve.max(e8[:, t, :], ein[:, t, :])
                st.then(ins)
                for t in range(TT):
                    ins = ve.max_index(ei8[:, t, :], e8[:, t, :], ein[:, t, :])
                st.then(ins)
                ve.tensor_tensor(dv[:, :].unsqueeze(2), e8[:, :, 1:2], e8[:, :, 0:1], ALU.subtract).then_inc(s["plan_v"], 1)
                st.then(ve.tensor_copy(eid[:, :, :], ei8[:, :, 0:2]))
                st.then(ve.scalar_tensor_tensor(eid[:, :, :], bcast(gidx[:, :].unsqueeze(2), [P, TT, 2]), float(NE), eid[:, :, :], ALU.mult, ALU.add))
                st.then(ve.tensor_tensor(oh[:, :, :, :].rearrange("p t c e -> p (t c) e"), bcast(io[:, 0:NX].unsqueeze(1), [P, 8, NX]),
                                         bcast(eid[:, :, :].rearrange("p t c -> p (t c)").unsqueeze(2), [P, 8, NX]), ALU.is_equal))
                ve.tensor_tensor(msk[:, :, :], oh[:, :, 0, :], oh[:, :, 1, :], ALU.add).then_inc(s["plan_v"], 1)
                dve.wait_ge(s["plan_a"], 2 * L + 2)
                st.then(ve.tensor_reduce(pg[:, :], gex[:, :, :], AX.X, ALU.add))
                st.then(ve.tensor_scalar(dv[:, :], ee[:, :], 1.0, None, ALU.add))
                st.then(ve.tensor_tensor(pg[:, :], pg[:, :], dv[:, :], ALU.mult))
                st.then(ve.reciprocal(gate[:, :, 0:1], pg[:, :].unsqueeze(2)))
                st.then(ve.tensor_tensor(gate[:, :, 1:2], gate[:, :, 0:1], ee[:, :].unsqueeze(2), ALU.mult))
                dve.wait_ge(s["plan_p"], 3 * L + 2)
                ve.tensor_copy(rk[:, :, :], ps[:, 5, 0:P].rearrange("p (t e) -> p t e", t=TT))
                st.then(ve.tensor_copy(cn[:, :], ps[:, 5, P:P + NX]))
                c8 = cmp[:, 0:NX * 8].rearrange("p (e k) -> p e k", k=8)
                st.then(ve.tensor_tensor(c8, bcast(cn[:, :].unsqueeze(2), [P, NX, 8]), bcast(io64[:, :].unsqueeze(1), [P, NX, 8]), ALU.is_gt))
                st.then(ve.tensor_reduce(nb[:, :], c8, AX.X, ALU.add))
                st.then(ve.tensor_tensor_scan(pend[:, :], ones[:, 0:NX], nb[:, :], 0.0, ALU.mult, ALU.add))
                st.then(ve.tensor_tensor(pst[:, :], pend[:, :], nb[:, :], ALU.subtract))
                oh8 = oh[:, :, :, :].rearrange("p t c e -> p (t c) e")
                pe8 = cmp[:, 0:8 * NX].rearrange("p (i e) -> p i e", i=8)
                for ci in range(2):
                    ins = ve.tensor_tensor(cmp[:, 0:8 * NX].rearrange("p (t c e) -> p t c e", t=TT, c=2)[:, :, ci, :], oh[:, :, ci, :], rk[:, :, :], ALU.mult)
                st.then(ins)
                st.then(ve.tensor_reduce(selr[:, :], pe8, AX.X, ALU.add))
                st.then(ve.tensor_tensor(pe8, oh8, bcast(pst[:, :].unsqueeze(1), [P, 8, NX]), ALU.mult))
                st.then(ve.tensor_reduce(selp[:, :], pe8, AX.X, ALU.add))
                r8 = cmp[:, 0:64].rearrange("p (i k) -> p i k", k=8)
                st.then(ve.tensor_tensor(r8, bcast(selr[:, :].unsqueeze(2), [P, 8, 8]), bcast(io64[:, :].unsqueeze(1), [P, 8, 8]), ALU.is_ge))
                st.then(ve.tensor_reduce(rq[:, :], r8, AX.X, ALU.add))
                st.then(ve.tensor_scalar(rq[:, :], rq[:, :], -1.0, None, ALU.add))
                st.then(ve.tensor_tensor(blk[:, :], selp[:, :], rq[:, :], ALU.add))
                st.then(ve.scalar_tensor_tensor(brk[:, :], rq[:, :], -float(BLK), selr[:, :], ALU.mult, ALU.add))
                st.then(ve.scalar_tensor_tensor(selr[:, :], blk[:, :], float(BLK), brk[:, :], ALU.mult, ALU.add))
                st.then(ve.tensor_copy(sloti[:, :], selr[:, :]))
                st.then(ve.tensor_tensor(rhot[:, :, :], bcast(io[:, :].unsqueeze(1), [P, 8, BLK]), bcast(brk[:, :].unsqueeze(2), [P, 8, BLK]), ALU.is_equal))
                st.then(ve.tensor_tensor(bhot[:, :, :], bcast(io[:, 0:NBLK].unsqueeze(1), [P, 8, NBLK]), bcast(blk[:, :].unsqueeze(2), [P, 8, NBLK]), ALU.is_equal))
                for t in range(TT):
                    ins = ve.tensor_scalar(bhot[:, 2 * t:2 * t + 2, :], bhot[:, 2 * t:2 * t + 2, :], tokid[:, t:t + 1], None, ALU.mult)
                ins.then_inc(s["plan_v"], 1)
                ce = cmp[:, :].rearrange("p (b e) -> p b e", e=NX)
                st.then(ve.tensor_tensor(ce, bcast(pend[:, :].unsqueeze(1), [P, NBLK, NX]), bcast(io[:, 0:NBLK].unsqueeze(2), [P, NBLK, NX]), ALU.is_le))
                st.then(ve.tensor_reduce(bef[:, :], ce, AX.X, ALU.add))
                st.then(ve.tensor_scalar(bef[:, :], bef[:, :], float(NX - 1), None, ALU.min))
                st.then(ve.tensor_copy(bei[:, :], bef[:, :]))
                st.then(ve.tensor_scalar(cmp[:, 0:NBLK // 2], io[:, 0:NBLK // 2], 2.0, pend[:, NX - 1:NX], ALU.mult, ALU.is_lt))
                st.then(ve.tensor_reduce(nitf[:, 0:1], cmp[:, 0:NBLK // 2], AX.X, ALU.add))
                st.then(ve.tensor_copy(nit[:, 0:1], nitf[:, 0:1]))
                dve.wait_ge(s["plan_p"], 3 * L + 3)
                ve.tensor_copy(idx[:, :], ps[0:BLK, 6, 0:NBLK]).then_inc(s["plan_v"], 1)
                dve.wait_ge(s["plan_v"], PLAN_V * (L + 1))
                trips = dve.value_load(nit[0:1, 0:1], min_val=1, max_val=NROW // BLK // 2)

                def take_rows(b, turned):
                    dve.wait_ge(s["xg_turned"], turned)
                    ve.tensor_copy(xgT[b][:, :, :], ps[:, b, :].rearrange("p (k c) -> p k c", k=KD)).then_inc(s["xgT_in"], 1)

                take_rows(0, before + (L + 2))
                with dve.Fori(0, trips) as i:
                    for b in range(2):
                        k = i * 2 + (before + b)
                        take_rows(1 - b, k + (L + 3))
                        dve.wait_ge(s["sl_in"], k + 1)
                        ve.tensor_tensor(act_[b][:, :, :], ps[:, 4 + b, :].rearrange("p (f c) -> p f c", f=4)[:, :, BLK:2 * BLK],
                                         sl[b][:, :, :], ALU.mult).then_inc(s["act_in"], 1)
                dve.wait_ge(s["y_back"], 16 * 8 * (L + 1))
                for t in range(TT):
                    st.then(ve.tensor_scalar(yg[2 * t][:, :], yg[2 * t][:, :], gate[:, t, 0:1], None, ALU.mult))
                    ve.scalar_tensor_tensor(yg[2 * t][:, :], yg[2 * t + 1][:, :], gate[:, t, 1:2], yg[2 * t][:, :], ALU.mult, ALU.add).then_inc(s["y_sum"], 1)
                for k in range(KD):
                    dve.wait_ge(s["y_turned"], KD * L + k + 1)
                    ve.tensor_tensor(XT[:, k, :], ps[:, k, :], XT[:, k, :], ALU.add).then_inc(s["xt_ready"], 1)
                return trips

            even()
            cross(0)
            before = moe(0, 0) * 2
            odd()
            cross(1)
            moe(1, before)
            norm(XT, HT, SEQ, "norm_final", 0)


_INS = ["x", "mem", "norm_mix", "norm_xattn", "norm_moe", "norm_final", "ev_w_in", "ev_sinks", "ev_mu", "ev_w0", "ev_w2",
        "ev_a0", "ev_a2", "ev_g2", "ev_k_k", "ev_k_a", "ev_r_k", "ev_lnx_w", "ev_lnx_b", "ev_w_out", "od_w_in",
        "od_gate_up", "od_gate_b", "od_onorm", "od_w_out", "mem_norm", "mem_wk", "mem_wv", "xa_wq", "xa_wo",
        "moe_w_group", "moe_b_group", "moe_w_expert", "moe_b_expert", "moe_w1", "moe_w3", "moe_w2"]


def kernel(**inputs):
    import numpy as _np
    import concourse.bacc as _bacc
    from concourse import mybir as _mybir
    from concourse.bass_utils import run_bass_kernel_spmd as _run

    nc = _bacc.Bacc("TRN2", target_bir_lowering=False, num_devices=1)
    arrays, args = {}, {}
    for name in _INS:
        arr = _np.ascontiguousarray(inputs[name])
        arrays[f"in_{name}"] = arr
        args[name] = nc.dram_tensor(f"in_{name}", arr.shape, _mybir.dt.from_np(arr.dtype), kind="ExternalInput").ap()
    hrows = nc.dram_tensor("hrows", (SEQ, D), F32, kind="Internal").ap()
    yrows = nc.dram_tensor("yrows", (NROW, D), F32, kind="Internal").ap()
    out = nc.dram_tensor("out_0", (1, SEQ, D), F32, kind="ExternalOutput").ap()
    trunk(nc, args, hrows, yrows, out)
    r = _run(nc, [arrays], core_ids=[0])
    return r.results[0]["out_0"]
```

```python
from contextlib import ExitStack

import concourse.bass as bass
from concourse import mybir
from concourse.alu_op_type import AluOpType as ALU

F32 = mybir.dt.float32
I32 = mybir.dt.int32
U32 = mybir.dt.uint32
ACT = mybir.ActivationFunctionType
AX = mybir.AxisListType

P = 128
SEQ, D, MEM = 512, 1024, 256
KD = D // P
TT = SEQ // P
MT = MEM // P
HD = 64
CH = 128
NCH = SEQ // CH
LEVELS = 7
EPS = 1e-6
GN_EPS = 64e-5
DECAY = 0.6065306597126334
GATE_NORM = 16.0
NEG = -1e30
NG, NE, NX = 4, 8, 32
NR = NG + NX
BLK = 64
NBLK = 52
NPAIR = NBLK // 2
MAX_TRIPS = 24
FF = 512

PARAMS = {}
NPAR = 0
for _name, _n in (("norm_mix", 16), ("norm_xattn", 16), ("norm_moe", 16), ("norm_final", 8), ("mem_norm", 8),
                  ("ev_mu", 14), ("ev_w0", 4), ("ev_a0", 4), ("ev_k_k", 4), ("ev_k_a", 4), ("ev_r_k", 4),
                  ("ev_lnx_w", 4), ("ev_lnx_b", 4), ("od_gate_b", 4), ("od_onorm", 2)):
    PARAMS[_name] = (NPAR, _n)
    NPAR += _n

LOADS = [("ev_q", 2), ("ev_kvx", 0), ("ev_r", 1), ("ev_k", 2), ("ev_v", 0), ("ev_o0", 1), ("ev_o1", 2),
         ("xk", 0), ("xv", 1), ("xq0", 2), ("xo0", 0),
         ("od_q", 0), ("od_k", 1), ("od_v0", 2), ("od_v1", 0), ("od_gd", 1), ("od_og0", 2), ("od_og1", 0),
         ("od_o0", 1), ("od_o1", 2), ("xq1", 0), ("xo1", 1)]
LAYER0_LOADS = 11
DMAS_OF = {"ev_q": 16, "ev_kvx": 2, "ev_o0": 3, "ev_o1": 3}


DONE = {"ev_q": ("proj_done", 4), "ev_kvx": ("proj_done", 8), "ev_r": ("proj_done", 12), "ev_k": ("proj_done", 16),
        "ev_v": ("proj_done", 20), "ev_o0": ("res_done", 8), "ev_o1": ("res_done", 8),
        "xk": ("proj_done", 32), "xv": ("proj_done", 34), "xq0": ("proj_done", 38), "xo0": ("res_done", 16),
        "od_q": ("proj_done", 42), "od_k": ("proj_done", 46), "od_v0": ("proj_done", 50), "od_v1": ("proj_done", 54),
        "od_gd": ("proj_done", 55), "od_og0": ("proj_done", 63), "od_og1": ("proj_done", 67),
        "od_o0": ("res_done", 24), "od_o1": ("res_done", 24), "xq1": ("proj_done", 71), "xo1": ("res_done", 32)}
PLAN_V = 5


def use_of(name):
    slot, loaded, former = dict(LOADS)[name], 0, None
    for n, sl in LOADS:
        if sl == slot:
            loaded += 16 * DMAS_OF.get(n, 1)
            if n == name:
                return slot, loaded, former
            former = DONE[n]


class Steps:

    def __init__(self, eng, sem):
        self.eng, self.sem, self.n, self.base = eng, sem, 0, 0

    def did(self, ins):
        ins.then_inc(self.sem, 1)
        self.n += 1

    def settle(self):
        self.eng.wait_ge(self.sem, self.base + self.n)

    def then(self, ins):
        self.did(ins)
        self.settle()

    def enter(self, i, per):
        self.outer, self.per = self.base + self.n, per
        self.base, self.n = i * per + self.outer, 0

    def leave(self, trips):
        assert self.n == self.per, (self.n, self.per)
        self.base, self.n = 0, self.outer + trips * self.per


def halves(ap, l):
    blocks = ap.rearrange("p (b h w) -> p b h w", h=2, w=1 << l)
    return blocks[:, :, 0, :], blocks[:, :, 1, :]


def trunk(nc, a, hrows, out):
    with ExitStack() as ctx:
        KB = 1024
        cursor = [16512]

        def sb(name, shape, dt=F32, at=None):
            size = 4
            for n in shape[1:]:
                size *= n
            if at is None:
                at = cursor[0]
                cursor[0] += -(-size // 32) * 32
            return nc.alloc_sbuf_tensor_at(name, shape, dt, offset=at, align_bytes=4)

        XT = sb("XT", [P, KD, SEQ])
        HT_AT = cursor[0]
        HT = sb("HT", [P, KD, SEQ])
        RING = cursor[0]
        W = [sb(f"W{i}", [P, 4096]) for i in range(6)]
        W8 = [w[:, :].rearrange("p (k n) -> p k n", k=8) for w in W]
        W4 = [w[:, :].rearrange("p (k n) -> p k n", k=4) for w in W]
        WORK = cursor[0]
        cursor[0] += 72 * KB
        ident = sb("ident", [P, P])
        ones = sb("ones", [P, P])
        pair = sb("pair", [P, P])
        tri = sb("tri", [P, 2, P])
        level = sb("level", [P, LEVELS, P])
        par = sb("par", [P, NPAR])
        omu = sb("omu", [P, 14])
        oka = sb("oka", [P, 4])
        bc = sb("bc", [P, 80])
        cst = sb("cst", [P, 2])
        small = sb("small", [P, 10, 8])
        assert cursor[0] <= nc.sbuf_usable_end, cursor[0]
        rs = sb("rs", [P, SEQ], at=WORK + 62 * KB)

        def col(name, k):
            c = PARAMS[name][0] + k
            return par[:, c:c + 1]

        xin = sb("xin", [P, TT, D], at=WORK + 8 * KB)
        prow = sb("prow", [NPAR, P], at=WORK)
        brow = sb("brow", [1, 80], at=WORK + KB)
        Rt = sb("Rt", [P, 4, SEQ], at=WORK)
        Kt = sb("Kt", [P, 4, SEQ], at=WORK + 8 * KB)
        Vt = sb("Vt", [P, 4, SEQ], at=WORK + 16 * KB)
        KKt = sb("KKt", [P, 4, SEQ], at=WORK + 24 * KB)
        At = sb("At", [P, 4, SEQ], at=WORK + 32 * KB)
        SGt = sb("SGt", [P, 4, SEQ], at=WORK + 40 * KB)
        SO = sb("SO", [P, 4, SEQ], at=WORK + 48 * KB)
        X2 = sb("X2", [P, 2, SEQ], at=WORK + 56 * KB)
        shf = sb("shf", [P, 2, SEQ], at=WORK + 60 * KB)
        lora = sb("lora", [P, 2, SEQ], at=WORK + 64 * KB)
        S3 = RING + 48 * KB
        sqT = sb("sqT", [P, 4, SEQ], at=S3)
        skT = sb("skT", [P, 5 * P], at=S3 + 8 * KB)
        sv = sb("sv", [P, 5, P], at=S3 + 8 * KB + 2560)
        smask = sb("smask", [P, 2, 2 * P], at=S3 + 14 * KB)
        sp = sb("sp", [P, 8, 2 * P], at=S3 + 16 * KB)
        spT = sb("spT", [P, 16 * P], at=S3 + 24 * KB)
        AR = sb("AR", [P, 4, 2, CH], at=S3)
        BT = sb("BT", [P, 4, CH], at=S3 + 4 * KB)
        KT = sb("KT", [P, 4, CH], at=S3 + 6 * KB)
        TOK = sb("TOK", [P, 4, 512], at=S3 + 8 * KB)
        MA = sb("MA", [P, 4, 2, 2, CH], at=S3 + 16 * KB)
        MK = sb("MK", [P, 4, 2, 2, CH], at=S3 + 24 * KB)
        XI = [sb(f"XI{r}", [P, 4, CH], at=S3 + (32 + 8 * r) * KB) for r in range(2)]
        XJ = [sb(f"XJ{r}", [P, 4, CH], at=S3 + (34 + 8 * r) * KB) for r in range(2)]
        TL = [sb(f"TL{r}", [P, 4, CH], at=S3 + (36 + 8 * r) * KB) for r in range(2)]
        UL = [sb(f"UL{r}", [P, 4, CH], at=S3 + (38 + 8 * r) * KB) for r in range(2)]
        AKV = sb("AKV", [P, 512], at=HT_AT)
        WT = sb("WT", [P, 4, CH], at=HT_AT + 2 * KB)
        Us = sb("Us", [P, 4, 2, HD], at=HT_AT + 4 * KB)
        CS = sb("CS", [P, 4, CH], at=HT_AT + 6 * KB)
        Dp = sb("Dp", [P, 4, CH], at=WORK + 60 * KB)
        Em = sb("Em", [P, 4, CH], at=WORK + 62 * KB)
        St = sb("St", [P, 4, HD], at=WORK + 64 * KB)
        Sn = sb("Sn", [P, 4, HD], at=WORK + 65 * KB)
        VC = sb("VC", [P, 4, CH], at=WORK + 68 * KB)
        Ep = sb("Ep", [P, 4, CH], at=WORK + 70 * KB)
        Epp = Dp
        mid = small[:, 0, 0:4]
        pc = small[:, 1, 0:4]
        fc = small[:, 2, 0:4]
        smx = small[:, 3, :]
        snm = small[:, 4, :]
        ses = small[:, 5, :]
        sden = small[:, 6, :]
        srec = small[:, 7, :]
        gq = sb("gq", [P, 4, SEQ], at=WORK)
        gk = sb("gk", [P, 4, SEQ], at=WORK + 8 * KB)
        gv = sb("gv", [P, TT, D], at=WORK + 16 * KB)
        gl = sb("gl", [P, 4, SEQ], at=WORK + 32 * KB)
        og = sb("og", [P, KD, SEQ], at=WORK + 40 * KB)
        gup = sb("gup", [16, SEQ], at=WORK + 56 * KB)
        gdT = sb("gdT", [16, SEQ], at=WORK + 58 * KB)
        gz = sb("gz", [P, 4, SEQ], at=S3)
        ge = sb("ge", [P, 4, SEQ], at=S3 + 8 * KB)
        gqc = sb("gqc", [P, 4, CH], at=S3 + 16 * KB)
        gkc = sb("gkc", [P, 4, CH], at=S3 + 18 * KB)
        gkt = sb("gkt", [P, 512], at=S3 + 20 * KB)
        gat = sb("gat", [P, 4, CH], at=S3 + 22 * KB)
        gvc = sb("gvc", [P, D], at=S3 + 24 * KB)
        gcs = sb("gcs", [P, 4, CH], at=S3 + 28 * KB)
        gep = sb("gep", [P, 4, CH], at=S3 + 30 * KB)
        gem = sb("gem", [P, 4, CH], at=S3 + 32 * KB)
        gst = sb("gst", [P, 4, 256], at=S3 + 34 * KB)
        gsn = sb("gsn", [P, 4, 256], at=S3 + 38 * KB)
        gsq = sb("gsq", [P, KD, SEQ], at=WORK)
        grs = sb("grs", [P, 4, SEQ], at=WORK + 16 * KB)
        mkT = sb("mkT", [P, 4, MEM], at=WORK + 64 * KB)
        mv = sb("mv", [P, MT, 512], at=WORK + 68 * KB)
        memin = sb("memin", [P, MT, D], at=WORK)
        memT = sb("memT", [P, KD, MEM], at=WORK + 8 * KB)
        memN = sb("memN", [P, KD, MEM], at=WORK + 16 * KB)
        xq = sb("xq", [P, 4, SEQ], at=WORK + 24 * KB)
        xo = sb("xo", [P, 4, SEQ], at=WORK + 32 * KB)
        xp = sb("xp", [P, 2, 4, MEM], at=WORK + 40 * KB)
        xpT = HT
        wr = sb("wr", [P, KD, NR], at=WORK)
        hk = sb("hk", [P, TT, D], at=WORK + 4 * KB)
        lg = sb("lg", [P, TT, NR], at=WORK + 20 * KB)
        M0 = WORK + 20 * KB + 1024
        glp = sb("glp", [P, TT, 8], at=M0)
        g8 = sb("g8", [P, TT, 8], at=M0 + 128)
        gi8 = sb("gi8", [P, TT, 8], U32, at=M0 + 256)
        ein = sb("ein", [P, TT, 8], at=M0 + 384)
        e8 = sb("e8", [P, TT, 8], at=M0 + 512)
        ei8 = sb("ei8", [P, TT, 8], U32, at=M0 + 640)
        gidx = sb("gidx", [P, TT], at=M0 + 768)
        ogh = sb("ogh", [P, TT, 4], at=M0 + 784)
        gex = sb("gex", [P, TT, 4], at=M0 + 848)
        pg = sb("pg", [P, TT], at=M0 + 912)
        dv = sb("dv", [P, TT], at=M0 + 928)
        ee = sb("ee", [P, TT], at=M0 + 944)
        gate = sb("gate", [P, TT, 2], at=M0 + 960)
        eid = sb("eid", [P, TT, 2], at=M0 + 992)
        M1 = M0 + 1024
        oh = sb("oh", [P, TT, 2, NX], at=M1)
        msk = sb("msk", [P, TT, NX], at=M1 + 1024)
        rk = sb("rk", [P, TT, NX], at=M1 + 1536)
        cn = sb("cn", [P, NX], at=M1 + 2048)
        nb = sb("nb", [P, NX], at=M1 + 2176)
        pend = sb("pend", [P, NX], at=M1 + 2304)
        pst = sb("pst", [P, NX], at=M1 + 2432)
        selr = sb("selr", [P, 8], at=M1 + 2560)
        selp = sb("selp", [P, 8], at=M1 + 2592)
        rq = sb("rq", [P, 8], at=M1 + 2624)
        blk = sb("blk", [P, 8], at=M1 + 2656)
        brk = sb("brk", [P, 8], at=M1 + 2688)
        idc = sb("idc", [P, 1], I32, at=M1 + 2720)
        nit = sb("nit", [P, 2], I32, at=M1 + 2752)
        nitf = sb("nitf", [P, 2], at=M1 + 2760)
        bei = sb("bei", [P, NBLK], I32, at=M1 + 2816)
        bef = sb("bef", [P, NBLK], at=M1 + 3072)
        idx = sb("idx", [P, NPAIR], I32, at=M1 + 3328)
        slot_gate = sb("slot_gate", [P, NPAIR], at=M1 + 3328 + 256)
        io = sb("io", [P, SEQ], at=M1 + 4096)
        M2 = M1 + 4096 + 2048
        io64 = sb("io64", [P, 8], at=M2)
        tokid = sb("tokid", [P, TT], at=M2 + 32)
        rhot = sb("rhot", [P, 8, BLK], at=M2 + 64)
        bhot = sb("bhot", [P, 8, NBLK], at=M2 + 64 + 2048)
        cmp = sb("cmp", [P, NBLK * NX], at=M2 + 64 + 4096)
        bgate = sb("bgate", [P, 8, NBLK], at=M2 + 64 + 4096 + 4 * NBLK * NX)
        slot_tok = sb("slot_tok", [P, NPAIR], at=M2 + 64 + 4096 + 4 * NBLK * (NX + 8))
        M3 = WORK + 42 * KB
        assert M2 + 64 + 4096 + 4 * NBLK * (NX + 9) <= M3
        xg = sb("xg", [P, D], at=M3)
        xgT = sb("xgT", [P, KD, P], at=M3 + 4 * KB)
        ysb = sb("ysb", [P, D], at=M3 + 8 * KB)
        hs = [sb(f"hs{b}", [P, FF], at=M3 + 12 * KB + 2 * KB * b) for b in range(2)]
        sl = [sb(f"sl{b}", [P, 4, BLK], at=M3 + 16 * KB + KB * b) for b in range(2)]
        act_ = [sb(f"act{b}", [P, 4, BLK], at=M3 + 18 * KB + KB * b) for b in range(2)]
        spread = sb("spread", [P, SEQ], at=M3 + 20 * KB)
        osb = sb("osb", [P, TT, D], at=WORK)

        ps = ctx.enter_context(nc.psum_tensor("ps", [P, 8, 512], F32))

        s = {n: ctx.enter_context(nc.semaphore(n)) for n in (
            "v_step", "a_step", "g_step",
            "consts", "par_in", "par_turned", "par_ready", "x_in", "x_turned", "lora_in",
            "xt_ready", "sq_ready", "sum_ready", "rstd_ready", "h_ready", "proj_done", "proj_taken", "res_done",
            "sm_scored", "sm_max", "sm_exp", "sm_norm", "sm_turned", "sm_pt", "sm_pv", "sm_out", 
            "shifted", "pre_v", "pre_a", "pre_p", "post_v", "post_a", "post_p",
            "ck_cs", "ck_exp", "ck_el", "ck_vc", "ck_turned", "ck_tok", "ck_mat", "ck_masked", "ck_y", "ck_y_in", "ck_s",
            "iv_tl", "iv_u", "iv_ul", "iv_v", "iv_x", "gst_read", "akv_done", "akv_in", "wt_done", "wt_in", "u_done", "u_in",
            "mem_in", "mem_turned", "gup_in",
            "wr_in", "plan_v", "plan_a", "plan_p", "plan_g", "h_turned", "h_taken", "h_stored",
            "xg_turned", "xgT_in", "hh_done", "hs_in", "hs_turned", "sl_in", "act_in", "y_done", "y_in",
            "xg_in", "spread_in", "added", "add_in", "last_added", "gb_step", "go",
            "f_turned", "f_taken", "out_stored")}
        w_loaded = [ctx.enter_context(nc.semaphore(f"w_loaded{i}")) for i in range(3)]
        w13_in, w2_in = ([ctx.enter_context(nc.semaphore(f"{n}{b}")) for b in range(2)] for n in ("w13_in", "w2_in"))
        block = ctx.enter_context(nc.Block())

        @block.sync
        def _(sp):
            sources = {
                "ev_kvx": [(W8[0][:, :, 0:256], a["ev_w_in"][0][:, 512:768]), (W8[0][:, :, 256:512], a["ev_w_in"][0][:, 2304:2560])],
                "ev_r": [(W8[1], a["ev_w_in"][0][:, 768:1280])],
                "ev_k": [(W8[2], a["ev_w_in"][0][:, 1280:1792])],
                "ev_v": [(W8[0], a["ev_w_in"][0][:, 1792:2304])],
                "xk": [(W8[0], a["mem_wk"])], "xv": [(W8[1], a["mem_wv"])],
                "xq0": [(W8[2], a["xa_wq"][0])], "xq1": [(W8[0], a["xa_wq"][1])],
                "xo0": [(W4[0], a["xa_wo"][0])], "xo1": [(W4[1], a["xa_wo"][1])],
                "od_q": [(W8[0], a["od_w_in"][0][:, 0:512])], "od_k": [(W8[1], a["od_w_in"][0][:, 512:1024])],
                "od_v0": [(W8[2], a["od_w_in"][0][:, 1024:1536])], "od_v1": [(W8[0], a["od_w_in"][0][:, 1536:2048])],
                "od_gd": [(W8[1][:, :, 0:16], a["od_w_in"][0][:, 2048:2064])],
                "od_og0": [(W8[2], a["od_w_in"][0][:, 2064:2576])], "od_og1": [(W8[0], a["od_w_in"][0][:, 2576:3088])],
                "od_o0": [(W8[1], a["od_w_out"][0][:, 0:512])], "od_o1": [(W8[2], a["od_w_out"][0][:, 512:1024])],
            }
            sources["ev_q"] = [(W8[2].rearrange("p k (j g d) -> p k j g d", j=4, g=2)[:, k, :, g, :],
                                a["ev_w_in"][0][k * P:k * P + P, 256 * g:256 * g + 256].rearrange("p (j d) -> p j d", j=4))
                               for k in range(KD) for g in range(2)]
            for h, name in enumerate(("ev_o0", "ev_o1")):
                w = a["ev_w_out"][0][:, 512 * h:512 * h + 512]
                dst = W8[dict(LOADS)[name]]
                sources[name] = [(dst[0:64, 0:4, :], w[0:256, :].rearrange("(j d) n -> d j n", d=HD)),
                                 (dst[64:128, 0:4, :], w[256:512, :].rearrange("(j d) n -> d j n", d=HD)),
                                 (dst[:, 4:8, :], w[512:1024, :].rearrange("(k p) n -> p k n", p=P))]

            def load(name):
                slot, _, former = use_of(name)
                if former:
                    sp.wait_ge(s[former[0]], former[1])
                for dst, src in sources[name]:
                    if len(dst.shape) == 3 and len(src.shape) == 2:
                        src = src.rearrange("(k p) n -> p k n", p=P)
                    sp.dma_start(dst, src).then_inc(w_loaded[slot], 16)

            def experts(L, pairs):
                before = pairs * 2
                sp.wait_ge(s["plan_v"], PLAN_V * (L + 1))
                trips = sp.value_load(nit[0:1, 0:1], min_val=1, max_val=MAX_TRIPS)
                sp.wait_ge(s["hh_done"], before + (L + 2))
                sp.sem_inc(s["go"], 1)
                with sp.Fori(0, trips) as i:
                    for b in range(2):
                        n = i * 2 + b
                        e = sp.value_load(bei[0:1, bass.ds(n, 1)], min_val=0, max_val=NX - 1)
                        w1, w3, w2 = (a[k][L][bass.ds(e, 1)][0].rearrange("(k p) n -> p k n", p=P) for k in ("moe_w1", "moe_w3", "moe_w2"))
                        sp.wait_ge(s["hh_done"], n + (before + L + 1))
                        sp.dma_start(W8[3 * b], w1).then_inc(w13_in[b], 16)
                        sp.dma_start(W8[3 * b + 1], w3).then_inc(w13_in[b], 16)
                        sp.wait_ge(s["y_done"], n + (before + L + 1))
                        sp.dma_start(W4[3 * b + 2], w2).then_inc(w2_in[b], 16)
                return trips

            for i, (name, _) in enumerate(LOADS[:LAYER0_LOADS]):
                load(name)
            pairs = experts(0, 0)
            sp.wait_ge(s["y_done"], pairs * 2 + 2)
            for name, _ in LOADS[LAYER0_LOADS:]:
                load(name)
            experts(1, pairs)
            dst = out[0].rearrange("(t p) d -> t p d", p=P)
            for t in range(TT):
                sp.wait_ge(s["f_taken"], t + 1)
                sp.dma_start(dst[t], osb[:, t, :]).then_inc(s["out_stored"], 16)
            sp.wait_ge(s["out_stored"], 16 * TT)

        @block.gpsimd
        def _(pool):
            st = Steps(pool, s["g_step"])
            g = nc.gpsimd
            st.then(g.memset(ident[:, :], 0.0))
            st.then(g.affine_select(out=ident[:, :], in_=ident[:, :], compare_op=ALU.not_equal, fill=1.0, base=0,
                                    pattern=[[-1, P]], channel_multiplier=1))
            st.then(g.memset(ones[:, :], 1.0))
            st.then(g.memset(cst[:, 0:1], EPS))
            st.then(g.memset(cst[:, 1:2], GN_EPS))
            st.then(g.memset(pair[:, :], 0.0))
            for r in range(2):
                st.then(g.memset(pair[64 * r:64 * r + 64, 64 * r:64 * r + 64], 1.0))
            for v in range(2):
                st.then(g.memset(tri[:, v, :], 1.0))
                st.then(g.affine_select(out=tri[:, v, :], in_=tri[:, v, :], compare_op=ALU.is_ge, fill=0.0, base=v - 1,
                                        pattern=[[1, P]], channel_multiplier=-1))
            st.then(g.memset(level[:, :, :], 0.0))
            for l in range(LEVELS):
                h = 1 << l
                half = level[:, l, :].rearrange("p (b h w) -> p b h w", h=2, w=h)[:, :, 1, :]
                st.then(g.memset(half, 1.0))
                st.then(g.affine_select(out=half, in_=half, compare_op=ALU.is_ge, fill=0.0, base=0,
                                        pattern=[[-2 * h, P // (2 * h)], [0, h]], channel_multiplier=1))
                st.then(g.affine_select(out=half, in_=half, compare_op=ALU.is_ge, fill=0.0, base=h - 1,
                                        pattern=[[2 * h, P // (2 * h)], [0, h]], channel_multiplier=-1))
            st.then(g.memset(smask[:, :, :], 0.0))
            st.then(g.affine_select(out=smask[:, 1, 0:P], in_=smask[:, 1, 0:P], compare_op=ALU.is_ge, fill=NEG, base=-1,
                                    pattern=[[1, P]], channel_multiplier=-1))
            for v in range(2):
                st.then(g.affine_select(out=smask[:, v, P:2 * P], in_=smask[:, v, P:2 * P], compare_op=ALU.is_ge, fill=NEG,
                                        base=0, pattern=[[-1, P]], channel_multiplier=1))
            st.then(g.memset(smask[:, 0, 0:P], NEG))
            st.then(g.memset(skT[:, 0:P], 0.0))
            g.memset(sv[:, 0, :], 0.0).then_inc(s["consts"], 1)

            def even():
                with pool.Fori(0, NCH) as c:
                    pool.wait_ge(s["pre_v"], 2)
                    pool.wait_ge(s["ck_turned"], c * 4 + 1)
                    g.tensor_copy(VC[:, :, :], Vt[:, :, bass.ds(c * CH, CH)]).then_inc(s["ck_vc"], 1)

            def odd():
                with pool.Fori(0, NCH) as c:
                    pool.wait_ge(s["proj_taken"], DONE["od_v1"][1])
                    pool.wait_ge(s["ck_s"], c + NCH)
                    g.tensor_copy(gvc[:, :], gv[:, bass.ds(c, 1), :].rearrange("p a d -> p (a d)")).then_inc(s["ck_vc"], 1)

            def moe(L, pairs):
                pool.wait_ge(s["h_ready"], 8 * (4 + 3 * L))
                st.then(g.iota(io[:, :], pattern=[[1, SEQ]], base=0, channel_multiplier=0, allow_small_or_imprecise_dtypes=True))
                st.then(g.iota(io64[:, :], pattern=[[64, 8]], base=0, channel_multiplier=0, allow_small_or_imprecise_dtypes=True))
                g.iota(tokid[:, :], pattern=[[P, TT]], base=0, channel_multiplier=1,
                       allow_small_or_imprecise_dtypes=True).then_inc(s["plan_g"], 1)
                pool.wait_ge(s["plan_v"], PLAN_V * (L + 1))
                pool.wait_ge(s["h_stored"], 16 * TT * (L + 1))
                trips = pool.value_load(nit[0:1, 0:1], min_val=1, max_val=MAX_TRIPS)

                def gather(column):
                    st2.then(g.tensor_copy(idc[:, :], column))
                    pool.sem_inc(s["go"], 1)
                    g.indirect_dma_start(out=xg[:, :], out_offset=None, in_=hrows[:, :],
                                         in_offset=bass.IndirectOffsetOnAxis(ap=idc[:, :], axis=0)).then_inc(s["xg_in"], 16)

                st2 = Steps(pool, s["gb_step"])
                st2.base = pairs + L
                gather(idx[:, 0:1])
                with pool.Fori(0, trips) as i:
                    st2.enter(i, 1)
                    pool.wait_ge(s["xg_in"], (i + (pairs + L + 1)) * 16)
                    pool.wait_ge(s["xg_turned"], i + (pairs + L + 2))
                    gather(idx[:, bass.ds(i + 1, 1)])
                pool.wait_ge(s["xg_in"], (trips + 1 + pairs + L) * 16)
                pool.sem_inc(s["go"], 1)
                return trips

            even()
            pairs = moe(0, 0)
            odd()
            moe(1, pairs)

        @block.scalar
        def _(act):
            st = Steps(act, s["a_step"])
            sc = nc.scalar
            n = {"proj": 0, "norm": 0, "xt": 8}

            act.sem_inc(s["ck_y_in"], 1)
            act.sem_inc(s["y_in"], 1)
            act.dma_start(xin[:, :, :], a["x"][0].rearrange("(t p) d -> p t d", p=P)).then_inc(s["x_in"], 16)
            for name, (c0, k) in PARAMS.items():
                src = a[name]
                while len(src.shape) > 1:
                    src = src.rearrange({2: "a b -> (a b)", 3: "a b c -> (a b c)"}[len(src.shape)])
                act.dma_start(prow[c0:c0 + k, :], src.rearrange("(r p) -> r p", p=P)).then_inc(s["par_in"], 16)
            act.dma_start(brow[0:1, 0:8], a["ev_sinks"]).then_inc(s["par_in"], 16)
            for L in range(2):
                o = 8 + NR * L
                act.dma_start(brow[0:1, o:o + NG], a["moe_b_group"][L:L + 1, :]).then_inc(s["par_in"], 16)
                act.dma_start(brow[0:1, o + NG:o + NR], a["moe_b_expert"][L:L + 1, :]).then_inc(s["par_in"], 16)
            act.dma_start(lora[0:64, 0, :], a["ev_w2"][0]).then_inc(s["lora_in"], 16)
            act.dma_start(lora[64:128, 0, :], a["ev_a2"][0]).then_inc(s["lora_in"], 16)
            act.dma_start(lora[:, 1, :], a["ev_g2"][0]).then_inc(s["lora_in"], 16)

            def norm(src, dst, width, early=False):
                for q in range(4):
                    if early:
                        act.wait_ge(s["xt_ready"], n["xt"] - 6 + 2 * q)
                    sc.activation(dst[:, 2 * q:2 * q + 2, :], src[:, 2 * q:2 * q + 2, :], ACT.Square).then_inc(s["sq_ready"], 1)
                n["norm"] += 1
                act.wait_ge(s["sum_ready"], n["norm"])
                if n["norm"] > 1:
                    act.wait_ge(s["h_ready"], 8 * (n["norm"] - 1))
                inverse_root(rs[:, 0:width], ps[:, 7, 0:width], D, 0).then_inc(s["rstd_ready"], 1)

            def inverse_root(dst, src, count, eps):
                st.then(sc.activation(dst, src, ACT.Ln, bias=cst[:, eps:eps + 1], scale=1.0 / count))
                return sc.activation(dst, dst, ACT.Exp, scale=-0.5)

            def take(dst, src=None, last=True, func=ACT.Copy, **k):
                act.wait_ge(s["proj_done"], n["proj"] + 1)
                if src is None:
                    src = ps[:, n["proj"] % 2, :]
                ins = sc.activation(dst, src, func, **k)
                if last:
                    ins.then_inc(s["proj_taken"], 1)
                    n["proj"] += 1

            def even():
                norm(XT, HT, SEQ, early=True)
                act.wait_ge(s["consts"], 1)
                for j in range(4):
                    take(sqT[:, j, :])
                take(skT[:, P:5 * P])
                take(sv[:, 1:5, :].rearrange("p t n -> p (t n)"))

                def swa_exp(b):
                    act.wait_ge(s["sm_max"], b + 1)
                    for h in range(8):
                        sc.activation(sp[:, h, :], sp[:, h, :], ACT.Exp, bias=snm[:, h:h + 1], accum_out=sden[:, h:h + 1])
                    sc.activation(ses, ses, ACT.Exp).then_inc(s["sm_exp"], 1)

                def swa_pt(b):
                    act.wait_ge(s["sm_turned"], b + 1)
                    sc.activation(spT[:, :].rearrange("p (b n) -> p b n", b=4), ps[:, 4:8, :], ACT.Copy).then_inc(s["sm_pt"], 1)

                def swa_out(b):
                    act.wait_ge(s["sm_pv"], b + 1)
                    sc.activation(SO[:, :, b * P:b * P + P], ps[:, 2, :].rearrange("p (j q) -> p j q", j=4), ACT.Copy).then_inc(s["sm_out"], 1)

                tiles = [X2[:, 0, :], X2[:, 1, :]] + [t[:, j, :] for t in (Rt, Kt, Vt) for j in range(4)]
                mus = [12, 13] + list(range(12))
                for i, (dst, mu) in enumerate(zip(tiles, mus)):
                    take(dst, func=ACT.Copy, scale=omu[:, mu:mu + 1], last=False)
                    if i >= 2:
                        act.wait_ge(s["shifted"], i - 1)
                    take(shf[:, i % 2, :], func=ACT.Copy, scale=col("ev_mu", mu))
                    if i >= 4 and (i - 4) % 3 == 0:
                        swa_pt((i - 4) // 3)
                    if i >= 5 and (i - 5) % 3 == 0:
                        swa_out((i - 5) // 3)
                    if i >= 2 and (i - 2) % 3 == 0 and (i - 2) // 3 < 4:
                        swa_exp((i - 2) // 3)
                swa_out(3)

                act.wait_ge(s["shifted"], 14)
                sc.activation(X2[0:64, 0, :], X2[0:64, 0, :], ACT.Tanh).then_inc(s["pre_a"], 1)
                sc.activation(X2[:, 1, :], X2[:, 1, :], ACT.Sigmoid).then_inc(s["pre_a"], 1)
                for j in range(8):
                    act.wait_ge(s["proj_done"], n["proj"] + 1)
                    dst = (SGt, At)[j // 4][:, j % 4, :]
                    sc.activation(dst, ps[:, n["proj"] % 2, :], ACT.Sigmoid, bias=col("ev_w0", j)).then_inc(s["proj_taken"], 1)
                    n["proj"] += 1
                for j in range(4):
                    sc.activation(HT[:, j, :], Kt[:, j, :], ACT.Square, scale=col("ev_k_k", j)).then_inc(s["pre_a"], 1)

                act.wait_ge(s["pre_v"], 1)
                st.then(sc.activation(KKt[:, :, :], KKt[:, :, :], ACT.Ln))
                sc.activation(KKt[:, :, :], KKt[:, :, :], ACT.Exp, scale=-0.5).then_inc(s["pre_a"], 1)

                with act.Fori(0, NCH) as c:
                    act.wait_ge(s["ck_cs"], c + 1)
                    sc.activation(Ep[:, :, :], CS[:, :, :], ACT.Exp, scale=-DECAY)
                    sc.activation(Em[:, :, :], CS[:, :, :], ACT.Exp, scale=DECAY)
                    sc.activation(Epp[:, :, :], Dp[:, :, :], ACT.Exp, scale=-DECAY)
                    sc.activation(pc, mid, ACT.Exp, scale=-DECAY).then_inc(s["ck_exp"], 1)
                    for k in range(4):
                        act.wait_ge(s["ck_turned"], c * 4 + (k + 2))
                        sc.activation(TOK[:, k, :], ps[:, k, :], ACT.Copy).then_inc(s["ck_tok"], 1)
                    act.wait_ge(s["akv_done"], c + 1)
                    sc.activation(AKV[:, :], ps[:, 3, :], ACT.Copy).then_inc(s["akv_in"], 1)
                    for l in range(LEVELS):
                        for r in range(2):
                            k = 2 * l + r
                            act.wait_ge(s["iv_u"], c * (2 * LEVELS) + (k + 1))
                            sc.activation((XI if l == 0 else UL)[r][:, :, :].rearrange("p j t -> p (j t)"), ps[:, r, :],
                                          ACT.Copy).then_inc(s["iv_ul"], 1)
                    act.wait_ge(s["wt_done"], c + 1)
                    sc.activation(WT[:, :, :].rearrange("p j t -> p (j t)"), ps[:, 7, :], ACT.Copy).then_inc(s["wt_in"], 1)
                    act.wait_ge(s["u_done"], c + 1)
                    sc.activation(Us[:, :, :, :].rearrange("p j r v -> p r j v"),
                                  ps[:, 0:2, 0:256].rearrange("p r (j v) -> p r j v", j=4), ACT.Copy).then_inc(s["u_in"], 1)
                    act.wait_ge(s["ck_y"], c + 1)
                    sc.activation(HT[:, 4:8, bass.ds(c * CH, CH)], ps[:, 4, :].rearrange("p (j t) -> p j t", j=4),
                                  ACT.Copy).then_inc(s["ck_y_in"], 1)

                act.wait_ge(s["post_v"], 3)
                sc.activation(KKt[:, :, :], HT[:, 4:8, :], ACT.Square).then_inc(s["post_a"], 1)
                act.wait_ge(s["post_p"], 4)
                inverse_root(At[:, :, :], ps[:, 4:8, :], HD, 1).then_inc(s["post_a"], 1)
                n["xt"] += 8

            def cross(L):
                act.wait_ge(s["xt_ready"], n["xt"])
                if L == 0:
                    act.dma_start(memin[:, :, :], a["mem"][0].rearrange("(t p) d -> p t d", p=P)).then_inc(s["mem_in"], 16)
                norm(XT, HT, SEQ)
                if L == 0:
                    act.wait_ge(s["mem_turned"], 4)
                    for q in range(4):
                        st.then(sc.activation(memT[:, 2 * q:2 * q + 2, :], ps[:, q, :].rearrange("p (k t) -> p k t", k=2), ACT.Copy))
                    norm(memT, memN, MEM)
                    for j in range(4):
                        take(mkT[:, j, :], ps[:, n["proj"] % 2, 0:MEM])
                    for t in range(MT):
                        take(mv[:, t, :])
                for h in range(4):
                    take(xq[:, h, :])
                off = 4 * (L + 1)
                for t in range(TT):
                    act.wait_ge(s["sm_max"], off + t + 1)
                    for h in range(4):
                        ins = sc.activation(xp[:, t % 2, h, :], ps[:, 4 + h // 2, MEM * (h % 2):MEM * (h % 2) + MEM], ACT.Exp,
                                            bias=snm[:, h:h + 1], scale=P ** -0.5, accum_out=sden[:, h:h + 1])
                    ins.then_inc(s["sm_exp"], 1)
                    act.wait_ge(s["sm_turned"], off + t + 1)
                    sc.activation(xpT[:, :, t * P:t * P + P], ps[:, 2:4, :].rearrange("p b (c q) -> p (b c) q", c=4), ACT.Copy).then_inc(s["sm_pt"], 1)
                for h in range(4):
                    act.wait_ge(s["sm_pv"], 4 + 4 * L + h + 1)
                    sc.activation(xo[:, h, :], ps[:, 4 + h, :], ACT.Copy).then_inc(s["sm_out"], 1)
                n["xt"] += 8

            def odd():
                norm(XT, HT, SEQ, early=True)
                act.dma_start(gup[:, :], a["od_gate_up"][0]).then_inc(s["gup_in"], 16)
                for t in (gq, gk):
                    for j in range(4):
                        take(t[:, j, :])
                for h in range(2):
                    for t in range(TT):
                        take(gv[:, t, 512 * h:512 * h + 512])
                take(gdT[:, :], ps[0:16, n["proj"] % 2, :])
                for j in range(4):
                    take(gl[:, j, :], func=ACT.Identity, bias=col("od_gate_b", j))
                act.wait_ge(s["proj_taken"], n["proj"])
                st.then(sc.activation(ge[:, :, :], gl[:, :, :], ACT.Abs))
                st.then(sc.activation(ge[:, :, :], ge[:, :, :], ACT.Exp, scale=-1.0))
                sc.activation(ge[:, :, :], ge[:, :, :], ACT.Ln, bias=1.0).then_inc(s["pre_a"], 1)
                for j in range(KD):
                    take(og[:, j, :], func=ACT.Silu)
                with act.Fori(0, NCH) as c:
                    act.wait_ge(s["ck_cs"], c + (NCH + 1))
                    sc.activation(gep[:, :, :], gcs[:, :, :], ACT.Exp, scale=1.0 / GATE_NORM)
                    sc.activation(gem[:, :, :], gcs[:, :, :], ACT.Exp, scale=-1.0 / GATE_NORM)
                    sc.activation(pc, mid, ACT.Exp, scale=1.0 / GATE_NORM).then_inc(s["ck_exp"], 1)
                    act.wait_ge(s["ck_turned"], c + (4 * NCH + 2))
                    sc.activation(gkt[:, :], ps[:, 0, :], ACT.Copy).then_inc(s["ck_tok"], 1)
                    act.wait_ge(s["ck_y"], c + (NCH + 1))
                    sc.activation(HT[:, :, bass.ds(c * CH, CH)], ps[:, 2:4, :].rearrange("p b (k t) -> p (b k) t", k=4),
                                  ACT.Copy).then_inc(s["ck_y_in"], 1)
                act.wait_ge(s["ck_y_in"], 2 * NCH + 1)
                act.wait_ge(s["ck_s"], 2 * NCH)
                sc.activation(gsq[:, :, :], HT[:, :, :], ACT.Square).then_inc(s["post_a"], 1)
                act.wait_ge(s["post_p"], 5)
                inverse_root(grs[:, :, :], ps[:, 4:8, :], 256, 0).then_inc(s["post_a"], 1)
                n["xt"] += 8

            def moe(L, pairs):
                for o, k, w in ((0, NG, a["moe_w_group"]), (NG, NX, a["moe_w_expert"])):
                    act.dma_start(wr[:, :, o:o + k], w[L].rearrange("(k p) n -> p k n", p=P)).then_inc(s["wr_in"], 16)
                norm(XT, HT, SEQ, early=True)
                for t in range(TT):
                    act.wait_ge(s["h_turned"], TT * L + t + 1)
                    sc.activation(hk[:, t, :].rearrange("p (b n) -> p b n", b=2), ps[:, 2 * (t % 2):2 * (t % 2) + 2, :], ACT.Copy).then_inc(s["h_taken"], 1)
                    act.wait_ge(s["h_taken"], TT * L + t + 1)
                    act.dma_start(hrows[t * P:t * P + P, :], hk[:, t, :]).then_inc(s["h_stored"], 16)
                act.wait_ge(s["plan_v"], PLAN_V * L + 1)
                sc.activation(gex[:, :, :], gex[:, :, :], ACT.Exp).then_inc(s["plan_a"], 1)
                act.wait_ge(s["plan_v"], PLAN_V * L + 2)
                sc.activation(ee[:, :], dv[:, :], ACT.Exp).then_inc(s["plan_a"], 1)

                act.wait_ge(s["plan_v"], PLAN_V * (L + 1))
                trips = act.value_load(nit[0:1, 0:1], min_val=1, max_val=MAX_TRIPS)
                with act.Fori(0, trips) as i:
                    for b in range(2):
                        k = i * 2 + (pairs * 2 + b)
                        act.wait_ge(s["hh_done"], k + (L + 3))
                        sc.activation(hs[b][:, :], ps[:, 2 + b, :], ACT.Copy).then_inc(s["hs_in"], 1)
                        act.wait_ge(s["hs_turned"], k + 1)
                        sc.activation(sl[b][:, :, :], ps[:, 4, :].rearrange("p (f c) -> p f c", f=4)[:, :, 0:BLK], ACT.Silu).then_inc(s["sl_in"], 1)
                        act.wait_ge(s["y_done"], k + (L + 3))
                        for h in range(2):
                            ins = sc.activation(ysb[64 * b:64 * b + 64, 512 * h:512 * h + 512], ps[64 * h:64 * h + 64, 6, :], ACT.Copy)
                        ins.then_inc(s["y_in"], 1)
                n["xt"] += 8
                return trips

            even()
            cross(0)
            pairs = moe(0, 0)
            odd()
            cross(1)
            moe(1, pairs)
            norm(XT, HT, SEQ, early=True)
            for t in range(TT):
                act.wait_ge(s["f_turned"], t + 1)
                sc.activation(osb[:, t, :].rearrange("p (b n) -> p b n", b=2), ps[:, 2 * (t % 2):2 * (t % 2) + 2, :], ACT.Copy).then_inc(s["f_taken"], 1)

        @block.tensor
        def _(pe):
            te = nc.tensor
            n = {"proj": 0, "norm": 0, "h": 0, "xt": 8}

            def mm(o, l, r, first=True, last=True):
                return te.matmul(o, l, r, start=first, stop=last)

            for name in ("ck_turned", "hh_done", "y_done", "xg_turned"):
                pe.sem_inc(s[name], 1)
            pe.wait_ge(s["consts"], 1)
            pe.wait_ge(s["x_in"], 16)
            for k in range(KD):
                for t in range(TT):
                    ins = te.transpose(ps[:, k, t * P:t * P + P], xin[:, t, k * P:k * P + P], ident[:, :])
                ins.then_inc(s["x_turned"], 1)
            pe.wait_ge(s["xt_ready"], 2)
            pe.wait_ge(s["par_in"], 16 * (len(PARAMS) + 5))
            te.transpose(ps[:, 0, 0:NPAR], prow[:, :], ident[0:NPAR, 0:NPAR]).then_inc(s["par_turned"], 1)
            mm(ps[:, 1, 0:80], ones[0:1, :], brow[0:1, :]).then_inc(s["par_turned"], 1)

            def norm(dst, width):
                pe.wait_ge(s["xt_ready"], n["xt"])
                if n["norm"]:
                    pe.wait_ge(s["rstd_ready"], n["norm"])
                for q in range(4):
                    pe.wait_ge(s["sq_ready"], 4 * n["norm"] + q + 1)
                    for k in (2 * q, 2 * q + 1):
                        ins = mm(ps[:, 7, 0:width], ones[:, :], dst[:, k, :], k == 0, k == KD - 1)
                ins.then_inc(s["sum_ready"], 1)
                n["norm"] += 1

            def project(o, pairs, free=None):
                if n["proj"] >= 2:
                    pe.wait_ge(s["proj_taken"], n["proj"] - 1)
                for k, (l, r) in enumerate(pairs):
                    ins = mm(o, l, r, k == 0, k == len(pairs) - 1)
                n["proj"] += 1
                ins.then_inc(s["proj_done"], 1)

            def bank():
                return ps[:, n["proj"] % 2, :]

            def weights(name):
                slot, loaded, _ = use_of(name)
                pe.wait_ge(w_loaded[slot], loaded)
                return slot

            def residual(tiles_of, count):
                for mt in range(KD):
                    if mt >= 2:
                        pe.wait_ge(s["xt_ready"], n["xt"] + mt - 1)
                    pairs = tiles_of(mt)
                    for k, (l, r) in enumerate(pairs):
                        ins = mm(ps[:, 2 + mt % 2, :], l, r, k == 0, k == len(pairs) - 1)
                    ins.then_inc(s["res_done"], 1)
                n["xt"] += 8

            def even():
                norm(HT, SEQ)
                pe.wait_ge(s["h_ready"], 8)
                slot = weights("ev_q")
                for j in range(4):
                    project(bank(), [(W8[slot][:, k, P * j:P * j + P], HT[:, k, :]) for k in range(KD)])
                slot = weights("ev_kvx")
                project(bank(), [(W8[slot][:, k, 0:P], HT[:, k, :]) for k in range(KD)])
                pe.wait_ge(s["proj_taken"], n["proj"] - 1)
                for t in range(TT):
                    for k in range(KD):
                        ins = mm(ps[:, n["proj"] % 2, t * P:t * P + P], HT[:, k, t * P:t * P + P], W8[slot][:, k, P:2 * P],
                                 k == 0, k == KD - 1)
                n["proj"] += 1
                ins.then_inc(s["proj_done"], 1)

                def scores(b):
                    pe.wait_ge(s["proj_taken"], 5 if b == 0 else 6)
                    if b:
                        pe.wait_ge(s["sm_pt"], b)
                    for j in range(4):
                        for g in range(2):
                            r = slice(64 * g, 64 * g + 64)
                            ins = mm(ps[:, 4 + 2 * g + j // 2, 256 * (j % 2):256 * (j % 2) + 256],
                                     sqT[r, j, b * P:b * P + P], skT[r, b * P:b * P + 2 * P])
                    ins.then_inc(s["sm_scored"], 1)

                def turn(b):
                    pe.wait_ge(s["sm_norm"], b + 1)
                    for i in range(16):
                        ins = te.transpose(ps[:, 4 + i // 4, P * (i % 4):P * (i % 4) + P], sp[:, i // 2, P * (i % 2):P * (i % 2) + P], ident[:, :])
                    ins.then_inc(s["sm_turned"], 1)

                def pv(b):
                    pe.wait_ge(s["sm_pt"], b + 1)
                    if b:
                        pe.wait_ge(s["sm_out"], b)
                    for j in range(4):
                        for g in range(2):
                            for half in range(2):
                                i = 2 * (4 * g + j) + half
                                ins = mm(ps[64 * g:64 * g + 64, 2, j * P:j * P + P], sv[:, b + half, 64 * g:64 * g + 64],
                                         spT[:, P * i:P * i + P], half == 0, half == 1)
                    ins.then_inc(s["sm_pv"], 1)

                i = 0
                for name, off, k_tiles in (("ev_kvx", 256, 2), ("ev_r", 0, 4), ("ev_k", 0, 4), ("ev_v", 0, 4)):
                    slot = weights(name)
                    for j in range(k_tiles):
                        o = off + j * P
                        project(bank(), [(W8[slot][:, k, o:o + P], HT[:, k, :]) for k in range(KD)])
                        if i >= 4 and (i - 4) % 3 == 0:
                            turn((i - 4) // 3)
                        if i >= 5 and (i - 5) % 3 == 0:
                            pv((i - 5) // 3)
                        if i >= 2 and (i - 2) % 3 == 0 and (i - 2) // 3 < 4:
                            scores((i - 2) // 3)
                        i += 1
                pv(3)

                pe.wait_ge(s["lora_in"], 48)
                pe.wait_ge(s["pre_a"], 1)
                for r in range(2):
                    q = slice(64 * r, 64 * r + 64)
                    for j in range(4):
                        project(bank(), [(lora[q, 0, j * P:j * P + P], X2[q, 0, :])])
                for j in range(4):
                    pe.wait_ge(s["pre_a"], 3 + j)
                    mm(ps[:, 4 + j, :], pair[:, :], HT[:, j, :]).then_inc(s["pre_p"], 1)

                with pe.Fori(0, NCH) as c:
                    pe.wait_ge(s["ck_el"], c + 1)
                    pe.wait_ge(s["ck_vc"], c + 1)
                    pe.wait_ge(s["ck_y_in"], c + 1)
                    for k, src in enumerate((AR[:, :, 0, :], BT[:, :, :], KT[:, :, :], VC[:, :, :])):
                        for j in range(4):
                            ins = te.transpose(ps[:, k, j * P:j * P + P], src[:, j, :], ident[:, :])
                        ins.then_inc(s["ck_turned"], 1)
                    for x, lt in enumerate((BT, KT)):
                        for q in range(2):
                            for r in range(2):
                                if x:
                                    pe.wait_ge(s["ck_masked"], c * 8 + (2 * q + r + 1))
                                rr = slice(64 * r, 64 * r + 64)
                                for j in (2 * q, 2 * q + 1):
                                    ins = mm(ps[:, 4 + 2 * q + r, 256 * (j % 2):256 * (j % 2) + 256], lt[rr, j, :],
                                             AR[rr, j, :, :].rearrange("p x t -> p (x t)"))
                                ins.then_inc(s["ck_mat"], 1)
                    pe.wait_ge(s["ck_masked"], c * 8 + 8)
                    pe.wait_ge(s["ck_tok"], c * 4 + 4)
                    for j in range(4):
                        for r in range(2):
                            h = 64 * (2 * j + r)
                            ins = mm(ps[:, 3, h:h + 64], MK[:, j, r, 0, :], TOK[:, 3, h:h + 64])
                    ins.then_inc(s["akv_done"], 1)
                    for l in range(LEVELS):
                        for r in range(2):
                            k = 2 * l + r
                            pe.wait_ge(s["iv_tl"], c * (2 * LEVELS) + (k + 1))
                            if l == 1:
                                pe.wait_ge(s["iv_ul"], c * (2 * LEVELS) + (r + 1))
                            if l > 1:
                                pe.wait_ge(s["iv_x"], c * (2 * LEVELS - 2) + (k - 3))
                            for j in range(4):
                                o = ps[:, r, j * P:j * P + P]
                                if l == 0:
                                    ins = te.transpose(o, XJ[r][:, j, :], ident[:, :])
                                else:
                                    ins = mm(o, TL[r][:, j, :], XI[r][:, j, :])
                            ins.then_inc(s["iv_u"], 1)
                        if l == 0:
                            continue
                        for r in range(2):
                            k = 2 * l + r
                            pe.wait_ge(s["iv_ul"], c * (2 * LEVELS) + (k + 1))
                            for j in range(4):
                                if l < LEVELS - 1:
                                    mm(ps[:, 5 + r, j * HD:j * HD + HD], XJ[r][:, j, :], halves(UL[r][:, j, :], l)[0])
                                ins = mm(ps[:, (2, 4)[r], j * HD:j * HD + HD], UL[r][:, j, :], halves(XJ[r][:, j, :], l)[1])
                            ins.then_inc(s["iv_v"], 1)
                    for r in range(2):
                        pe.wait_ge(s["iv_x"], c * (2 * LEVELS - 2) + (2 * LEVELS - 3 + r))
                        for j in range(4):
                            h = 64 * (2 * j + r)
                            ins = mm(ps[64 * r:64 * r + 64, 7, j * P:j * P + P], TOK[:, 0, h:h + 64], XJ[r][:, j, :])
                    ins.then_inc(s["wt_done"], 1)
                    pe.wait_ge(s["akv_in"], c + 1)
                    pe.wait_ge(s["wt_in"], c + 1)
                    for j in range(4):
                        for r in range(2):
                            h, rr = 64 * (2 * j + r), slice(64 * r, 64 * r + 64)
                            o = ps[:, r, j * HD:j * HD + HD]
                            mm(o, XJ[r][:, j, :], AKV[:, h:h + 64], True, False)
                            ins = mm(o, WT[rr, j, :], Sn[rr, j, :], False, True)
                    ins.then_inc(s["u_done"], 1)
                    pe.wait_ge(s["u_in"], c + 1)
                    for j in range(4):
                        for r in range(2):
                            h, rr = 64 * (2 * j + r), slice(64 * r, 64 * r + 64)
                            o = ps[rr, 4, j * P:j * P + P]
                            mm(o, Us[:, j, r, :], MA[:, j, r, 1, :], True, False)
                            mm(o, TOK[:, 3, h:h + 64], MK[:, j, r, 1, :], False, False)
                            ins = mm(o, Sn[rr, j, :], AR[rr, j, 1, :], False, True)
                    ins.then_inc(s["ck_y"], 1)
                    for j in range(4):
                        for r in range(2):
                            h, rr = 64 * (2 * j + r), slice(64 * r, 64 * r + 64)
                            o = ps[rr, 5, j * HD:j * HD + HD]
                            mm(o, TOK[:, 1, h:h + 64], Us[:, j, r, :], True, False)
                            ins = mm(o, TOK[:, 2, h:h + 64], TOK[:, 3, h:h + 64], False, True)
                    ins.then_inc(s["ck_s"], 1)

                pe.wait_ge(s["ck_y_in"], NCH + 1)
                for j in range(4):
                    ins = mm(ps[:, j, :], lora[:, 1, j * P:j * P + P], X2[:, 1, :])
                ins.then_inc(s["post_p"], 1)
                pe.wait_ge(s["post_v"], 1)
                for j in range(4):
                    ins = mm(ps[:, 4 + j, :], pair[:, :], KKt[:, j, :])
                ins.then_inc(s["post_p"], 1)
                pe.wait_ge(s["post_v"], 2)
                for j in range(4):
                    ins = mm(ps[:, 4 + j, :], pair[:, :], HT[:, 4 + j, :])
                ins.then_inc(s["post_p"], 1)
                pe.wait_ge(s["post_a"], 1)
                for j in range(4):
                    ins = mm(ps[:, 4 + j, :], pair[:, :], KKt[:, j, :])
                ins.then_inc(s["post_p"], 1)

                pe.wait_ge(s["post_v"], 4)
                slots = [weights("ev_o0"), weights("ev_o1")]
                residual(lambda mt: [(W8[slots[mt // 4]][:, k, P * (mt % 4):P * (mt % 4) + P],
                                      (SO if k < 4 else HT)[:, k, :]) for k in range(KD)], KD)

            def cross(L):
                norm(HT, SEQ)
                if L == 0:
                    pe.wait_ge(s["mem_in"], 16)
                    for q in range(4):
                        for k in (2 * q, 2 * q + 1):
                            for t in range(MT):
                                o = 256 * (k % 2) + t * P
                                ins = te.transpose(ps[:, q, o:o + P], memin[:, t, k * P:k * P + P], ident[:, :])
                        ins.then_inc(s["mem_turned"], 1)
                    norm(memN, MEM)
                    pe.wait_ge(s["h_ready"], 8 * n["norm"])
                    slot = weights("xk")
                    for j in range(4):
                        project(ps[:, n["proj"] % 2, 0:MEM], [(W8[slot][:, k, P * j:P * j + P], memN[:, k, :]) for k in range(KD)])
                    slot = weights("xv")
                    for t in range(MT):
                        project(bank(), [(memN[:, k, t * P:t * P + P], W8[slot][:, k, :]) for k in range(KD)])
                pe.wait_ge(s["h_ready"], 8 * n["norm"])
                slot = weights(f"xq{L}")
                for h in range(4):
                    project(bank(), [(W8[slot][:, k, P * h:P * h + P], HT[:, k, :]) for k in range(KD)])
                off = 4 * (L + 1)
                pe.wait_ge(s["proj_taken"], n["proj"])
                for t in range(TT):
                    if t:
                        pe.wait_ge(s["sm_exp"], off + t)
                    for h in range(4):
                        ins = mm(ps[:, 4 + h // 2, MEM * (h % 2):MEM * (h % 2) + MEM], xq[:, h, t * P:t * P + P], mkT[:, h, :])
                    ins.then_inc(s["sm_scored"], 1)
                    pe.wait_ge(s["sm_norm"], off + t + 1)
                    if t:
                        pe.wait_ge(s["sm_pt"], off + t)
                    for i in range(8):
                        ins = te.transpose(ps[:, 2 + i // 4, P * (i % 4):P * (i % 4) + P], xp[:, t % 2, i // 2, P * (i % 2):P * (i % 2) + P], ident[:, :])
                    ins.then_inc(s["sm_turned"], 1)
                pe.wait_ge(s["sm_pt"], off + TT)
                for h in range(4):
                    for t in range(MT):
                        ins = mm(ps[:, 4 + h, :], mv[:, t, P * h:P * h + P], xpT[:, 2 * h + t, :], t == 0, t == 1)
                    ins.then_inc(s["sm_pv"], 1)
                slot = weights(f"xo{L}")
                pe.wait_ge(s["sm_out"], off + TT)
                residual(lambda mt: [(W4[slot][:, k, P * mt:P * mt + P], xo[:, k, :]) for k in range(4)], 4)

            def odd():
                norm(HT, SEQ)
                pe.wait_ge(s["h_ready"], 8 * n["norm"])
                for name in ("od_q", "od_k"):
                    slot = weights(name)
                    for j in range(4):
                        project(bank(), [(W8[slot][:, k, P * j:P * j + P], HT[:, k, :]) for k in range(KD)])
                for name in ("od_v0", "od_v1"):
                    slot = weights(name)
                    for t in range(TT):
                        project(bank(), [(HT[:, k, t * P:t * P + P], W8[slot][:, k, :]) for k in range(KD)])
                slot = weights("od_gd")
                project(ps[0:16, n["proj"] % 2, :], [(W8[slot][:, k, 0:16], HT[:, k, :]) for k in range(KD)])
                pe.wait_ge(s["gup_in"], 16)
                pe.wait_ge(s["proj_taken"], n["proj"])
                for j in range(4):
                    project(bank(), [(gup[:, P * j:P * j + P], gdT[:, :])])
                for name in ("od_og0", "od_og1"):
                    slot = weights(name)
                    for j in range(4):
                        project(bank(), [(W8[slot][:, k, P * j:P * j + P], HT[:, k, :]) for k in range(KD)])
                pe.wait_ge(s["proj_taken"], n["proj"])
                with pe.Fori(0, NCH) as c:
                    pe.wait_ge(s["ck_el"], c + (NCH + 1))
                    pe.wait_ge(s["ck_vc"], c + (NCH + 1))
                    pe.wait_ge(s["ck_y_in"], c + (NCH + 1))
                    for h in range(4):
                        ins = te.transpose(ps[:, 0, h * P:h * P + P], gkc[:, h, :], ident[:, :])
                    ins.then_inc(s["ck_turned"], 1)
                    for h in range(4):
                        ins = mm(ps[:, 1, h * P:h * P + P], gkc[:, h, :], gqc[:, h, :])
                    ins.then_inc(s["ck_mat"], 1)
                    pe.wait_ge(s["ck_masked"], c + (8 * NCH + 1))
                    for e in range(KD):
                        o = ps[:, 2 + e // 4, P * (e % 4):P * (e % 4) + P]
                        mm(o, gvc[:, e * P:e * P + P], gat[:, e // 2, :], True, False)
                        ins = mm(o, gsn[:, e // 2, P * (e % 2):P * (e % 2) + P], gqc[:, e // 2, :], False, True)
                    ins.then_inc(s["ck_y"], 1)
                    pe.wait_ge(s["ck_tok"], c + (4 * NCH + 1))
                    for h in range(4):
                        ins = mm(ps[:, 4 + h // 2, 256 * (h % 2):256 * (h % 2) + 256], gkt[:, h * P:h * P + P], gvc[:, 256 * h:256 * h + 256])
                    ins.then_inc(s["ck_s"], 1)
                pe.wait_ge(s["post_a"], 3)
                pe.wait_ge(s["gst_read"], 1)
                for h in range(4):
                    for t in range(2):
                        ins = mm(ps[:, 4 + h, :], ones[:, :], gsq[:, 2 * h + t, :], t == 0, t == 1)
                ins.then_inc(s["post_p"], 1)
                pe.wait_ge(s["post_v"], 5)
                slots = [weights("od_o0"), weights("od_o1")]
                residual(lambda mt: [(W8[slots[mt // 4]][:, k, P * (mt % 4):P * (mt % 4) + P], HT[:, k, :]) for k in range(KD)], KD)

            def moe(L, pairs):
                norm(HT, SEQ)
                pe.wait_ge(s["h_ready"], 8 * n["norm"])
                pe.wait_ge(s["wr_in"], 32 * (L + 1))
                for t in range(TT):
                    for k in range(KD):
                        ins = mm(ps[:, 4, 64 * t:64 * t + NR], HT[:, k, t * P:t * P + P], wr[:, k, :], k == 0, k == KD - 1)
                ins.then_inc(s["plan_p"], 1)
                for t in range(TT):
                    if t >= 2:
                        pe.wait_ge(s["h_taken"], TT * L + t - 1)
                    for k in range(KD):
                        ins = te.transpose(ps[:, 2 * (t % 2) + k // 4, P * (k % 4):P * (k % 4) + P], HT[:, k, t * P:t * P + P], ident[:, :])
                    ins.then_inc(s["h_turned"], 1)
                pe.wait_ge(s["plan_v"], PLAN_V * L + 3)
                for t in range(TT):
                    for u in range(t + 1):
                        mm(ps[:, 5, NX * t:NX * t + NX], (tri[:, 0, :] if u == t else ones[:, :]), msk[:, u, :], u == 0, u == t)
                for u in range(TT):
                    ins = mm(ps[:, 5, P:P + NX], ones[:, :], msk[:, u, :], u == 0, u == TT - 1)
                ins.then_inc(s["plan_p"], 1)
                pe.wait_ge(s["plan_v"], PLAN_V * L + 4)
                for v, table in enumerate((bhot, bgate)):
                    for b in range(2):
                        for i in range(8):
                            ins = mm(ps[64 * b:64 * b + 64, 6, 32 * v:32 * v + NPAIR], rhot[:, i, :],
                                     table[:, i, :].rearrange("p (n b) -> p b n", b=2)[:, b, :], i == 0, i == 7)
                ins.then_inc(s["plan_p"], 1)
                pe.wait_ge(s["plan_p"], 3 * (L + 1))
                pe.sem_inc(s["hh_done"], 1)
                pe.sem_inc(s["y_done"], 1)
                pe.wait_ge(s["plan_v"], PLAN_V * (L + 1))
                trips = pe.value_load(nit[0:1, 0:1], min_val=1, max_val=MAX_TRIPS)

                def turn_rows(arrived):
                    pe.wait_ge(s["xg_in"], arrived)
                    for k in range(KD):
                        ins = te.transpose(ps[:, k // 4, P * (k % 4):P * (k % 4) + P], xg[:, k * P:k * P + P], ident[:, :])
                    ins.then_inc(s["xg_turned"], 1)

                def add_pair(free):
                    for k in range(KD):
                        free(k)
                        ins = mm(ps[:, (5, 7)[k % 2], :], ysb[:, k * P:k * P + P], spread[:, :])
                        ins.then_inc(s["added"], 1)

                turn_rows(pairs * 16 + 16 * (L + 1))
                with pe.Fori(0, trips) as i:
                    for b in range(2):
                        k0 = i * 2 + (pairs * 2 + b)
                        if b == 0:
                            pe.wait_ge(s["xgT_in"], i + (pairs + (L + 1)))
                        pe.wait_ge(w13_in[b], (i + 1) * 32 + pairs * 32)
                        for k in range(KD):
                            x = xgT[:, k, BLK * b:BLK * b + BLK]
                            mm(ps[0:64, 2 + b, :], x, W8[3 * b][:, k, :], k == 0, k == KD - 1)
                            ins = mm(ps[64:128, 2 + b, :], x, W8[3 * b + 1][:, k, :], k == 0, k == KD - 1)
                        ins.then_inc(s["hh_done"], 1)
                        if b == 0:
                            pe.wait_ge(s["y_in"], k0 + 1)
                            pe.wait_ge(s["spread_in"], i + (pairs + (L + 1)))
                            add_pair(lambda k: pe.wait_ge(s["add_in"], i * 8 + (pairs * 8 + (k + 1))))
                        else:
                            turn_rows(i * 16 + (pairs * 16 + 16 * (L + 2)))
                        pe.wait_ge(s["hs_in"], k0 + 1)
                        for f in range(4):
                            ins = te.transpose(ps[:, 4, f * P:f * P + P], hs[b][:, f * P:f * P + P], ident[:, :])
                        ins.then_inc(s["hs_turned"], 1)
                        pe.wait_ge(s["act_in"], k0 + 1)
                        pe.wait_ge(w2_in[b], (i + 1) * 16 + pairs * 16)
                        pe.wait_ge(s["y_in"], k0 + 1)
                        for f in range(4):
                            for h in range(2):
                                ins = mm(ps[64 * h:64 * h + 64, 6, :], act_[b][:, f, :], W4[3 * b + 2][:, f, 512 * h:512 * h + 512],
                                         f == 0, f == 3)
                        ins.then_inc(s["y_done"], 1)
                pe.wait_ge(s["y_in"], (trips + pairs) * 2 + 1)
                pe.wait_ge(s["spread_in"], trips + (pairs + (L + 1)))
                pe.wait_ge(s["add_in"], (trips + pairs) * 8 + 2)
                pe.sem_inc(s["go"], 1)

                def taken(k):
                    if k >= 2:
                        pe.wait_ge(s["xt_ready"], n["xt"] + k - 1)

                add_pair(taken)
                n["xt"] += 8
                return trips

            even()
            cross(0)
            pairs = moe(0, 0)
            odd()
            cross(1)
            moe(1, pairs)
            norm(HT, SEQ)
            pe.wait_ge(s["h_ready"], 8 * n["norm"])
            for t in range(TT):
                if t >= 2:
                    pe.wait_ge(s["f_taken"], t - 1)
                for k in range(KD):
                    ins = te.transpose(ps[:, 2 * (t % 2) + k // 4, P * (k % 4):P * (k % 4) + P], HT[:, k, t * P:t * P + P], ident[:, :])
                ins.then_inc(s["f_turned"], 1)

        @block.vector
        def _(dve):
            st = Steps(dve, s["v_step"])
            ve = nc.vector
            n = {"norm": 0, "xt": 8}

            def bcast(ap, shape):
                return ap.broadcast_to(shape)

            dve.sem_inc(s["add_in"], 2)
            for k in range(KD):
                dve.wait_ge(s["x_turned"], k + 1)
                ve.tensor_copy(XT[:, k, :], ps[:, k, :]).then_inc(s["xt_ready"], 1)
            dve.wait_ge(s["par_turned"], 2)
            st.then(ve.tensor_copy(par[:, :], ps[:, 0, 0:NPAR]))
            st.then(ve.tensor_copy(bc[:, :], ps[:, 1, 0:80]))
            ve.tensor_scalar(omu[:, :], par[:, PARAMS["ev_mu"][0]:PARAMS["ev_mu"][0] + 14], -1.0, 1.0, ALU.mult, ALU.add)
            ve.tensor_scalar(oka[:, :], par[:, PARAMS["ev_k_a"][0]:PARAMS["ev_k_a"][0] + 4], -1.0, 1.0, ALU.mult, ALU.add).then_inc(s["par_ready"], 1)

            def norm(src, dst, width, gain, first):
                n["norm"] += 1
                dve.wait_ge(s["rstd_ready"], n["norm"])
                for k in range(KD):
                    ve.scalar_tensor_tensor(dst[:, k, :], src[:, k, :], col(gain, first + k), rs[:, 0:width], ALU.mult, ALU.mult).then_inc(s["h_ready"], 1)

            def residual():
                for mt in range(KD):
                    dve.wait_ge(s["res_done"], n["res"] + mt + 1)
                    ve.tensor_tensor(XT[:, mt, :], ps[:, 2 + mt % 2, :], XT[:, mt, :], ALU.add).then_inc(s["xt_ready"], 1)
                n["res"] += 8

            n["res"] = 0

            def even():
                dve.wait_ge(s["par_ready"], 1)
                norm(XT, HT, SEQ, "norm_mix", 0)

                def softmax(b):
                    dve.wait_ge(s["sm_scored"], b + 1)
                    dve.wait_ge(s["sm_turned"], b)
                    st.then(ve.scalar_tensor_tensor(sp[:, :, :], ps[:, 4:8, :].rearrange("p b (h k) -> p (b h) k", h=2), HD ** -0.5,
                                                    bcast(smask[:, min(b, 1), :].unsqueeze(1), [P, 8, 2 * P]), ALU.mult, ALU.add))
                    st.then(ve.tensor_reduce(smx, sp[:, :, :], AX.X, ALU.max))
                    st.then(ve.tensor_tensor(smx, smx, bc[:, 0:8], ALU.max))
                    ve.tensor_scalar(snm, smx, -1.0, None, ALU.mult)
                    ve.tensor_tensor(ses, bc[:, 0:8], smx, ALU.subtract).then_inc(s["sm_max"], 1)
                    dve.wait_ge(s["sm_exp"], b + 1)
                    st.then(ve.tensor_tensor(sden, sden, ses, ALU.add))
                    st.then(ve.reciprocal(srec, sden))
                    ve.tensor_tensor(sp[:, :, :], sp[:, :, :], bcast(srec.unsqueeze(2), [P, 8, 2 * P]), ALU.mult).then_inc(s["sm_norm"], 1)

                tiles = [X2[:, 0, :], X2[:, 1, :]] + [t[:, j, :] for t in (Rt, Kt, Vt) for j in range(4)]
                for i, dst in enumerate(tiles):
                    dve.wait_ge(s["proj_taken"], 6 + i + 1)
                    ve.tensor_tensor(dst[:, 1:SEQ], dst[:, 1:SEQ], shf[:, i % 2, 0:SEQ - 1], ALU.add).then_inc(s["shifted"], 1)
                    if i >= 2 and (i - 2) % 3 == 0 and (i - 2) // 3 < 4:
                        softmax((i - 2) // 3)

                dve.wait_ge(s["proj_taken"], 28)
                dve.wait_ge(s["pre_p"], 4)
                ve.tensor_scalar(KKt[:, :, :], ps[:, 4:8, :], 1e-24, None, ALU.max).then_inc(s["pre_v"], 1)
                tmp = HT[:, 0:4, :]
                for j in range(4):
                    ve.tensor_scalar(tmp[:, j, :], At[:, j, :], col("ev_k_a", j), oka[:, j:j + 1], ALU.mult, ALU.add)
                dve.wait_ge(s["pre_a"], 7)
                for j in range(4):
                    ins = ve.scalar_tensor_tensor(KKt[:, j, :], Kt[:, j, :], col("ev_k_k", j), KKt[:, j, :], ALU.mult, ALU.mult)
                st.then(ins)
                st.then(ve.tensor_tensor(Kt[:, :, :], Kt[:, :, :], tmp, ALU.mult))
                st.then(ve.tensor_tensor(At[:, :, :], At[:, :, :], KKt[:, :, :], ALU.mult))
                ve.memset(St[:, :, :], 0.0).then_inc(s["pre_v"], 1)
                dve.wait_ge(s["pre_v"], 2)

                with dve.Fori(0, NCH) as c:
                    st.enter(c, 9 + 2 + 2 * (LEVELS - 1))
                    t = bass.ds(c * CH, CH)
                    for j in range(4):
                        ins = ve.tensor_tensor_scan(CS[:, j, :], ones[:, :], SGt[:, j, t], 0.0, ALU.mult, ALU.add)
                    st.then(ins)
                    st.then(ve.tensor_copy(mid.unsqueeze(2), CS[:, :, CH // 2 - 1:CH // 2]))
                    st.then(ve.tensor_tensor(CS[:, :, :], CS[:, :, :], bcast(mid.unsqueeze(2), [P, 4, CH]), ALU.subtract))
                    ve.tensor_tensor(Dp[:, :, :], CS[:, :, :], SGt[:, :, t], ALU.subtract).then_inc(s["ck_cs"], 1)
                    dve.wait_ge(s["ck_exp"], c + 1)
                    ve.tensor_tensor(AR[:, :, 1, :], Rt[:, :, t], Ep[:, :, :], ALU.mult)
                    ve.scalar_tensor_tensor(AR[:, :, 0, :], KKt[:, :, t], -1.0, Epp[:, :, :], ALU.mult, ALU.mult)
                    ve.tensor_tensor(BT[:, :, :], At[:, :, t], Em[:, :, :], ALU.mult)
                    ve.tensor_tensor(Sn[:, :, :], St[:, :, :], bcast(pc.unsqueeze(2), [P, 4, HD]), ALU.mult)
                    ve.tensor_tensor(KT[:, :, :], Kt[:, :, t], Em[:, :, :], ALU.mult).then_inc(s["ck_el"], 1)
                    for x, dst in enumerate((MA, MK)):
                        for q in range(2):
                            for r in range(2):
                                k = 4 * x + 2 * q + r
                                dve.wait_ge(s["ck_mat"], c * 8 + (k + 1))
                                ve.tensor_tensor(dst[:, 2 * q:2 * q + 2, r, :, :].rearrange("p j x t -> p j (x t)"),
                                                 ps[:, 4 + 2 * q + r, :].rearrange("p (j n) -> p j n", j=2),
                                                 bcast(tri[:, :, :].rearrange("p x t -> p (x t)").unsqueeze(1), [P, 2, 2 * CH]),
                                                 ALU.mult).then_inc(s["ck_masked"], 1)
                    dve.wait_ge(s["ck_masked"], c * 8 + 8)

                    def masked(r, l):
                        return ve.tensor_tensor(TL[r][:, :, :] if l else XJ[r][:, :, :], MA[:, :, r, 0, :],
                                                bcast(level[:, l, :].unsqueeze(1), [P, 4, CH]), ALU.mult)

                    for r in range(2):
                        st.then(masked(r, 0))
                        ve.tensor_tensor(XJ[r][:, :, :], XJ[r][:, :, :], bcast(ident[:, :].unsqueeze(1), [P, 4, CH]), ALU.add).then_inc(s["iv_tl"], 1)
                    for r in range(2):
                        masked(r, 1).then_inc(s["iv_tl"], 1)
                    for l in range(1, LEVELS):
                        if l + 1 < LEVELS:
                            for r in range(2):
                                dve.wait_ge(s["iv_u"], c * (2 * LEVELS) + (2 * l + r + 1))
                                masked(r, l + 1).then_inc(s["iv_tl"], 1)
                        for r in range(2):
                            dve.wait_ge(s["iv_v"], c * (2 * LEVELS - 2) + (2 * l + r - 1))
                            if l == 1:
                                dve.wait_ge(s["iv_tl"], c * (2 * LEVELS) + (r + 1))
                                dve.wait_ge(s["iv_ul"], c * (2 * LEVELS) + (r + 1))
                            else:
                                dve.wait_ge(s["iv_x"], c * (2 * LEVELS - 2) + (2 * l + r - 3))
                            w = 1 << l
                            if l + 1 < LEVELS:
                                o = halves(XI[r][:, :, :].rearrange("p j t -> p (j t)"), l)[0]
                                st.then(ve.tensor_tensor(o, ps[:, 5 + r, 0:256].rearrange("p (b w) -> p b w", w=w), o, ALU.add))
                            o = halves(XJ[r][:, :, :].rearrange("p j t -> p (j t)"), l)[1]
                            ve.tensor_tensor(o, ps[:, (2, 4)[r], 0:256].rearrange("p (b w) -> p b w", w=w), o, ALU.add).then_inc(s["iv_x"], 1)
                    st.then(ve.tensor_copy(fc.unsqueeze(2), Ep[:, :, CH - 1:CH]))
                    dve.wait_ge(s["ck_s"], c + 1)
                    st.then(ve.tensor_tensor(Sn[:, :, :], ps[:, 5, 0:4 * HD].rearrange("p (j v) -> p j v", j=4), Sn[:, :, :], ALU.add))
                    st.then(ve.tensor_tensor(St[:, :, :], Sn[:, :, :], bcast(fc.unsqueeze(2), [P, 4, HD]), ALU.mult))
                    while st.n < st.per:
                        st.then(ve.tensor_copy(mid, fc))
                    st.leave(NCH)

                for j in range(4):
                    ins = ve.scalar_tensor_tensor(KKt[:, j, :], Rt[:, j, :], col("ev_r_k", j), Kt[:, j, :], ALU.mult, ALU.mult)
                ins.then_inc(s["post_v"], 1)
                dve.wait_ge(s["post_p"], 2)
                ve.tensor_tensor(Vt[:, :, :], ps[:, 4:8, :], Vt[:, :, :], ALU.mult).then_inc(s["post_v"], 1)
                dve.wait_ge(s["post_p"], 3)
                ve.scalar_tensor_tensor(HT[:, 4:8, :], ps[:, 4:8, :], -1.0 / HD, HT[:, 4:8, :], ALU.mult, ALU.add).then_inc(s["post_v"], 1)
                dve.wait_ge(s["post_a"], 2)
                st.then(ve.tensor_tensor(HT[:, 4:8, :], HT[:, 4:8, :], At[:, :, :], ALU.mult))
                for j in range(4):
                    ins = ve.tensor_scalar(HT[:, 4 + j, :], HT[:, 4 + j, :], col("ev_lnx_w", j), col("ev_lnx_b", j), ALU.mult, ALU.add)
                st.then(ins)
                st.then(ve.tensor_tensor(HT[:, 4:8, :], HT[:, 4:8, :], Vt[:, :, :], ALU.add))
                ve.tensor_tensor(HT[:, 4:8, :], ps[:, 0:4, :], HT[:, 4:8, :], ALU.mult).then_inc(s["post_v"], 1)
                residual()

            def cross(L):
                norm(XT, HT, SEQ, "norm_xattn", 8 * L)
                if L == 0:
                    norm(memT, memN, MEM, "mem_norm", 0)
                off = 4 * (L + 1)
                for t in range(TT):
                    dve.wait_ge(s["sm_scored"], off + t + 1)
                    st.then(ve.tensor_reduce(smx[:, 0:4], ps[:, 4:6, :].rearrange("p b (h k) -> p (b h) k", h=2), AX.X, ALU.max))
                    ve.tensor_scalar(snm[:, 0:4], smx[:, 0:4], -(P ** -0.5), None, ALU.mult).then_inc(s["sm_max"], 1)
                    dve.wait_ge(s["sm_exp"], off + t + 1)
                    st.then(ve.reciprocal(srec[:, 0:4], sden[:, 0:4]))
                    ve.tensor_tensor(xp[:, t % 2, :, :], xp[:, t % 2, :, :], bcast(srec[:, 0:4].unsqueeze(2), [P, 4, MEM]), ALU.mult).then_inc(s["sm_norm"], 1)
                residual()

            def odd():
                norm(XT, HT, SEQ, "norm_mix", 8)
                dve.wait_ge(s["proj_taken"], 59)
                st.then(ve.tensor_scalar(gz[:, :, :], gl[:, :, :], 0.0, None, ALU.min))
                dve.wait_ge(s["pre_a"], 8)
                st.then(ve.tensor_tensor(gl[:, :, :], gz[:, :, :], ge[:, :, :], ALU.subtract))
                st.then(ve.memset(gst[:, :, :], 0.0))
                with dve.Fori(0, NCH) as c:
                    st.enter(c, 5)
                    t = bass.ds(c * CH, CH)
                    for j in range(4):
                        ins = ve.tensor_tensor_scan(gcs[:, j, :], ones[:, :], gl[:, j, t], 0.0, ALU.mult, ALU.add)
                    st.then(ins)
                    st.then(ve.tensor_copy(mid.unsqueeze(2), gcs[:, :, CH // 2 - 1:CH // 2]))
                    ve.tensor_tensor(gcs[:, :, :], gcs[:, :, :], bcast(mid.unsqueeze(2), [P, 4, CH]), ALU.subtract).then_inc(s["ck_cs"], 1)
                    dve.wait_ge(s["ck_exp"], c + (NCH + 1))
                    ve.scalar_tensor_tensor(gqc[:, :, :], gq[:, :, t], P ** -0.5, gep[:, :, :], ALU.mult, ALU.mult)
                    ve.tensor_tensor(gsn[:, :, :], gst[:, :, :], bcast(pc.unsqueeze(2), [P, 4, 256]), ALU.mult)
                    st.then(ve.tensor_copy(fc.unsqueeze(2), gep[:, :, CH - 1:CH]))
                    ve.tensor_tensor(gkc[:, :, :], gk[:, :, t], gem[:, :, :], ALU.mult).then_inc(s["ck_el"], 1)
                    dve.wait_ge(s["ck_mat"], c + (8 * NCH + 1))
                    ve.tensor_tensor(gat[:, :, :], ps[:, 1, :].rearrange("p (h t) -> p h t", h=4),
                                     bcast(tri[:, 1, :].unsqueeze(1), [P, 4, CH]), ALU.mult).then_inc(s["ck_masked"], 1)
                    dve.wait_ge(s["ck_s"], c + (NCH + 1))
                    st.then(ve.tensor_tensor(gsn[:, :, :], ps[:, 4:6, :].rearrange("p b (h v) -> p (b h) v", h=2), gsn[:, :, :], ALU.add))
                    st.then(ve.tensor_tensor(gst[:, :, :], gsn[:, :, :], bcast(fc.unsqueeze(2), [P, 4, 256]), ALU.mult))
                    st.leave(NCH)
                dve.sem_inc(s["gst_read"], 1)
                dve.wait_ge(s["post_a"], 4)
                for k in range(KD):
                    ins = ve.scalar_tensor_tensor(HT[:, k, :], HT[:, k, :], col("od_onorm", k % 2), grs[:, k // 2, :], ALU.mult, ALU.mult)
                st.then(ins)
                ve.tensor_tensor(HT[:, :, :], HT[:, :, :], og[:, :, :], ALU.mult).then_inc(s["post_v"], 1)
                residual()

            def moe(L, pairs):
                norm(XT, HT, SEQ, "norm_moe", 8 * L)
                done = {"plan": PLAN_V * L}
                dve.wait_ge(s["plan_g"], L + 1)
                dve.wait_ge(s["plan_p"], 3 * L + 1)
                o = 8 + NR * L
                st.then(ve.memset(glp[:, :, :], NEG))
                st.then(ve.tensor_tensor(lg[:, :, :], ps[:, 4, 0:256].rearrange("p (t n) -> p t n", t=TT)[:, :, 0:NR],
                                         bcast(bc[:, o:o + NR].unsqueeze(1), [P, TT, NR]), ALU.add))
                st.then(ve.tensor_copy(glp[:, :, 0:NG], lg[:, :, 0:NG]))
                for t in range(TT):
                    ins = ve.max(g8[:, t, :], glp[:, t, :])
                st.then(ins)
                for t in range(TT):
                    ins = ve.max_index(gi8[:, t, :], g8[:, t, :], glp[:, t, :])
                st.then(ins)
                ve.tensor_tensor(gex[:, :, :], lg[:, :, 0:NG], bcast(g8[:, :, 0:1], [P, TT, NG]), ALU.subtract).then_inc(s["plan_v"], 1)
                st.then(ve.tensor_copy(gidx[:, :].unsqueeze(2), gi8[:, :, 0:1]))
                st.then(ve.tensor_tensor(ogh[:, :, :], bcast(io[:, 0:NG].unsqueeze(1), [P, TT, NG]),
                                         bcast(gidx[:, :].unsqueeze(2), [P, TT, NG]), ALU.is_equal))
                prod = cmp[:, 0:TT * NX].rearrange("p (t e g) -> p t e g", t=TT, e=NE)
                for g in range(NG):
                    ins = ve.tensor_tensor(prod[:, :, :, g], lg[:, :, NG + NE * g:NG + NE * g + NE], bcast(ogh[:, :, g:g + 1], [P, TT, NE]), ALU.mult)
                st.then(ins)
                st.then(ve.tensor_reduce(ein[:, :, :], prod, AX.X, ALU.add))
                for t in range(TT):
                    ins = ve.max(e8[:, t, :], ein[:, t, :])
                st.then(ins)
                for t in range(TT):
                    ins = ve.max_index(ei8[:, t, :], e8[:, t, :], ein[:, t, :])
                st.then(ins)
                ve.tensor_tensor(dv[:, :].unsqueeze(2), e8[:, :, 1:2], e8[:, :, 0:1], ALU.subtract).then_inc(s["plan_v"], 1)
                st.then(ve.tensor_copy(eid[:, :, :], ei8[:, :, 0:2]))
                st.then(ve.scalar_tensor_tensor(eid[:, :, :], bcast(gidx[:, :].unsqueeze(2), [P, TT, 2]), float(NE), eid[:, :, :], ALU.mult, ALU.add))
                st.then(ve.tensor_tensor(oh[:, :, :, :].rearrange("p t c e -> p (t c) e"), bcast(io[:, 0:NX].unsqueeze(1), [P, 8, NX]),
                                         bcast(eid[:, :, :].rearrange("p t c -> p (t c)").unsqueeze(2), [P, 8, NX]), ALU.is_equal))
                ve.tensor_tensor(msk[:, :, :], oh[:, :, 0, :], oh[:, :, 1, :], ALU.add).then_inc(s["plan_v"], 1)
                dve.wait_ge(s["plan_a"], 2 * L + 2)
                st.then(ve.tensor_reduce(pg[:, :], gex[:, :, :], AX.X, ALU.add))
                st.then(ve.tensor_scalar(dv[:, :], ee[:, :], 1.0, None, ALU.add))
                st.then(ve.tensor_tensor(pg[:, :], pg[:, :], dv[:, :], ALU.mult))
                st.then(ve.reciprocal(gate[:, :, 0:1], pg[:, :].unsqueeze(2)))
                st.then(ve.tensor_tensor(gate[:, :, 1:2], gate[:, :, 0:1], ee[:, :].unsqueeze(2), ALU.mult))
                dve.wait_ge(s["plan_p"], 3 * L + 2)
                ve.tensor_copy(rk[:, :, :], ps[:, 5, 0:P].rearrange("p (t e) -> p t e", t=TT))
                st.then(ve.tensor_copy(cn[:, :], ps[:, 5, P:P + NX]))
                c8 = cmp[:, 0:NX * 8].rearrange("p (e k) -> p e k", k=8)
                st.then(ve.tensor_tensor(c8, bcast(cn[:, :].unsqueeze(2), [P, NX, 8]), bcast(io64[:, :].unsqueeze(1), [P, NX, 8]), ALU.is_gt))
                st.then(ve.tensor_reduce(nb[:, :], c8, AX.X, ALU.add))
                st.then(ve.tensor_tensor_scan(pend[:, :], ones[:, 0:NX], nb[:, :], 0.0, ALU.mult, ALU.add))
                st.then(ve.tensor_tensor(pst[:, :], pend[:, :], nb[:, :], ALU.subtract))
                oh8 = oh[:, :, :, :].rearrange("p t c e -> p (t c) e")
                pe8 = cmp[:, 0:8 * NX].rearrange("p (i e) -> p i e", i=8)
                for ci in range(2):
                    ins = ve.tensor_tensor(cmp[:, 0:8 * NX].rearrange("p (t c e) -> p t c e", t=TT, c=2)[:, :, ci, :], oh[:, :, ci, :], rk[:, :, :], ALU.mult)
                st.then(ins)
                st.then(ve.tensor_reduce(selr[:, :], pe8, AX.X, ALU.add))
                st.then(ve.tensor_tensor(pe8, oh8, bcast(pst[:, :].unsqueeze(1), [P, 8, NX]), ALU.mult))
                st.then(ve.tensor_reduce(selp[:, :], pe8, AX.X, ALU.add))
                r8 = cmp[:, 0:64].rearrange("p (i k) -> p i k", k=8)
                st.then(ve.tensor_tensor(r8, bcast(selr[:, :].unsqueeze(2), [P, 8, 8]), bcast(io64[:, :].unsqueeze(1), [P, 8, 8]), ALU.is_ge))
                st.then(ve.tensor_reduce(rq[:, :], r8, AX.X, ALU.add))
                st.then(ve.tensor_scalar(rq[:, :], rq[:, :], -1.0, None, ALU.add))
                st.then(ve.tensor_tensor(blk[:, :], selp[:, :], rq[:, :], ALU.add))
                st.then(ve.scalar_tensor_tensor(brk[:, :], rq[:, :], -float(BLK), selr[:, :], ALU.mult, ALU.add))
                st.then(ve.tensor_tensor(rhot[:, :, :], bcast(io[:, 0:BLK].unsqueeze(1), [P, 8, BLK]), bcast(brk[:, :].unsqueeze(2), [P, 8, BLK]), ALU.is_equal))
                st.then(ve.tensor_tensor(bhot[:, :, :], bcast(io[:, 0:NBLK].unsqueeze(1), [P, 8, NBLK]), bcast(blk[:, :].unsqueeze(2), [P, 8, NBLK]), ALU.is_equal))
                st.then(ve.tensor_tensor(bgate[:, :, :], bhot[:, :, :], bcast(gate[:, :, :].rearrange("p t c -> p (t c)").unsqueeze(2), [P, 8, NBLK]), ALU.mult))
                for t in range(TT):
                    ins = ve.tensor_scalar(bhot[:, 2 * t:2 * t + 2, :], bhot[:, 2 * t:2 * t + 2, :], tokid[:, t:t + 1], None, ALU.mult)
                ins.then_inc(s["plan_v"], 1)
                ce = cmp[:, :].rearrange("p (b e) -> p b e", e=NX)
                st.then(ve.tensor_tensor(ce, bcast(pend[:, :].unsqueeze(1), [P, NBLK, NX]), bcast(io[:, 0:NBLK].unsqueeze(2), [P, NBLK, NX]), ALU.is_le))
                st.then(ve.tensor_reduce(bef[:, :], ce, AX.X, ALU.add))
                st.then(ve.tensor_scalar(bef[:, :], bef[:, :], float(NX - 1), None, ALU.min))
                st.then(ve.tensor_copy(bei[:, :], bef[:, :]))
                st.then(ve.tensor_scalar(cmp[:, 0:NBLK // 2], io[:, 0:NBLK // 2], 2.0, pend[:, NX - 1:NX], ALU.mult, ALU.is_lt))
                st.then(ve.tensor_reduce(nitf[:, 0:1], cmp[:, 0:NBLK // 2], AX.X, ALU.add))
                st.then(ve.tensor_copy(nit[:, 0:1], nitf[:, 0:1]))
                dve.wait_ge(s["plan_p"], 3 * L + 3)
                st.then(ve.tensor_copy(slot_gate[:, :], ps[:, 6, 32:32 + NPAIR]))
                st.then(ve.tensor_copy(idx[:, :], ps[:, 6, 0:NPAIR]))
                ve.tensor_copy(slot_tok[:, :], idx[:, :]).then_inc(s["plan_v"], 1)
                ve.memset(ysb[:, :], 0.0)
                ve.memset(spread[:, :], 0.0).then_inc(s["spread_in"], 1)
                dve.wait_ge(s["plan_v"], PLAN_V * (L + 1))
                trips = dve.value_load(nit[0:1, 0:1], min_val=1, max_val=MAX_TRIPS)
                dve.wait_ge(s["spread_in"], pairs + (L + 1))

                def take_rows(turned):
                    dve.wait_ge(s["xg_turned"], turned)
                    ve.tensor_copy(xgT[:, :, :], ps[:, 0:2, :].rearrange("p b (k c) -> p (b k) c", k=4)).then_inc(s["xgT_in"], 1)

                take_rows(pairs + (L + 2))
                with dve.Fori(0, trips) as i:
                    for k in range(KD):
                        dve.wait_ge(s["added"], i * 8 + (pairs * 8 + (8 * L + k + 1)))
                        ve.tensor_tensor(XT[:, k, :], ps[:, (5, 7)[k % 2], :], XT[:, k, :], ALU.add).then_inc(s["add_in"], 1)
                    ve.tensor_scalar(spread[:, :], io[:, :], slot_tok[:, bass.ds(i, 1)], slot_gate[:, bass.ds(i, 1)],
                                     ALU.is_equal, ALU.mult).then_inc(s["spread_in"], 1)
                    for b in range(2):
                        if b == 1:
                            take_rows(i + (pairs + (L + 3)))
                        dve.wait_ge(s["sl_in"], i * 2 + (pairs * 2 + (b + 1)))
                        ve.tensor_tensor(act_[b][:, :, :], ps[:, 4, :].rearrange("p (f c) -> p f c", f=4)[:, :, BLK:2 * BLK],
                                         sl[b][:, :, :], ALU.mult).then_inc(s["act_in"], 1)
                dve.wait_ge(s["add_in"], (trips + pairs) * 8 + 2)
                for k in range(KD):
                    dve.wait_ge(s["added"], (trips + pairs) * 8 + (8 * L + k + 1))
                    ve.tensor_tensor(XT[:, k, :], ps[:, (5, 7)[k % 2], :], XT[:, k, :], ALU.add).then_inc(s["xt_ready"], 1)
                return trips

            even()
            cross(0)
            pairs = moe(0, 0)
            odd()
            cross(1)
            moe(1, pairs)
            norm(XT, HT, SEQ, "norm_final", 0)


_INS = ["x", "mem", "norm_mix", "norm_xattn", "norm_moe", "norm_final", "ev_w_in", "ev_sinks", "ev_mu", "ev_w0", "ev_w2",
        "ev_a0", "ev_a2", "ev_g2", "ev_k_k", "ev_k_a", "ev_r_k", "ev_lnx_w", "ev_lnx_b", "ev_w_out", "od_w_in",
        "od_gate_up", "od_gate_b", "od_onorm", "od_w_out", "mem_norm", "mem_wk", "mem_wv", "xa_wq", "xa_wo",
        "moe_w_group", "moe_b_group", "moe_w_expert", "moe_b_expert", "moe_w1", "moe_w3", "moe_w2"]


def kernel(**inputs):
    import numpy as _np
    import concourse.bacc as _bacc
    from concourse import mybir as _mybir
    from concourse.bass_utils import run_bass_kernel_spmd as _run

    nc = _bacc.Bacc("TRN2", target_bir_lowering=False, num_devices=1)
    arrays, args = {}, {}
    for name in _INS:
        arr = _np.ascontiguousarray(inputs[name])
        arrays[f"in_{name}"] = arr
        args[name] = nc.dram_tensor(f"in_{name}", arr.shape, _mybir.dt.from_np(arr.dtype), kind="ExternalInput").ap()
    hrows = nc.dram_tensor("hrows", (SEQ, D), F32, kind="Internal").ap()
    out = nc.dram_tensor("out_0", (1, SEQ, D), F32, kind="ExternalOutput").ap()
    trunk(nc, args, hrows, out)
    r = _run(nc, [arrays], core_ids=[0])
    return r.results[0]["out_0"]
```

```python
from contextlib import ExitStack

import concourse.bass as bass
from concourse import mybir
from concourse.alu_op_type import AluOpType as ALU

F32 = mybir.dt.float32
I32 = mybir.dt.int32
U32 = mybir.dt.uint32
ACT = mybir.ActivationFunctionType
AX = mybir.AxisListType

P = 128
SEQ, D, MEM = 512, 1024, 256
KD = D // P
TT = SEQ // P
MT = MEM // P
HD = 64
CH = 128
NCH = SEQ // CH
LEVELS = 7
SQUARE = 5
EPS = 1e-6
GN_EPS = 64e-5
DECAY = 0.6065306597126334
GATE_NORM = 16.0
NEG = -1e30
NG, NE, NX = 4, 8, 32
NR = NG + NX
BLK = 64
NBLK = 52
NPAIR = NBLK // 2
MIN_TRIPS, MAX_TRIPS = 2 * SEQ // BLK // 2, (2 * SEQ // BLK + NX) // 2
EXPERT = (3, 0)
FF = 512

PARAMS = {}
NPAR = 0
for _name, _n in (("norm_mix", 16), ("norm_xattn", 16), ("norm_moe", 16), ("norm_final", 8), ("mem_norm", 8),
                  ("ev_mu", 14), ("ev_w0", 4), ("ev_a0", 4), ("ev_k_k", 4), ("ev_k_a", 4), ("ev_r_k", 4),
                  ("ev_lnx_w", 4), ("ev_lnx_b", 4), ("od_gate_b", 4), ("od_onorm", 2)):
    PARAMS[_name] = (NPAR, _n)
    NPAR += _n

LOADS = [("ev_q", 2), ("ev_kvx", 0), ("ev_r", 1), ("ev_k", 2), ("ev_v", 0), ("ev_o0", 1), ("ev_o1", 2),
         ("xk", 0), ("xv", 1), ("xq0", 2), ("xo0", 0),
         ("od_q", 0), ("od_k", 1), ("od_v0", 2), ("od_v1", 0), ("od_gd", 1), ("od_og0", 2), ("od_og1", 0),
         ("od_o0", 1), ("od_o1", 2), ("xq1", 0), ("xo1", 1)]
LAYER0_LOADS = 11
DMAS_OF = {"ev_q": 16, "ev_kvx": 2, "ev_o0": 3, "ev_o1": 3}
DONE = {"ev_q": ("proj_done", 4), "ev_kvx": ("proj_done", 8), "ev_r": ("proj_done", 12), "ev_k": ("proj_done", 16),
        "ev_v": ("proj_done", 20), "ev_o0": ("res_done", 8), "ev_o1": ("res_done", 8),
        "xk": ("proj_done", 32), "xv": ("proj_done", 34), "xq0": ("proj_done", 38), "xo0": ("res_done", 16),
        "od_q": ("proj_done", 42), "od_k": ("proj_done", 46), "od_v0": ("proj_done", 50), "od_v1": ("proj_done", 54),
        "od_gd": ("proj_done", 55), "od_og0": ("proj_done", 63), "od_og1": ("proj_done", 67),
        "od_o0": ("res_done", 24), "od_o1": ("res_done", 24), "xq1": ("proj_done", 71), "xo1": ("res_done", 32)}
PLAN_V = 5


def use_of(name):
    slot, loaded, former = dict(LOADS)[name], 0, None
    for n, sl in LOADS:
        if sl == slot:
            loaded += 16 * DMAS_OF.get(n, 1)
            if n == name:
                return slot, loaded, former
            former = DONE[n]


class Steps:

    def __init__(self, eng, sem):
        self.eng, self.sem, self.n, self.base = eng, sem, 0, 0

    def did(self, ins):
        ins.then_inc(self.sem, 1)
        self.n += 1

    def settle(self):
        self.eng.wait_ge(self.sem, self.base + self.n)

    def then(self, ins):
        self.did(ins)
        self.settle()

    def enter(self, i, per):
        self.outer, self.per = self.base + self.n, per
        self.base, self.n = i * per + self.outer, 0

    def leave(self, trips):
        assert self.n == self.per, (self.n, self.per)
        self.base, self.n = 0, self.outer + trips * self.per


def halves(ap, l):
    blocks = ap.rearrange("p (b h w) -> p b h w", h=2, w=1 << l)
    return blocks[:, :, 0, :], blocks[:, :, 1, :]


def trunk(nc, a, hrows, out):
    with ExitStack() as ctx:
        KB = 1024
        cursor = [16512]

        def sb(name, shape, dt=F32, at=None):
            size = 4
            for n in shape[1:]:
                size *= n
            if at is None:
                at = cursor[0]
                cursor[0] += -(-size // 32) * 32
            return nc.alloc_sbuf_tensor_at(name, shape, dt, offset=at, align_bytes=4)

        XT = sb("XT", [P, KD, SEQ])
        HT_AT = cursor[0]
        HT = sb("HT", [P, KD, SEQ])
        RING = cursor[0]
        W = [sb(f"W{i}", [P, 4096]) for i in range(6)]
        W8 = [w[:, :].rearrange("p (k n) -> p k n", k=8) for w in W]
        W4 = [w[:, :].rearrange("p (k n) -> p k n", k=4) for w in W]
        WORK = cursor[0]
        cursor[0] += 72 * KB
        ident = sb("ident", [P, P])
        ones = sb("ones", [P, P])
        pair = sb("pair", [P, P])
        tri = sb("tri", [P, 2, P])
        level = sb("level", [P, LEVELS, P])
        par = sb("par", [P, NPAR])
        omu = sb("omu", [P, 14])
        oka = sb("oka", [P, 4])
        bc = sb("bc", [P, 80])
        cst = sb("cst", [P, 2])
        small = sb("small", [P, 10, 8])
        assert cursor[0] <= nc.sbuf_usable_end, cursor[0]
        rs = sb("rs", [P, SEQ], at=WORK + 62 * KB)

        def col(name, k):
            c = PARAMS[name][0] + k
            return par[:, c:c + 1]

        xin = sb("xin", [P, TT, D], at=WORK + 8 * KB)
        prow = sb("prow", [NPAR, P], at=WORK)
        brow = sb("brow", [1, 80], at=WORK + KB)
        Rt = sb("Rt", [P, 4, SEQ], at=WORK)
        Kt = sb("Kt", [P, 4, SEQ], at=WORK + 8 * KB)
        Vt = sb("Vt", [P, 4, SEQ], at=WORK + 16 * KB)
        KKt = sb("KKt", [P, 4, SEQ], at=WORK + 24 * KB)
        At = sb("At", [P, 4, SEQ], at=WORK + 32 * KB)
        SGt = sb("SGt", [P, 4, SEQ], at=WORK + 40 * KB)
        SO = sb("SO", [P, 4, SEQ], at=WORK + 48 * KB)
        X2 = sb("X2", [P, 2, SEQ], at=WORK + 56 * KB)
        shf = sb("shf", [P, 2, SEQ], at=WORK + 60 * KB)
        lora = sb("lora", [P, 2, SEQ], at=WORK + 64 * KB)
        S3 = RING + 48 * KB
        sqT = sb("sqT", [P, 4, SEQ], at=S3)
        skT = sb("skT", [P, 5 * P], at=S3 + 8 * KB)
        sv = sb("sv", [P, 5, P], at=S3 + 8 * KB + 2560)
        smask = sb("smask", [P, 2, 2 * P], at=S3 + 14 * KB)
        sp = sb("sp", [P, 8, 2 * P], at=S3 + 16 * KB)
        spT = sb("spT", [P, 16 * P], at=S3 + 24 * KB)
        AR = sb("AR", [P, 4, 2, CH], at=S3)
        BT = sb("BT", [P, 4, CH], at=S3 + 4 * KB)
        KT = sb("KT", [P, 4, CH], at=S3 + 6 * KB)
        TOK = sb("TOK", [P, 4, 512], at=S3 + 8 * KB)
        MA = sb("MA", [P, 4, 2, 2, CH], at=S3 + 16 * KB)
        MK = sb("MK", [P, 4, 2, 2, CH], at=S3 + 24 * KB)
        XI = [sb(f"XI{r}", [P, 4, CH], at=S3 + (32 + 8 * r) * KB) for r in range(2)]
        XJ = [sb(f"XJ{r}", [P, 4, CH], at=S3 + (34 + 8 * r) * KB) for r in range(2)]
        TL = [sb(f"TL{r}", [P, 4, CH], at=S3 + (36 + 8 * r) * KB) for r in range(2)]
        UL = [sb(f"UL{r}", [P, 4, CH], at=S3 + (38 + 8 * r) * KB) for r in range(2)]
        AKV = sb("AKV", [P, 512], at=HT_AT)
        WT = sb("WT", [P, 4, CH], at=HT_AT + 2 * KB)
        Us = sb("Us", [P, 4, 2, HD], at=HT_AT + 4 * KB)
        CS = sb("CS", [P, 4, CH], at=HT_AT + 6 * KB)
        Dp = sb("Dp", [P, 4, CH], at=WORK + 60 * KB)
        Em = sb("Em", [P, 4, CH], at=WORK + 62 * KB)
        St = sb("St", [P, 4, HD], at=WORK + 64 * KB)
        Sn = sb("Sn", [P, 4, HD], at=WORK + 65 * KB)
        VC = sb("VC", [P, 4, CH], at=WORK + 68 * KB)
        Ep = sb("Ep", [P, 4, CH], at=WORK + 70 * KB)
        Epp = Dp
        ktmp = sb("ktmp", [P, 4, SEQ], at=S3 + 32 * KB)
        RH = sb("RH", [P, 4, CH], at=WORK + 56 * KB)
        mid = small[:, 0, 0:4]
        pc = small[:, 1, 0:4]
        fc = small[:, 2, 0:4]
        smx = small[:, 3, :]
        snm = small[:, 4, :]
        ses = small[:, 5, :]
        sden = small[:, 6, :]
        srec = small[:, 7, :]
        gq = sb("gq", [P, 4, SEQ], at=WORK)
        gk = sb("gk", [P, 4, SEQ], at=WORK + 8 * KB)
        gv = sb("gv", [P, TT, D], at=WORK + 16 * KB)
        gl = sb("gl", [P, 4, SEQ], at=WORK + 32 * KB)
        og = sb("og", [P, KD, SEQ], at=WORK + 40 * KB)
        gup = sb("gup", [16, SEQ], at=WORK + 56 * KB)
        gdT = sb("gdT", [16, SEQ], at=WORK + 58 * KB)
        gz = sb("gz", [P, 4, SEQ], at=S3)
        ge = sb("ge", [P, 4, SEQ], at=S3 + 8 * KB)
        gcs = sb("gcs", [P, 4, SEQ], at=S3 + 16 * KB)
        gep = sb("gep", [P, 4, SEQ], at=S3 + 24 * KB)
        gem = sb("gem", [P, 4, SEQ], at=S3 + 32 * KB)
        gsq = sb("gsq", [P, KD, CH], at=S3)
        grs = sb("grs", [P, 4, CH], at=S3 + 4 * KB)
        gvc = [sb(f"gvc{b}", [P, D], at=S3 + (16 + 4 * b) * KB) for b in range(2)]
        gsn = sb("gsn", [P, 4, 256], at=S3 + 24 * KB)
        gkc = [sb(f"gkc{b}", [P, 4, CH], at=S3 + (40 + 2 * b) * KB) for b in range(2)]
        gkt = sb("gkt", [P, 512], at=S3 + 44 * KB)
        gat = sb("gat", [P, 4, CH], at=S3 + 46 * KB)
        gmid = sb("gmid", [P, 4, NCH])
        gfirst = sb("gfirst", [P, 4, NCH])
        gnext = sb("gnext", [P, 4, NCH])
        mkT = sb("mkT", [P, 4, MEM], at=WORK + 64 * KB)
        mv = sb("mv", [P, MT, 512], at=WORK + 68 * KB)
        xsq = sb("xsq", [P, KD, SEQ], at=WORK + 24 * KB)
        memin = sb("memin", [P, MT, D], at=WORK)
        memT = sb("memT", [P, KD, MEM], at=WORK + 8 * KB)
        memN = sb("memN", [P, KD, MEM], at=WORK + 16 * KB)
        xq = sb("xq", [P, 4, SEQ], at=WORK + 24 * KB)
        xo = sb("xo", [P, 4, SEQ], at=WORK + 32 * KB)
        xp = sb("xp", [P, 2, 4, MEM], at=WORK + 40 * KB)
        xpT = HT
        wr = sb("wr", [P, KD, NR], at=WORK)
        hk = sb("hk", [P, TT, D], at=WORK + 4 * KB)
        lg = sb("lg", [P, TT, NR], at=WORK + 20 * KB)
        M0 = WORK + 20 * KB + 1024
        glp = sb("glp", [P, TT, 8], at=M0)
        g8 = sb("g8", [P, TT, 8], at=M0 + 128)
        gi8 = sb("gi8", [P, TT, 8], U32, at=M0 + 256)
        ein = sb("ein", [P, TT, 8], at=M0 + 384)
        e8 = sb("e8", [P, TT, 8], at=M0 + 512)
        ei8 = sb("ei8", [P, TT, 8], U32, at=M0 + 640)
        gidx = sb("gidx", [P, TT], at=M0 + 768)
        ogh = sb("ogh", [P, TT, 4], at=M0 + 784)
        gex = sb("gex", [P, TT, 4], at=M0 + 848)
        pg = sb("pg", [P, TT], at=M0 + 912)
        dv = sb("dv", [P, TT], at=M0 + 928)
        ee = sb("ee", [P, TT], at=M0 + 944)
        gate = sb("gate", [P, TT, 2], at=M0 + 960)
        eid = sb("eid", [P, TT, 2], at=M0 + 992)
        M1 = M0 + 1024
        oh = sb("oh", [P, TT, 2, NX], at=M1)
        msk = sb("msk", [P, TT, NX], at=M1 + 1024)
        rk = sb("rk", [P, TT, NX], at=M1 + 1536)
        cn = sb("cn", [P, NX], at=M1 + 2048)
        nb = sb("nb", [P, NX], at=M1 + 2176)
        pend = sb("pend", [P, NX], at=M1 + 2304)
        pst = sb("pst", [P, NX], at=M1 + 2432)
        selr = sb("selr", [P, 8], at=M1 + 2560)
        selp = sb("selp", [P, 8], at=M1 + 2592)
        rq = sb("rq", [P, 8], at=M1 + 2624)
        blk = sb("blk", [P, 8], at=M1 + 2656)
        brk = sb("brk", [P, 8], at=M1 + 2688)
        idc = sb("idc", [P, 1], I32, at=M1 + 2720)
        nit = sb("nit", [P, 2], I32, at=M1 + 2752)
        nitf = sb("nitf", [P, 2], at=M1 + 2760)
        bei = sb("bei", [P, NBLK], I32, at=M1 + 2816)
        bef = sb("bef", [P, NBLK], at=M1 + 3072)
        idx = sb("idx", [P, NPAIR], I32, at=M1 + 3328)
        slot_gate = sb("slot_gate", [P, NPAIR], at=M1 + 3328 + 256)
        io = sb("io", [P, SEQ], at=M1 + 4096)
        M2 = M1 + 4096 + 2048
        io64 = sb("io64", [P, 8], at=M2)
        tokid = sb("tokid", [P, TT], at=M2 + 32)
        rhot = sb("rhot", [P, 8, BLK], at=M2 + 64)
        bhot = sb("bhot", [P, 8, NBLK], at=M2 + 64 + 2048)
        cmp = sb("cmp", [P, NBLK * NX], at=M2 + 64 + 4096)
        bgate = sb("bgate", [P, 8, NBLK], at=M2 + 64 + 4096 + 4 * NBLK * NX)
        slot_tok = sb("slot_tok", [P, NPAIR], at=M2 + 64 + 4096 + 4 * NBLK * (NX + 8))
        M3 = WORK + 42 * KB
        assert M2 + 64 + 4096 + 4 * NBLK * (NX + 9) <= M3
        xg = sb("xg", [P, D], at=M3)
        xgT = sb("xgT", [P, KD, P], at=M3 + 4 * KB)
        ysb = sb("ysb", [P, D], at=M3 + 8 * KB)
        hs = [sb(f"hs{b}", [P, FF], at=M3 + 12 * KB + 2 * KB * b) for b in range(2)]
        sl = [sb(f"sl{b}", [P, 4, BLK], at=M3 + 16 * KB + KB * b) for b in range(2)]
        act_ = [sb(f"act{b}", [P, 4, BLK], at=M3 + 18 * KB + KB * b) for b in range(2)]
        spread = sb("spread", [P, SEQ], at=M3 + 20 * KB)
        osb = sb("osb", [P, TT, D], at=WORK)

        ps = ctx.enter_context(nc.psum_tensor("ps", [P, 8, 512], F32))

        s = {n: ctx.enter_context(nc.semaphore(n)) for n in (
            "v_step", "a_step", "g_step",
            "ident_in", "consts", "par_in", "par_turned", "par_ready", "x_in", "x_turned", "lora_in",
            "xt_ready", "sq_ready", "sum_ready", "rstd_ready", "h_ready", "proj_done", "proj_taken", "res_done",
            "sm_scored", "sm_max", "sm_exp", "sm_norm", "sm_turned", "sm_pt", "sm_pv", "sm_out", 
            "shifted", "pre_v", "pre_a", "pre_p", "post_v", "post_a", "post_p",
            "ck_scan", "ck_mid", "ck_cs", "ck_rh", "ck_sn", "ck_exp", "ck_el", "ck_vc", "ck_turned", "ck_tok", "ck_mat", "ck_masked", "ck_y", "ck_y_in", "ck_s",
            "iv_tl", "iv_u", "iv_ul", "iv_v", "iv_x", "akv_done", "akv_in", "wt_done", "wt_in", "u_done", "u_in",
            "g_cs", "g_exp", "g_scaled", "g_copied", "g_turned", "g_tok", "g_mat", "g_masked", "g_y", "g_sq", "g_sum", "g_ln", "g_rs",
            "g_added", "g_state", "g_half", "g_out",
            "mem_in", "mem_turned", "gup_in",
            "wr_in", "plan_v", "plan_a", "plan_p", "plan_g", "first_in", "slots_in", "h_turned", "h_taken", "h_stored",
            "xg_turned", "xgT_in", "hh_done", "hs_in", "hs_turned", "sl_in", "act_in", "y_done", "y_in",
            "xg_in", "spread_in", "added", "add_in", "gb_step", "go",
            "f_turned", "f_taken", "out_stored")}
        w_loaded = [ctx.enter_context(nc.semaphore(f"w_loaded{i}")) for i in range(3)]
        w13_in, w2_in = ([ctx.enter_context(nc.semaphore(f"{n}{b}")) for b in range(2)] for n in ("w13_in", "w2_in"))
        block = ctx.enter_context(nc.Block())

        @block.sync
        def _(sp):
            sources = {
                "ev_kvx": [(W8[0][:, :, 0:256], a["ev_w_in"][0][:, 512:768]), (W8[0][:, :, 256:512], a["ev_w_in"][0][:, 2304:2560])],
                "ev_r": [(W8[1], a["ev_w_in"][0][:, 768:1280])],
                "ev_k": [(W8[2], a["ev_w_in"][0][:, 1280:1792])],
                "ev_v": [(W8[0], a["ev_w_in"][0][:, 1792:2304])],
                "xk": [(W8[0], a["mem_wk"])], "xv": [(W8[1], a["mem_wv"])],
                "xq0": [(W8[2], a["xa_wq"][0])], "xq1": [(W8[0], a["xa_wq"][1])],
                "xo0": [(W4[0], a["xa_wo"][0])], "xo1": [(W4[1], a["xa_wo"][1])],
                "od_q": [(W8[0], a["od_w_in"][0][:, 0:512])], "od_k": [(W8[1], a["od_w_in"][0][:, 512:1024])],
                "od_v0": [(W8[2], a["od_w_in"][0][:, 1024:1536])], "od_v1": [(W8[0], a["od_w_in"][0][:, 1536:2048])],
                "od_gd": [(W8[1][:, :, 0:16], a["od_w_in"][0][:, 2048:2064])],
                "od_og0": [(W8[2], a["od_w_in"][0][:, 2064:2576])], "od_og1": [(W8[0], a["od_w_in"][0][:, 2576:3088])],
                "od_o0": [(W8[1], a["od_w_out"][0][:, 0:512])], "od_o1": [(W8[2], a["od_w_out"][0][:, 512:1024])],
            }
            sources["ev_q"] = [(W8[2].rearrange("p k (j g d) -> p k j g d", j=4, g=2)[:, k, :, g, :],
                                a["ev_w_in"][0][k * P:k * P + P, 256 * g:256 * g + 256].rearrange("p (j d) -> p j d", j=4))
                               for k in range(KD) for g in range(2)]
            for h, name in enumerate(("ev_o0", "ev_o1")):
                w = a["ev_w_out"][0][:, 512 * h:512 * h + 512]
                dst = W8[dict(LOADS)[name]]
                sources[name] = [(dst[0:64, 0:4, :], w[0:256, :].rearrange("(j d) n -> d j n", d=HD)),
                                 (dst[64:128, 0:4, :], w[256:512, :].rearrange("(j d) n -> d j n", d=HD)),
                                 (dst[:, 4:8, :], w[512:1024, :].rearrange("(k p) n -> p k n", p=P))]

            def load(name):
                slot, _, former = use_of(name)
                if former:
                    sp.wait_ge(s[former[0]], former[1])
                for dst, src in sources[name]:
                    if len(dst.shape) == 3 and len(src.shape) == 2:
                        src = src.rearrange("(k p) n -> p k n", p=P)
                    sp.dma_start(dst, src).then_inc(w_loaded[slot], 16)

            def load_expert(L, b, e, i, pairs, gathered=None):
                w1, w3, w2 = (a[k][L][e][0].rearrange("(k p) n -> p k n", p=P) for k in ("moe_w1", "moe_w3", "moe_w2"))
                if i is not None:
                    sp.wait_ge(s["hh_done"], i * 2 + (pairs * 2 + (b + L + 1)))
                sp.dma_start(W8[EXPERT[b]], w1).then_inc(w13_in[b], 16)
                sp.dma_start(W8[EXPERT[b] + 1], w3).then_inc(w13_in[b], 16)
                if gathered is not None:
                    sp.wait_ge(s["xg_in"], gathered)
                if i is not None:
                    sp.wait_ge(s["y_done"], i * 2 + (pairs * 2 + (b + L + 1)))
                sp.dma_start(W4[EXPERT[b] + 2], w2).then_inc(w2_in[b], 16)

            def experts(L, pairs):
                def block(b, i):
                    e = sp.value_load(bei[0:1, b:b + 1] if i is None else bei[0:1, bass.ds(i * 2 + b, 1)], min_val=0, max_val=NX - 1)
                    if i is None:
                        load_expert(L, b, bass.ds(e, 1), None, pairs, gathered=pairs * 16 + 16 * (L + 1))
                    else:
                        load_expert(L, b, bass.ds(e, 1), i, pairs)

                sp.wait_ge(s["first_in"], L + 1)
                sp.wait_ge(s["plan_p"], 3 * L + 1)
                block(1, None)
                sp.wait_ge(s["plan_v"], PLAN_V * (L + 1))
                trips = sp.value_load(nit[0:1, 0:1], min_val=MIN_TRIPS, max_val=MAX_TRIPS)
                with sp.Fori(1, trips) as i:
                    block(0, i)
                    block(1, i)
                return trips

            def first_expert(L, pairs):
                sp.wait_ge(s["res_done"], 8 + 16 * L)
                load_expert(L, 0, slice(0, 1), None, pairs)

            for i, (name, _) in enumerate(LOADS[:LAYER0_LOADS]):
                load(name)
                if name == "xk":
                    first_expert(0, 0)
            pairs = experts(0, 0)
            sp.wait_ge(s["y_done"], pairs * 2 + 2)
            for name, _ in LOADS[LAYER0_LOADS:]:
                load(name)
                if name == "xo1":
                    first_expert(1, pairs)
            experts(1, pairs)
            dst = out[0].rearrange("(t p) d -> t p d", p=P)
            for t in range(TT):
                sp.wait_ge(s["f_taken"], t + 1)
                sp.dma_start(dst[t], osb[:, t, :]).then_inc(s["out_stored"], 16)
            sp.wait_ge(s["out_stored"], 16 * TT)

        @block.gpsimd
        def _(pool):
            st = Steps(pool, s["g_step"])
            g = nc.gpsimd
            st.then(g.memset(ident[:, :], 0.0))
            st.then(g.affine_select(out=ident[:, :], in_=ident[:, :], compare_op=ALU.not_equal, fill=1.0, base=0,
                                    pattern=[[-1, P]], channel_multiplier=1))
            st.then(g.memset(ones[:, :], 1.0))
            st.then(g.memset(cst[:, 0:1], EPS))
            st.then(g.memset(cst[:, 1:2], GN_EPS))
            pool.sem_inc(s["ident_in"], 1)
            st.then(g.memset(pair[:, :], 0.0))
            for r in range(2):
                st.then(g.memset(pair[64 * r:64 * r + 64, 64 * r:64 * r + 64], 1.0))
            for v in range(2):
                st.then(g.memset(tri[:, v, :], 1.0))
                st.then(g.affine_select(out=tri[:, v, :], in_=tri[:, v, :], compare_op=ALU.is_ge, fill=0.0, base=v - 1,
                                        pattern=[[1, P]], channel_multiplier=-1))
            st.then(g.memset(level[:, :, :], 0.0))
            for l in range(LEVELS):
                h = 1 << l
                half = level[:, l, :].rearrange("p (b h w) -> p b h w", h=2, w=h)[:, :, 1, :]
                st.then(g.memset(half, 1.0))
                st.then(g.affine_select(out=half, in_=half, compare_op=ALU.is_ge, fill=0.0, base=0,
                                        pattern=[[-2 * h, P // (2 * h)], [0, h]], channel_multiplier=1))
                st.then(g.affine_select(out=half, in_=half, compare_op=ALU.is_ge, fill=0.0, base=h - 1,
                                        pattern=[[2 * h, P // (2 * h)], [0, h]], channel_multiplier=-1))
            st.then(g.memset(smask[:, :, :], 0.0))
            st.then(g.affine_select(out=smask[:, 1, 0:P], in_=smask[:, 1, 0:P], compare_op=ALU.is_ge, fill=NEG, base=-1,
                                    pattern=[[1, P]], channel_multiplier=-1))
            for v in range(2):
                st.then(g.affine_select(out=smask[:, v, P:2 * P], in_=smask[:, v, P:2 * P], compare_op=ALU.is_ge, fill=NEG,
                                        base=0, pattern=[[-1, P]], channel_multiplier=1))
            st.then(g.memset(smask[:, 0, 0:P], NEG))
            st.then(g.memset(skT[:, 0:P], 0.0))
            g.memset(sv[:, 0, :], 0.0).then_inc(s["consts"], 1)

            def even():
                def from_middle(c, t):
                    pool.wait_ge(s["ck_scan"], c + 1)
                    pool.sem_inc(s["go"], 1)
                    g.tensor_tensor(CS[:, :, :], CS[:, :, :], mid.unsqueeze(2).broadcast_to([P, 4, CH]), ALU.subtract).then_inc(s["ck_mid"], 1)
                    pool.wait_ge(s["ck_mid"], c + 1)
                    pool.sem_inc(s["go"], 1)
                    g.tensor_tensor(Dp[:, :, :], CS[:, :, :], SGt[:, :, t], ALU.subtract).then_inc(s["ck_cs"], 1)

                from_middle(0, slice(0, CH))
                with pool.Fori(0, NCH) as c:
                    pool.wait_ge(s["ck_turned"], c * 4 + 1)
                    pool.sem_inc(s["go"], 1)
                    g.tensor_copy(VC[:, :, :], Vt[:, :, bass.ds(c * CH, CH)]).then_inc(s["ck_vc"], 1)
                    pool.wait_ge(s["ck_el"], c + 1)
                    pool.wait_ge(s["ck_y_in"], c + 1)
                    pool.sem_inc(s["go"], 1)
                    g.tensor_copy(RH[:, :, :], AR[:, :, 1, :]).then_inc(s["ck_rh"], 1)
                    t = bass.ds((c + 1) % NCH * CH, CH)
                    from_middle(c + 1, t)
                    pool.wait_ge(s["ck_mat"], c * 8 + 8)
                    pool.wait_ge(s["ck_rh"], c + 1)
                    pool.wait_ge(s["ck_exp"], c + 2)
                    pool.sem_inc(s["go"], 1)
                    g.tensor_tensor(AR[:, :, 1, :], Rt[:, :, t], Ep[:, :, :], ALU.mult)
                    g.tensor_tensor(AR[:, :, 0, :], KKt[:, :, t], Epp[:, :, :], ALU.mult)
                    g.tensor_tensor(BT[:, :, :], At[:, :, t], Em[:, :, :], ALU.mult)
                    g.tensor_tensor(KT[:, :, :], Kt[:, :, t], Em[:, :, :], ALU.mult).then_inc(s["ck_el"], 1)

            def odd():
                pool.sem_inc(s["g_out"], 1)
                pool.wait_ge(s["proj_taken"], DONE["od_v1"][1])
                pool.wait_ge(s["g_scaled"], 1)

                def copy(c):
                    pool.wait_ge(s["g_added"], c + 1)
                    g.tensor_copy(gkc[c % 2][:, :, :], gk[:, :, c * CH:c * CH + CH])
                    g.tensor_copy(gvc[c % 2][:, :], gv[:, c, :]).then_inc(s["g_copied"], 1)

                copy(0)
                copy(1)
                for c in range(NCH):
                    y = HT[:, :, c * CH:c * CH + CH]
                    yh = y.rearrange("p (h u) t -> p h u t", u=2)
                    pool.wait_ge(s["g_rs"], c + 1)
                    g.tensor_tensor(yh, yh, grs[:, :, :].unsqueeze(2).broadcast_to([P, 4, 2, CH]), ALU.mult).then_inc(s["g_half"], 1)
                    pool.wait_ge(s["g_half"], c + 1)
                    g.tensor_tensor(y, y, og[:, :, c * CH:c * CH + CH], ALU.mult).then_inc(s["g_out"], 1)
                    if c + 2 < NCH:
                        copy(c + 2)

            def moe(L, pairs):
                pool.wait_ge(s["h_ready"], 8 * (4 + 3 * L))
                st.then(g.iota(io[:, :], pattern=[[1, SEQ]], base=0, channel_multiplier=0, allow_small_or_imprecise_dtypes=True))
                st.then(g.iota(io64[:, :], pattern=[[64, 8]], base=0, channel_multiplier=0, allow_small_or_imprecise_dtypes=True))
                g.iota(tokid[:, :], pattern=[[P, TT]], base=0, channel_multiplier=1,
                       allow_small_or_imprecise_dtypes=True).then_inc(s["plan_g"], 1)

                def gather(column):
                    st2.then(g.tensor_copy(idc[:, :], column))
                    pool.sem_inc(s["go"], 1)
                    g.indirect_dma_start(out=xg[:, :], out_offset=None, in_=hrows[:, :],
                                         in_offset=bass.IndirectOffsetOnAxis(ap=idc[:, :], axis=0)).then_inc(s["xg_in"], 16)

                st2 = Steps(pool, s["gb_step"])
                st2.base = pairs + L
                pool.wait_ge(s["slots_in"], L + 1)
                pool.wait_ge(s["h_stored"], 16 * TT * (L + 1))
                gather(idx[:, 0:1])
                pool.wait_ge(s["plan_v"], PLAN_V * (L + 1))
                trips = pool.value_load(nit[0:1, 0:1], min_val=MIN_TRIPS, max_val=MAX_TRIPS)
                with pool.Fori(0, trips) as i:
                    st2.enter(i, 1)
                    pool.wait_ge(s["xg_in"], (i + (pairs + L + 1)) * 16)
                    pool.wait_ge(s["xg_turned"], i + (pairs + L + 2))
                    gather(idx[:, bass.ds(i + 1, 1)])
                pool.wait_ge(s["xg_in"], (trips + 1 + pairs + L) * 16)
                pool.sem_inc(s["go"], 1)
                return trips

            even()
            pairs = moe(0, 0)
            odd()
            moe(1, pairs)

        @block.scalar
        def _(act):
            st = Steps(act, s["a_step"])
            sc = nc.scalar
            n = {"proj": 0, "norm": 0, "xt": 8}

            act.sem_inc(s["ck_y_in"], 1)
            act.sem_inc(s["y_in"], 1)
            act.dma_start(xin[:, :, :], a["x"][0].rearrange("(t p) d -> p t d", p=P)).then_inc(s["x_in"], 16)
            for name, (c0, k) in PARAMS.items():
                src = a[name]
                while len(src.shape) > 1:
                    src = src.rearrange({2: "a b -> (a b)", 3: "a b c -> (a b c)"}[len(src.shape)])
                act.dma_start(prow[c0:c0 + k, :], src.rearrange("(r p) -> r p", p=P)).then_inc(s["par_in"], 16)
            act.dma_start(brow[0:1, 0:8], a["ev_sinks"]).then_inc(s["par_in"], 16)
            for L in range(2):
                o = 8 + NR * L
                act.dma_start(brow[0:1, o:o + NG], a["moe_b_group"][L:L + 1, :]).then_inc(s["par_in"], 16)
                act.dma_start(brow[0:1, o + NG:o + NR], a["moe_b_expert"][L:L + 1, :]).then_inc(s["par_in"], 16)
            act.dma_start(lora[0:64, 0, :], a["ev_w2"][0]).then_inc(s["lora_in"], 16)
            act.dma_start(lora[64:128, 0, :], a["ev_a2"][0]).then_inc(s["lora_in"], 16)
            act.dma_start(lora[:, 1, :], a["ev_g2"][0]).then_inc(s["lora_in"], 16)

            def norm(src, squares, width, early=False):
                for q in range(4):
                    if early:
                        act.wait_ge(s["xt_ready"], n["xt"] - 6 + 2 * q)
                    sc.activation(squares[:, 2 * q:2 * q + 2, :], src[:, 2 * q:2 * q + 2, :], ACT.Square).then_inc(s["sq_ready"], 1)
                n["norm"] += 1
                act.wait_ge(s["sum_ready"], n["norm"])
                if n["norm"] > 1:
                    act.wait_ge(s["h_ready"], 8 * (n["norm"] - 1))
                inverse_root(rs[:, 0:width], ps[:, 7, 0:width], D, 0).then_inc(s["rstd_ready"], 1)

            def inverse_root(dst, src, count, eps, sem=None, value=None):
                ins = sc.activation(dst, src, ACT.Ln, bias=cst[:, eps:eps + 1], scale=1.0 / count)
                if sem is None:
                    st.then(ins)
                else:
                    ins.then_inc(sem, 1)
                    act.wait_ge(sem, value)
                return sc.activation(dst, dst, ACT.Exp, scale=-0.5)

            def take(dst, src=None, last=True, func=ACT.Copy, **k):
                act.wait_ge(s["proj_done"], n["proj"] + 1)
                if src is None:
                    src = ps[:, n["proj"] % 2, :]
                ins = sc.activation(dst, src, func, **k)
                if last:
                    ins.then_inc(s["proj_taken"], 1)
                    n["proj"] += 1

            def even():
                norm(XT, HT, SEQ, early=True)
                act.wait_ge(s["consts"], 1)
                for j in range(4):
                    take(sqT[:, j, :])
                take(skT[:, P:5 * P])
                take(sv[:, 1:5, :].rearrange("p t n -> p (t n)"))

                def swa_exp(b):
                    act.wait_ge(s["sm_max"], b + 1)
                    for h in range(8):
                        sc.activation(sp[:, h, :], sp[:, h, :], ACT.Exp, bias=snm[:, h:h + 1], accum_out=sden[:, h:h + 1])
                    sc.activation(ses, ses, ACT.Exp).then_inc(s["sm_exp"], 1)

                def swa_pt(b):
                    act.wait_ge(s["sm_turned"], b + 1)
                    sc.activation(spT[:, :].rearrange("p (b n) -> p b n", b=4), ps[:, 4:8, :], ACT.Copy).then_inc(s["sm_pt"], 1)

                def swa_out(b):
                    act.wait_ge(s["sm_pv"], b + 1)
                    sc.activation(SO[:, :, b * P:b * P + P], ps[:, 2, :].rearrange("p (j q) -> p j q", j=4), ACT.Copy).then_inc(s["sm_out"], 1)

                tiles = [X2[:, 0, :], X2[:, 1, :]] + [t[:, j, :] for t in (Rt, Kt, Vt) for j in range(4)]
                mus = [12, 13] + list(range(12))
                for i, (dst, mu) in enumerate(zip(tiles, mus)):
                    take(dst, func=ACT.Copy, scale=omu[:, mu:mu + 1], last=False)
                    if i >= 2:
                        act.wait_ge(s["shifted"], i - 1)
                    take(shf[:, i % 2, :], func=ACT.Copy, scale=col("ev_mu", mu))
                    if i >= 4 and (i - 4) % 3 == 0:
                        swa_pt((i - 4) // 3)
                    if i >= 5 and (i - 5) % 3 == 0:
                        swa_out((i - 5) // 3)
                    if i >= 2 and (i - 2) % 3 == 0 and (i - 2) // 3 < 4:
                        swa_exp((i - 2) // 3)
                swa_out(3)

                act.wait_ge(s["shifted"], 14)
                sc.activation(X2[0:64, 0, :], X2[0:64, 0, :], ACT.Tanh).then_inc(s["pre_a"], 1)
                sc.activation(X2[:, 1, :], X2[:, 1, :], ACT.Sigmoid).then_inc(s["pre_a"], 1)
                for j in range(8):
                    act.wait_ge(s["proj_done"], n["proj"] + 1)
                    dst = (SGt, At)[j // 4][:, j % 4, :]
                    sc.activation(dst, ps[:, n["proj"] % 2, :], ACT.Sigmoid, bias=col("ev_w0", j)).then_inc(s["proj_taken"], 1)
                    n["proj"] += 1
                for j in range(4):
                    sc.activation(HT[:, j, :], Kt[:, j, :], ACT.Square, scale=col("ev_k_k", j)).then_inc(s["pre_a"], 1)

                act.wait_ge(s["pre_v"], 1)
                st.then(sc.activation(KKt[:, :, :], KKt[:, :, :], ACT.Ln))
                sc.activation(KKt[:, :, :], KKt[:, :, :], ACT.Exp, scale=-0.5).then_inc(s["pre_a"], 1)

                def decays(c):
                    act.wait_ge(s["ck_cs"], c + 1)
                    sc.activation(Ep[:, :, :], CS[:, :, :], ACT.Exp, scale=-DECAY)
                    sc.activation(Em[:, :, :], CS[:, :, :], ACT.Exp, scale=DECAY)
                    sc.activation(Epp[:, :, :], Dp[:, :, :], ACT.Exp, scale=-DECAY)
                    sc.activation(pc, mid, ACT.Exp, scale=-DECAY).then_inc(s["ck_exp"], 1)

                decays(0)
                with act.Fori(0, NCH) as c:
                    for k in range(4):
                        act.wait_ge(s["ck_turned"], c * 4 + (k + 2))
                        sc.activation(TOK[:, k, :], ps[:, k, :], ACT.Copy).then_inc(s["ck_tok"], 1)
                    for l in range(1, LEVELS):
                        for r in range(2):
                            act.wait_ge(s["iv_u"], c * (2 * LEVELS - 2) + (2 * l + r - 1))
                            sc.activation(UL[r][:, :, :].rearrange("p j t -> p (j t)"), ps[:, r, :], ACT.Copy).then_inc(s["iv_ul"], 1)
                        if l == 1:
                            act.wait_ge(s["akv_done"], c + 1)
                            sc.activation(AKV[:, :], ps[:, 3, :], ACT.Copy).then_inc(s["akv_in"], 1)
                        if l == 3:
                            decays(c + 1)
                    act.wait_ge(s["wt_done"], c + 1)
                    sc.activation(WT[:, :, :].rearrange("p j t -> p (j t)"), ps[:, 7, :], ACT.Copy).then_inc(s["wt_in"], 1)
                    act.wait_ge(s["u_done"], c + 1)
                    sc.activation(Us[:, :, :, :].rearrange("p j r v -> p r j v"),
                                  ps[:, 0:2, 0:256].rearrange("p r (j v) -> p r j v", j=4), ACT.Copy).then_inc(s["u_in"], 1)
                    act.wait_ge(s["ck_y"], c + 1)
                    sc.activation(HT[:, 4:8, bass.ds(c * CH, CH)], ps[:, 4, :].rearrange("p (j t) -> p j t", j=4),
                                  ACT.Copy).then_inc(s["ck_y_in"], 1)

                act.wait_ge(s["post_v"], 3)
                sc.activation(KKt[:, :, :], HT[:, 4:8, :], ACT.Square).then_inc(s["post_a"], 1)
                act.wait_ge(s["post_p"], 4)
                inverse_root(At[:, :, :], ps[:, 4:8, :], HD, 1).then_inc(s["post_a"], 1)
                n["xt"] += 8

            def cross(L):
                if L == 0:
                    act.wait_ge(s["xt_ready"], n["xt"] - 7)
                    act.dma_start(memin[:, :, :], a["mem"][0].rearrange("(t p) d -> p t d", p=P)).then_inc(s["mem_in"], 16)
                norm(XT, xsq, SEQ, early=True)
                if L == 0:
                    act.wait_ge(s["mem_turned"], 4)
                    for q in range(4):
                        st.then(sc.activation(memT[:, 2 * q:2 * q + 2, :], ps[:, q, :].rearrange("p (k t) -> p k t", k=2), ACT.Copy))
                    norm(memT, memN, MEM)
                    for j in range(4):
                        take(mkT[:, j, :], ps[:, n["proj"] % 2, 0:MEM])
                    for t in range(MT):
                        take(mv[:, t, :])
                for h in range(4):
                    take(xq[:, h, :])
                off = 4 * (L + 1)

                def exps(t):
                    act.wait_ge(s["sm_max"], off + t + 1)
                    for h in range(4):
                        q = 4 * (t % 2) + h
                        ins = sc.activation(xp[:, t % 2, h, :], ps[:, 4 + 2 * (t % 2) + h // 2, MEM * (h % 2):MEM * (h % 2) + MEM], ACT.Exp,
                                            bias=snm[:, q:q + 1], scale=P ** -0.5, accum_out=sden[:, q:q + 1])
                    ins.then_inc(s["sm_exp"], 1)

                exps(0)
                for t in range(TT):
                    if t + 1 < TT:
                        exps(t + 1)
                    act.wait_ge(s["sm_turned"], off + t + 1)
                    sc.activation(xpT[:, :, t * P:t * P + P], ps[:, 2:4, :].rearrange("p b (c q) -> p (b c) q", c=4), ACT.Copy).then_inc(s["sm_pt"], 1)
                for h in range(4):
                    act.wait_ge(s["sm_pv"], 4 + 4 * L + h + 1)
                    sc.activation(xo[:, h, :], ps[:, 4 + h, :], ACT.Copy).then_inc(s["sm_out"], 1)
                n["xt"] += 8

            def odd():
                norm(XT, HT, SEQ, early=True)
                act.dma_start(gup[:, :], a["od_gate_up"][0]).then_inc(s["gup_in"], 16)
                for t in (gq, gk):
                    for j in range(4):
                        take(t[:, j, :])
                for h in range(2):
                    for t in range(TT):
                        take(gv[:, t, 512 * h:512 * h + 512])
                take(gdT[:, :], ps[0:16, n["proj"] % 2, :])
                for j in range(4):
                    take(gl[:, j, :], func=ACT.Identity, bias=col("od_gate_b", j))
                act.wait_ge(s["proj_taken"], n["proj"])
                st.then(sc.activation(ge[:, :, :], gl[:, :, :], ACT.Abs))
                st.then(sc.activation(ge[:, :, :], ge[:, :, :], ACT.Exp, scale=-1.0))
                sc.activation(ge[:, :, :], ge[:, :, :], ACT.Ln, bias=1.0).then_inc(s["pre_a"], 1)
                for j in range(KD):
                    take(og[:, j, :], func=ACT.Silu)
                    if j == 2:
                        act.wait_ge(s["g_cs"], 1)
                        sc.activation(gep[:, :, :], gcs[:, :, :], ACT.Exp, scale=1.0 / GATE_NORM)
                        sc.activation(gem[:, :, :], gcs[:, :, :], ACT.Exp, scale=-1.0 / GATE_NORM)
                        sc.activation(gfirst[:, :, :], gmid[:, :, :], ACT.Exp, scale=1.0 / GATE_NORM).then_inc(s["g_exp"], 1)
                with act.Fori(0, NCH) as c:
                    act.wait_ge(s["g_turned"], c + 1)
                    sc.activation(gkt[:, :], ps[:, 0, :], ACT.Copy).then_inc(s["g_tok"], 1)
                    act.wait_ge(s["g_y"], c + 1)
                    y = ps[:, 2:4, :].rearrange("p b (k t) -> p (b k) t", k=4)
                    sc.activation(gsq[:, :, :], y, ACT.Square).then_inc(s["g_sq"], 1)
                    sc.activation(HT[:, :, bass.ds(c * CH, CH)], y, ACT.Copy).then_inc(s["g_sq"], 1)
                    act.wait_ge(s["g_sum"], c + 1)
                    act.wait_ge(s["g_out"], c + 1)
                    inverse_root(grs[:, :, :].rearrange("p h t -> p (h t)"), ps[:, 6, :], 256, 0, s["g_ln"], c + 1).then_inc(s["g_rs"], 1)
                n["xt"] += 8

            def moe(L, pairs):
                for o, k, w in ((0, NG, a["moe_w_group"]), (NG, NX, a["moe_w_expert"])):
                    act.dma_start(wr[:, :, o:o + k], w[L].rearrange("(k p) n -> p k n", p=P)).then_inc(s["wr_in"], 16)
                norm(XT, HT, SEQ, early=True)
                for t in range(TT):
                    act.wait_ge(s["h_turned"], TT * L + t + 1)
                    sc.activation(hk[:, t, :].rearrange("p (b n) -> p b n", b=2), ps[:, 2 * (t % 2):2 * (t % 2) + 2, :], ACT.Copy).then_inc(s["h_taken"], 1)
                    act.wait_ge(s["h_taken"], TT * L + t + 1)
                    act.dma_start(hrows[t * P:t * P + P, :], hk[:, t, :]).then_inc(s["h_stored"], 16)
                act.wait_ge(s["plan_v"], PLAN_V * L + 1)
                sc.activation(gex[:, :, :], gex[:, :, :], ACT.Exp).then_inc(s["plan_a"], 1)
                act.wait_ge(s["plan_v"], PLAN_V * L + 2)
                sc.activation(ee[:, :], dv[:, :], ACT.Exp).then_inc(s["plan_a"], 1)

                act.wait_ge(s["plan_v"], PLAN_V * (L + 1))
                trips = act.value_load(nit[0:1, 0:1], min_val=MIN_TRIPS, max_val=MAX_TRIPS)
                with act.Fori(0, trips) as i:
                    for b in range(2):
                        k = i * 2 + (pairs * 2 + b)
                        act.wait_ge(s["hh_done"], k + (L + 3))
                        sc.activation(hs[b][:, :], ps[:, 2 + b, :], ACT.Copy).then_inc(s["hs_in"], 1)
                        act.wait_ge(s["hs_turned"], k + 1)
                        sc.activation(sl[b][:, :, :], ps[:, 4, :].rearrange("p (f c) -> p f c", f=4)[:, :, 0:BLK], ACT.Silu).then_inc(s["sl_in"], 1)
                        act.wait_ge(s["y_done"], k + (L + 3))
                        for h in range(2):
                            ins = sc.activation(ysb[64 * b:64 * b + 64, 512 * h:512 * h + 512], ps[64 * h:64 * h + 64, 6, :], ACT.Copy)
                        ins.then_inc(s["y_in"], 1)
                n["xt"] += 8
                return trips

            even()
            cross(0)
            pairs = moe(0, 0)
            odd()
            cross(1)
            moe(1, pairs)
            norm(XT, HT, SEQ, early=True)
            for t in range(TT):
                act.wait_ge(s["f_turned"], t + 1)
                sc.activation(osb[:, t, :].rearrange("p (b n) -> p b n", b=2), ps[:, 2 * (t % 2):2 * (t % 2) + 2, :], ACT.Copy).then_inc(s["f_taken"], 1)

        @block.tensor
        def _(pe):
            te = nc.tensor
            n = {"proj": 0, "norm": 0, "xt": 8}

            def mm(o, l, r, first=True, last=True):
                return te.matmul(o, l, r, start=first, stop=last)

            for name, first in (("ck_turned", 1), ("hh_done", 1), ("y_done", 1), ("xg_turned", 1), ("g_added", 2)):
                pe.sem_inc(s[name], first)
            pe.wait_ge(s["ident_in"], 1)
            pe.wait_ge(s["x_in"], 16)
            for k in range(KD):
                for t in range(TT):
                    ins = te.transpose(ps[:, k, t * P:t * P + P], xin[:, t, k * P:k * P + P], ident[:, :])
                ins.then_inc(s["x_turned"], 1)
            def norm(dst, width):
                pe.wait_ge(s["xt_ready"], n["xt"])
                if n["norm"]:
                    pe.wait_ge(s["rstd_ready"], n["norm"])
                for q in range(4):
                    pe.wait_ge(s["sq_ready"], 4 * n["norm"] + q + 1)
                    for k in (2 * q, 2 * q + 1):
                        ins = mm(ps[:, 7, 0:width], ones[:, :], dst[:, k, :], k == 0, k == KD - 1)
                ins.then_inc(s["sum_ready"], 1)
                n["norm"] += 1

            def normed(k):
                pe.wait_ge(s["h_ready"], 8 * (n["norm"] - 1) + k + 1)

            def project(o, pairs, first=False):
                if n["proj"] >= 2:
                    pe.wait_ge(s["proj_taken"], n["proj"] - 1)
                for k, (l, r) in enumerate(pairs):
                    if first:
                        normed(k)
                    ins = mm(o, l, r, k == 0, k == len(pairs) - 1)
                n["proj"] += 1
                ins.then_inc(s["proj_done"], 1)

            def bank():
                return ps[:, n["proj"] % 2, :]

            def weights(name):
                slot, loaded, _ = use_of(name)
                pe.wait_ge(w_loaded[slot], loaded)
                return slot

            def residual(tiles_of, count):
                for mt in range(KD):
                    if mt >= 2:
                        pe.wait_ge(s["xt_ready"], n["xt"] + mt - 1)
                    pairs = tiles_of(mt)
                    for k, (l, r) in enumerate(pairs):
                        ins = mm(ps[:, 2 + mt % 2, :], l, r, k == 0, k == len(pairs) - 1)
                    ins.then_inc(s["res_done"], 1)
                n["xt"] += 8

            def even():
                norm(HT, SEQ)
                pe.wait_ge(s["xt_ready"], 2)
                pe.wait_ge(s["par_in"], 16 * (len(PARAMS) + 5))
                te.transpose(ps[:, 0, 0:NPAR], prow[:, :], ident[0:NPAR, 0:NPAR]).then_inc(s["par_turned"], 1)
                mm(ps[:, 1, 0:80], ones[0:1, :], brow[0:1, :]).then_inc(s["par_turned"], 1)
                pe.wait_ge(s["consts"], 1)
                slot = weights("ev_q")
                for j in range(4):
                    project(bank(), [(W8[slot][:, k, P * j:P * j + P], HT[:, k, :]) for k in range(KD)], first=j == 0)
                slot = weights("ev_kvx")
                project(bank(), [(W8[slot][:, k, 0:P], HT[:, k, :]) for k in range(KD)])
                pe.wait_ge(s["proj_taken"], n["proj"] - 1)
                for t in range(TT):
                    for k in range(KD):
                        ins = mm(ps[:, n["proj"] % 2, t * P:t * P + P], HT[:, k, t * P:t * P + P], W8[slot][:, k, P:2 * P],
                                 k == 0, k == KD - 1)
                n["proj"] += 1
                ins.then_inc(s["proj_done"], 1)

                def scores(b):
                    pe.wait_ge(s["proj_taken"], 5 if b == 0 else 6)
                    if b:
                        pe.wait_ge(s["sm_pt"], b)
                    for j in range(4):
                        for g in range(2):
                            r = slice(64 * g, 64 * g + 64)
                            ins = mm(ps[:, 4 + 2 * g + j // 2, 256 * (j % 2):256 * (j % 2) + 256],
                                     sqT[r, j, b * P:b * P + P], skT[r, b * P:b * P + 2 * P])
                    ins.then_inc(s["sm_scored"], 1)

                def turn(b):
                    pe.wait_ge(s["sm_norm"], b + 1)
                    for i in range(16):
                        ins = te.transpose(ps[:, 4 + i // 4, P * (i % 4):P * (i % 4) + P], sp[:, i // 2, P * (i % 2):P * (i % 2) + P], ident[:, :])
                    ins.then_inc(s["sm_turned"], 1)

                def pv(b):
                    pe.wait_ge(s["sm_pt"], b + 1)
                    if b:
                        pe.wait_ge(s["sm_out"], b)
                    for j in range(4):
                        for g in range(2):
                            for half in range(2):
                                i = 2 * (4 * g + j) + half
                                ins = mm(ps[64 * g:64 * g + 64, 2, j * P:j * P + P], sv[:, b + half, 64 * g:64 * g + 64],
                                         spT[:, P * i:P * i + P], half == 0, half == 1)
                    ins.then_inc(s["sm_pv"], 1)

                i = 0
                for name, off, k_tiles in (("ev_kvx", 256, 2), ("ev_r", 0, 4), ("ev_k", 0, 4), ("ev_v", 0, 4)):
                    slot = weights(name)
                    for j in range(k_tiles):
                        o = off + j * P
                        project(bank(), [(W8[slot][:, k, o:o + P], HT[:, k, :]) for k in range(KD)])
                        if i >= 4 and (i - 4) % 3 == 0:
                            turn((i - 4) // 3)
                        if i >= 5 and (i - 5) % 3 == 0:
                            pv((i - 5) // 3)
                        if i >= 2 and (i - 2) % 3 == 0 and (i - 2) // 3 < 4:
                            scores((i - 2) // 3)
                        i += 1
                pv(3)

                pe.wait_ge(s["lora_in"], 48)
                pe.wait_ge(s["pre_a"], 1)
                for r in range(2):
                    q = slice(64 * r, 64 * r + 64)
                    for j in range(4):
                        project(bank(), [(lora[q, 0, j * P:j * P + P], X2[q, 0, :])])
                for j in range(4):
                    pe.wait_ge(s["pre_a"], 3 + j)
                    mm(ps[:, 4 + j, :], pair[:, :], HT[:, j, :]).then_inc(s["pre_p"], 1)

                with pe.Fori(0, NCH) as c:
                    pe.wait_ge(s["ck_el"], c + 1)
                    pe.wait_ge(s["ck_vc"], c + 1)
                    pe.wait_ge(s["ck_y_in"], c + 1)
                    for k, src in enumerate((AR[:, :, 0, :], BT[:, :, :], KT[:, :, :], VC[:, :, :])):
                        for j in range(4):
                            ins = te.transpose(ps[:, k, j * P:j * P + P], src[:, j, :], ident[:, :])
                        ins.then_inc(s["ck_turned"], 1)
                    pe.wait_ge(s["ck_sn"], c + 1)
                    for x, lt in enumerate((BT, KT)):
                        for q in range(2):
                            for r in range(2):
                                if x:
                                    pe.wait_ge(s["ck_masked"], c * 8 + (2 * q + r + 1))
                                rr = slice(64 * r, 64 * r + 64)
                                for j in (2 * q, 2 * q + 1):
                                    ins = mm(ps[:, 4 + 2 * q + r, 256 * (j % 2):256 * (j % 2) + 256], lt[rr, j, :],
                                             AR[rr, j, :, :].rearrange("p x t -> p (x t)"))
                                ins.then_inc(s["ck_mat"], 1)
                    pe.wait_ge(s["ck_tok"], c * 4 + 4)
                    for l in range(1, LEVELS):
                        for r in range(2):
                            k = 2 * (l - 1) + r
                            pe.wait_ge(s["iv_x"], c * (2 * LEVELS) + (k + 1))
                            pe.wait_ge(s["iv_tl"], c * (2 * LEVELS - 2) + (k + 1))
                            for j in range(4):
                                ins = mm(ps[:, r, j * P:j * P + P], TL[r][:, j, :], XI[r][:, j, :])
                            ins.then_inc(s["iv_u"], 1)
                        if l == 1:
                            pe.wait_ge(s["ck_masked"], c * 8 + 8)
                            for j in range(4):
                                for r in range(2):
                                    h = 64 * (2 * j + r)
                                    ins = mm(ps[:, 3, h:h + 64], MK[:, j, r, 0, :], TOK[:, 3, h:h + 64])
                            ins.then_inc(s["akv_done"], 1)
                        for r in range(2):
                            k = 2 * (l - 1) + r
                            pe.wait_ge(s["iv_ul"], c * (2 * LEVELS - 2) + (k + 1))
                            for j in range(4):
                                if l == SQUARE:
                                    mm(ps[:, 5 + r, j * HD:j * HD + HD], XJ[r][:, j, :], halves(UL[r][:, j, :], l)[0])
                                ins = mm(ps[:, (2, 4)[r], j * HD:j * HD + HD], UL[r][:, j, :], halves(XJ[r][:, j, :], l)[1])
                            ins.then_inc(s["iv_v"], 1)
                    for r in range(2):
                        pe.wait_ge(s["iv_x"], c * (2 * LEVELS) + (2 * LEVELS - 1 + r))
                        for j in range(4):
                            h = 64 * (2 * j + r)
                            ins = mm(ps[64 * r:64 * r + 64, 7, j * P:j * P + P], TOK[:, 0, h:h + 64], XJ[r][:, j, :])
                    ins.then_inc(s["wt_done"], 1)
                    pe.wait_ge(s["akv_in"], c + 1)
                    pe.wait_ge(s["wt_in"], c + 1)
                    for j in range(4):
                        for r in range(2):
                            h, rr = 64 * (2 * j + r), slice(64 * r, 64 * r + 64)
                            o = ps[:, r, j * HD:j * HD + HD]
                            mm(o, XJ[r][:, j, :], AKV[:, h:h + 64], True, False)
                            ins = mm(o, WT[rr, j, :], Sn[rr, j, :], False, True)
                    ins.then_inc(s["u_done"], 1)
                    pe.wait_ge(s["u_in"], c + 1)
                    pe.wait_ge(s["ck_rh"], c + 1)
                    for j in range(4):
                        for r in range(2):
                            h, rr = 64 * (2 * j + r), slice(64 * r, 64 * r + 64)
                            o = ps[rr, 4, j * P:j * P + P]
                            mm(o, Us[:, j, r, :], MA[:, j, r, 1, :], True, False)
                            mm(o, TOK[:, 3, h:h + 64], MK[:, j, r, 1, :], False, False)
                            ins = mm(o, Sn[rr, j, :], RH[rr, j, :], False, True)
                    ins.then_inc(s["ck_y"], 1)
                    for j in range(4):
                        for r in range(2):
                            h, rr = 64 * (2 * j + r), slice(64 * r, 64 * r + 64)
                            o = ps[rr, 5, j * HD:j * HD + HD]
                            mm(o, TOK[:, 1, h:h + 64], Us[:, j, r, :], True, False)
                            ins = mm(o, TOK[:, 2, h:h + 64], TOK[:, 3, h:h + 64], False, True)
                    ins.then_inc(s["ck_s"], 1)

                pe.wait_ge(s["ck_y_in"], NCH + 1)
                for j in range(4):
                    ins = mm(ps[:, j, :], lora[:, 1, j * P:j * P + P], X2[:, 1, :])
                ins.then_inc(s["post_p"], 1)
                pe.wait_ge(s["post_v"], 1)
                for j in range(4):
                    ins = mm(ps[:, 4 + j, :], pair[:, :], KKt[:, j, :])
                ins.then_inc(s["post_p"], 1)
                pe.wait_ge(s["post_v"], 2)
                for j in range(4):
                    ins = mm(ps[:, 4 + j, :], pair[:, :], HT[:, 4 + j, :])
                ins.then_inc(s["post_p"], 1)
                pe.wait_ge(s["post_a"], 1)
                for j in range(4):
                    ins = mm(ps[:, 4 + j, :], pair[:, :], KKt[:, j, :])
                ins.then_inc(s["post_p"], 1)

                pe.wait_ge(s["post_v"], 4)
                slots = [weights("ev_o0"), weights("ev_o1")]
                residual(lambda mt: [(W8[slots[mt // 4]][:, k, P * (mt % 4):P * (mt % 4) + P],
                                      (SO if k < 4 else HT)[:, k, :]) for k in range(KD)], KD)

            def cross(L):
                norm(xsq, SEQ)
                if L == 0:
                    pe.wait_ge(s["mem_in"], 16)
                    for q in range(4):
                        for k in (2 * q, 2 * q + 1):
                            for t in range(MT):
                                o = 256 * (k % 2) + t * P
                                ins = te.transpose(ps[:, q, o:o + P], memin[:, t, k * P:k * P + P], ident[:, :])
                        ins.then_inc(s["mem_turned"], 1)
                    norm(memN, MEM)
                    slot = weights("xk")
                    for j in range(4):
                        project(ps[:, n["proj"] % 2, 0:MEM], [(W8[slot][:, k, P * j:P * j + P], memN[:, k, :]) for k in range(KD)], first=j == 0)
                    slot = weights("xv")
                    for t in range(MT):
                        project(bank(), [(memN[:, k, t * P:t * P + P], W8[slot][:, k, :]) for k in range(KD)])
                slot = weights(f"xq{L}")
                for h in range(4):
                    project(bank(), [(W8[slot][:, k, P * h:P * h + P], HT[:, k, :]) for k in range(KD)], first=h == 0)
                off = 4 * (L + 1)
                pe.wait_ge(s["proj_taken"], n["proj"])

                def scores(t):
                    if t >= 2:
                        pe.wait_ge(s["sm_exp"], off + t - 1)
                    for h in range(4):
                        ins = mm(ps[:, 4 + 2 * (t % 2) + h // 2, MEM * (h % 2):MEM * (h % 2) + MEM], xq[:, h, t * P:t * P + P], mkT[:, h, :])
                    ins.then_inc(s["sm_scored"], 1)

                scores(0)
                for t in range(TT):
                    if t + 1 < TT:
                        scores(t + 1)
                    pe.wait_ge(s["sm_norm"], off + t + 1)
                    if t:
                        pe.wait_ge(s["sm_pt"], off + t)
                    for i in range(8):
                        ins = te.transpose(ps[:, 2 + i // 4, P * (i % 4):P * (i % 4) + P], xp[:, t % 2, i // 2, P * (i % 2):P * (i % 2) + P], ident[:, :])
                    ins.then_inc(s["sm_turned"], 1)
                pe.wait_ge(s["sm_pt"], off + TT)
                for h in range(4):
                    for t in range(MT):
                        ins = mm(ps[:, 4 + h, :], mv[:, t, P * h:P * h + P], xpT[:, 2 * h + t, :], t == 0, t == 1)
                    ins.then_inc(s["sm_pv"], 1)
                slot = weights(f"xo{L}")
                pe.wait_ge(s["sm_out"], off + TT)
                residual(lambda mt: [(W4[slot][:, k, P * mt:P * mt + P], xo[:, k, :]) for k in range(4)], 4)

            def odd():
                norm(HT, SEQ)
                for name in ("od_q", "od_k"):
                    slot = weights(name)
                    for j in range(4):
                        project(bank(), [(W8[slot][:, k, P * j:P * j + P], HT[:, k, :]) for k in range(KD)],
                                first=name == "od_q" and j == 0)
                for name in ("od_v0", "od_v1"):
                    slot = weights(name)
                    for t in range(TT):
                        project(bank(), [(HT[:, k, t * P:t * P + P], W8[slot][:, k, :]) for k in range(KD)])
                slot = weights("od_gd")
                project(ps[0:16, n["proj"] % 2, :], [(W8[slot][:, k, 0:16], HT[:, k, :]) for k in range(KD)])
                pe.wait_ge(s["gup_in"], 16)
                pe.wait_ge(s["proj_taken"], n["proj"])
                for j in range(4):
                    project(bank(), [(gup[:, P * j:P * j + P], gdT[:, :])])
                for name in ("od_og0", "od_og1"):
                    slot = weights(name)
                    for j in range(4):
                        project(bank(), [(W8[slot][:, k, P * j:P * j + P], HT[:, k, :]) for k in range(KD)])
                pe.wait_ge(s["proj_taken"], n["proj"])
                pe.wait_ge(s["g_scaled"], 1)
                with pe.Fori(0, NCH // 2) as i:
                    for b in range(2):
                        c = i * 2 + b
                        t = bass.ds(c * CH, CH)
                        pe.wait_ge(s["g_copied"], c + 1)
                        for h in range(4):
                            ins = te.transpose(ps[:, 0, h * P:h * P + P], gkc[b][:, h, :], ident[:, :])
                        ins.then_inc(s["g_turned"], 1)
                        for h in range(4):
                            ins = mm(ps[:, 1, h * P:h * P + P], gkc[b][:, h, :], gq[:, h, t])
                        ins.then_inc(s["g_mat"], 1)
                        pe.wait_ge(s["g_masked"], c + 1)
                        pe.wait_ge(s["g_state"], c + 1)
                        for e in range(KD):
                            o = ps[:, 2 + e // 4, P * (e % 4):P * (e % 4) + P]
                            mm(o, gvc[b][:, e * P:e * P + P], gat[:, e // 2, :], True, False)
                            ins = mm(o, gsn[:, e // 2, P * (e % 2):P * (e % 2) + P], gq[:, e // 2, t], False, True)
                        ins.then_inc(s["g_y"], 1)
                        pe.wait_ge(s["g_tok"], c + 1)
                        for h in range(4):
                            ins = mm(ps[:, 4 + h // 2, 256 * (h % 2):256 * (h % 2) + 256], gkt[:, h * P:h * P + P], gvc[b][:, 256 * h:256 * h + 256])
                        ins.then_inc(s["g_added"], 1)
                        pe.wait_ge(s["g_sq"], c * 2 + 2)
                        for h in range(4):
                            for u in range(2):
                                ins = mm(ps[:, 6, h * P:h * P + P], ones[:, :], gsq[:, 2 * h + u, :], u == 0, u == 1)
                        ins.then_inc(s["g_sum"], 1)
                pe.wait_ge(s["g_out"], NCH + 1)
                slots = [weights("od_o0"), weights("od_o1")]
                residual(lambda mt: [(W8[slots[mt // 4]][:, k, P * (mt % 4):P * (mt % 4) + P], HT[:, k, :]) for k in range(KD)], KD)

            def moe(L, pairs):
                norm(HT, SEQ)
                pe.wait_ge(s["wr_in"], 32 * (L + 1))
                for t in range(TT):
                    for k in range(KD):
                        if t == 0:
                            normed(k)
                        ins = mm(ps[:, 4, 64 * t:64 * t + NR], HT[:, k, t * P:t * P + P], wr[:, k, :], k == 0, k == KD - 1)
                ins.then_inc(s["plan_p"], 1)
                for t in range(TT):
                    if t >= 2:
                        pe.wait_ge(s["h_taken"], TT * L + t - 1)
                    for k in range(KD):
                        ins = te.transpose(ps[:, 2 * (t % 2) + k // 4, P * (k % 4):P * (k % 4) + P], HT[:, k, t * P:t * P + P], ident[:, :])
                    ins.then_inc(s["h_turned"], 1)
                pe.wait_ge(s["plan_v"], PLAN_V * L + 3)
                for t in range(TT):
                    for u in range(t + 1):
                        mm(ps[:, 5, NX * t:NX * t + NX], (tri[:, 0, :] if u == t else ones[:, :]), msk[:, u, :], u == 0, u == t)
                for u in range(TT):
                    ins = mm(ps[:, 5, P:P + NX], ones[:, :], msk[:, u, :], u == 0, u == TT - 1)
                ins.then_inc(s["plan_p"], 1)
                pe.wait_ge(s["plan_v"], PLAN_V * L + 4)
                for v, table in enumerate((bhot, bgate)):
                    for b in range(2):
                        for i in range(8):
                            ins = mm(ps[64 * b:64 * b + 64, 6, 32 * v:32 * v + NPAIR], rhot[:, i, :],
                                     table[:, i, :].rearrange("p (n b) -> p b n", b=2)[:, b, :], i == 0, i == 7)
                ins.then_inc(s["plan_p"], 1)
                pe.wait_ge(s["plan_p"], 3 * (L + 1))
                pe.sem_inc(s["hh_done"], 1)
                pe.sem_inc(s["y_done"], 1)
                pe.wait_ge(s["plan_v"], PLAN_V * (L + 1))
                trips = pe.value_load(nit[0:1, 0:1], min_val=MIN_TRIPS, max_val=MAX_TRIPS)

                def turn_rows(arrived):
                    pe.wait_ge(s["xg_in"], arrived)
                    for k in range(KD):
                        ins = te.transpose(ps[:, k // 4, P * (k % 4):P * (k % 4) + P], xg[:, k * P:k * P + P], ident[:, :])
                    ins.then_inc(s["xg_turned"], 1)

                def add_pair(free):
                    for k in range(KD):
                        free(k)
                        ins = mm(ps[:, (5, 7)[k % 2], :], ysb[:, k * P:k * P + P], spread[:, :])
                        ins.then_inc(s["added"], 1)

                turn_rows(pairs * 16 + 16 * (L + 1))
                with pe.Fori(0, trips) as i:
                    for b in range(2):
                        k0 = i * 2 + (pairs * 2 + b)
                        if b == 0:
                            pe.wait_ge(s["xgT_in"], i + (pairs + (L + 1)))
                        pe.wait_ge(w13_in[b], (i + 1) * 32 + pairs * 32)
                        for k in range(KD):
                            x = xgT[:, k, BLK * b:BLK * b + BLK]
                            mm(ps[0:64, 2 + b, :], x, W8[EXPERT[b]][:, k, :], k == 0, k == KD - 1)
                            ins = mm(ps[64:128, 2 + b, :], x, W8[EXPERT[b] + 1][:, k, :], k == 0, k == KD - 1)
                        ins.then_inc(s["hh_done"], 1)
                        if b == 0:
                            pe.wait_ge(s["y_in"], k0 + 1)
                            pe.wait_ge(s["spread_in"], i + (pairs + (L + 1)))
                            add_pair(lambda k: pe.wait_ge(s["add_in"], i * 8 + (pairs * 8 + (k + 1))))
                        else:
                            turn_rows(i * 16 + (pairs * 16 + 16 * (L + 2)))
                        pe.wait_ge(s["hs_in"], k0 + 1)
                        for f in range(4):
                            ins = te.transpose(ps[:, 4, f * P:f * P + P], hs[b][:, f * P:f * P + P], ident[:, :])
                        ins.then_inc(s["hs_turned"], 1)
                        pe.wait_ge(s["act_in"], k0 + 1)
                        pe.wait_ge(w2_in[b], (i + 1) * 16 + pairs * 16)
                        pe.wait_ge(s["y_in"], k0 + 1)
                        for f in range(4):
                            for h in range(2):
                                ins = mm(ps[64 * h:64 * h + 64, 6, :], act_[b][:, f, :], W4[EXPERT[b] + 2][:, f, 512 * h:512 * h + 512],
                                         f == 0, f == 3)
                        ins.then_inc(s["y_done"], 1)
                pe.wait_ge(s["y_in"], (trips + pairs) * 2 + 1)
                pe.wait_ge(s["spread_in"], trips + (pairs + (L + 1)))
                pe.wait_ge(s["add_in"], (trips + pairs) * 8 + 2)
                pe.sem_inc(s["go"], 1)

                def taken(k):
                    if k >= 2:
                        pe.wait_ge(s["xt_ready"], n["xt"] + k - 1)

                add_pair(taken)
                n["xt"] += 8
                return trips

            even()
            cross(0)
            pairs = moe(0, 0)
            odd()
            cross(1)
            moe(1, pairs)
            norm(HT, SEQ)
            for t in range(TT):
                if t >= 2:
                    pe.wait_ge(s["f_taken"], t - 1)
                for k in range(KD):
                    if t == 0:
                        normed(k)
                    ins = te.transpose(ps[:, 2 * (t % 2) + k // 4, P * (k % 4):P * (k % 4) + P], HT[:, k, t * P:t * P + P], ident[:, :])
                ins.then_inc(s["f_turned"], 1)

        @block.vector
        def _(dve):
            st = Steps(dve, s["v_step"])
            ve = nc.vector
            n = {"norm": 0, "xt": 8}

            def bcast(ap, shape):
                return ap.broadcast_to(shape)

            dve.sem_inc(s["add_in"], 2)
            for k in range(KD):
                dve.wait_ge(s["x_turned"], k + 1)
                ve.tensor_copy(XT[:, k, :], ps[:, k, :]).then_inc(s["xt_ready"], 1)
            dve.wait_ge(s["par_turned"], 2)
            st.then(ve.tensor_copy(par[:, :], ps[:, 0, 0:NPAR]))
            st.then(ve.tensor_copy(bc[:, :], ps[:, 1, 0:80]))
            ve.tensor_scalar(omu[:, :], par[:, PARAMS["ev_mu"][0]:PARAMS["ev_mu"][0] + 14], -1.0, 1.0, ALU.mult, ALU.add)
            ve.tensor_scalar(oka[:, :], par[:, PARAMS["ev_k_a"][0]:PARAMS["ev_k_a"][0] + 4], -1.0, 1.0, ALU.mult, ALU.add).then_inc(s["par_ready"], 1)

            def norm(src, dst, width, gain, first):
                n["norm"] += 1
                dve.wait_ge(s["rstd_ready"], n["norm"])
                for k in range(KD):
                    ve.scalar_tensor_tensor(dst[:, k, :], src[:, k, :], col(gain, first + k), rs[:, 0:width], ALU.mult, ALU.mult).then_inc(s["h_ready"], 1)

            def residual():
                for mt in range(KD):
                    dve.wait_ge(s["res_done"], n["res"] + mt + 1)
                    ve.tensor_tensor(XT[:, mt, :], ps[:, 2 + mt % 2, :], XT[:, mt, :], ALU.add).then_inc(s["xt_ready"], 1)
                n["res"] += 8

            n["res"] = 0

            def even():
                dve.wait_ge(s["par_ready"], 1)
                norm(XT, HT, SEQ, "norm_mix", 0)

                def softmax(b):
                    dve.wait_ge(s["sm_scored"], b + 1)
                    dve.wait_ge(s["sm_turned"], b)
                    st.then(ve.scalar_tensor_tensor(sp[:, :, :], ps[:, 4:8, :].rearrange("p b (h k) -> p (b h) k", h=2), HD ** -0.5,
                                                    bcast(smask[:, min(b, 1), :].unsqueeze(1), [P, 8, 2 * P]), ALU.mult, ALU.add))
                    st.then(ve.tensor_reduce(smx, sp[:, :, :], AX.X, ALU.max))
                    st.then(ve.tensor_tensor(smx, smx, bc[:, 0:8], ALU.max))
                    ve.tensor_scalar(snm, smx, -1.0, None, ALU.mult)
                    ve.tensor_tensor(ses, bc[:, 0:8], smx, ALU.subtract).then_inc(s["sm_max"], 1)
                    dve.wait_ge(s["sm_exp"], b + 1)
                    st.then(ve.tensor_tensor(sden, sden, ses, ALU.add))
                    st.then(ve.reciprocal(srec, sden))
                    ve.tensor_tensor(sp[:, :, :], sp[:, :, :], bcast(srec.unsqueeze(2), [P, 8, 2 * P]), ALU.mult).then_inc(s["sm_norm"], 1)

                tiles = [X2[:, 0, :], X2[:, 1, :]] + [t[:, j, :] for t in (Rt, Kt, Vt) for j in range(4)]
                for i, dst in enumerate(tiles):
                    dve.wait_ge(s["proj_taken"], 6 + i + 1)
                    ve.tensor_tensor(dst[:, 1:SEQ], dst[:, 1:SEQ], shf[:, i % 2, 0:SEQ - 1], ALU.add).then_inc(s["shifted"], 1)
                    if i >= 2 and (i - 2) % 3 == 0 and (i - 2) // 3 < 4:
                        softmax((i - 2) // 3)

                dve.wait_ge(s["proj_taken"], 28)
                def cumulate(t):
                    for j in range(4):
                        ins = ve.tensor_tensor_scan(CS[:, j, :], ones[:, :], SGt[:, j, t], 0.0, ALU.mult, ALU.add)
                    st.then(ins)
                    ve.tensor_copy(mid.unsqueeze(2), CS[:, :, CH // 2 - 1:CH // 2]).then_inc(s["ck_scan"], 1)

                for j in range(4):
                    ve.tensor_scalar(HT[:, 4 + j, :], Kt[:, j, :], col("ev_k_k", j), None, ALU.mult)
                    ins = ve.tensor_scalar(ktmp[:, j, :], At[:, j, :], col("ev_k_a", j), oka[:, j:j + 1], ALU.mult, ALU.add)
                st.then(ins)
                dve.wait_ge(s["pre_a"], 6)
                st.then(ve.tensor_tensor(Kt[:, :, :], Kt[:, :, :], ktmp[:, :, :], ALU.mult))
                for j in range(4):
                    dve.wait_ge(s["pre_p"], j + 1)
                    ins = ve.tensor_scalar(KKt[:, j, :], ps[:, 4 + j, :], 1e-24, None, ALU.max)
                ins.then_inc(s["pre_v"], 1)
                cumulate(slice(0, CH))
                dve.wait_ge(s["pre_a"], 7)
                st.then(ve.scalar_tensor_tensor(KKt[:, :, :], HT[:, 4:8, :], -1.0, KKt[:, :, :], ALU.mult, ALU.mult))
                st.then(ve.scalar_tensor_tensor(At[:, :, :], At[:, :, :], -1.0, KKt[:, :, :], ALU.mult, ALU.mult))
                first = slice(0, CH)
                ve.memset(St[:, :, :], 0.0).then_inc(s["pre_v"], 1)
                dve.wait_ge(s["ck_exp"], 1)
                ve.tensor_tensor(AR[:, :, 1, :], Rt[:, :, first], Ep[:, :, :], ALU.mult)
                ve.tensor_tensor(AR[:, :, 0, :], KKt[:, :, first], Epp[:, :, :], ALU.mult)
                ve.tensor_tensor(BT[:, :, :], At[:, :, first], Em[:, :, :], ALU.mult)
                ve.tensor_tensor(KT[:, :, :], Kt[:, :, first], Em[:, :, :], ALU.mult).then_inc(s["ck_el"], 1)
                dve.wait_ge(s["pre_v"], 2)
                with dve.Fori(0, NCH) as c:
                    st.enter(c, 11 + 2 * SQUARE - 2)
                    following = bass.ds((c + 1) % NCH * CH, CH)
                    dve.wait_ge(s["ck_exp"], c + 1)
                    st.then(ve.tensor_copy(fc.unsqueeze(2), Ep[:, :, CH - 1:CH]))
                    st.then(ve.tensor_tensor(Sn[:, :, :], St[:, :, :], bcast(pc.unsqueeze(2), [P, 4, HD]), ALU.mult))
                    dve.sem_inc(s["ck_sn"], 1)
                    def mask(x):
                        for q in range(2):
                            for r in range(2):
                                k = 4 * x + 2 * q + r
                                dve.wait_ge(s["ck_mat"], c * 8 + (k + 1))
                                ve.tensor_tensor((MA, MK)[x][:, 2 * q:2 * q + 2, r, :, :].rearrange("p j x t -> p j (x t)"),
                                                 ps[:, 4 + 2 * q + r, :].rearrange("p (j n) -> p j n", j=2),
                                                 bcast(tri[:, :, :].rearrange("p x t -> p (x t)").unsqueeze(1), [P, 2, 2 * CH]),
                                                 ALU.mult).then_inc(s["ck_masked"], 1)

                    mask(0)
                    dve.wait_ge(s["ck_masked"], c * 8 + 4)

                    def masked(r, l):
                        return ve.tensor_tensor(TL[r][:, :, :] if l else XJ[r][:, :, :], MA[:, :, r, 0, :],
                                                bcast(level[:, l, :].unsqueeze(1), [P, 4, CH]), ALU.mult)

                    def flat(x):
                        return x[:, :, :].rearrange("p j t -> p (j t)")

                    for r in range(2):
                        st.then(masked(r, 0))
                        st.then(ve.tensor_tensor(XJ[r][:, :, :], XJ[r][:, :, :], bcast(ident[:, :].unsqueeze(1), [P, 4, CH]), ALU.add))
                        ve.transpose(flat(XI[r]), flat(XJ[r])).then_inc(s["iv_x"], 1)
                    for r in range(2):
                        masked(r, 1).then_inc(s["iv_tl"], 1)
                    mask(1)
                    for l in range(1, LEVELS):
                        k = 2 * (l - 1)
                        if l == 2:
                            cumulate(following)
                        if l + 1 < LEVELS:
                            for r in range(2):
                                dve.wait_ge(s["iv_u"], c * (2 * LEVELS - 2) + (k + r + 1))
                                masked(r, l + 1).then_inc(s["iv_tl"], 1)
                        for r in range(2):
                            dve.wait_ge(s["iv_v"], c * (2 * LEVELS - 2) + (k + r + 1))
                            dve.wait_ge(s["iv_x"], c * (2 * LEVELS) + (k + r + 1))
                            w = 1 << l
                            if l == SQUARE:
                                o = halves(flat(XI[r]), l)[0]
                                st.then(ve.tensor_tensor(o, ps[:, 5 + r, 0:256].rearrange("p (b w) -> p b w", w=w), o, ALU.add))
                            o = halves(flat(XJ[r]), l)[1]
                            ins = ve.tensor_tensor(o, ps[:, (2, 4)[r], 0:256].rearrange("p (b w) -> p b w", w=w), o, ALU.add)
                            if l < SQUARE:
                                st.then(ins)
                                ins = ve.transpose(flat(XI[r]), flat(XJ[r]))
                            ins.then_inc(s["iv_x"], 1)
                    dve.wait_ge(s["ck_s"], c + 1)
                    st.then(ve.tensor_tensor(Sn[:, :, :], ps[:, 5, 0:4 * HD].rearrange("p (j v) -> p j v", j=4), Sn[:, :, :], ALU.add))
                    st.then(ve.tensor_tensor(St[:, :, :], Sn[:, :, :], bcast(fc.unsqueeze(2), [P, 4, HD]), ALU.mult))
                    st.leave(NCH)

                dve.wait_ge(s["ck_el"], NCH + 1)
                for j in range(4):
                    ins = ve.scalar_tensor_tensor(KKt[:, j, :], Rt[:, j, :], col("ev_r_k", j), Kt[:, j, :], ALU.mult, ALU.mult)
                ins.then_inc(s["post_v"], 1)
                dve.wait_ge(s["post_p"], 2)
                ve.tensor_tensor(Vt[:, :, :], ps[:, 4:8, :], Vt[:, :, :], ALU.mult).then_inc(s["post_v"], 1)
                dve.wait_ge(s["post_p"], 3)
                ve.scalar_tensor_tensor(HT[:, 4:8, :], ps[:, 4:8, :], -1.0 / HD, HT[:, 4:8, :], ALU.mult, ALU.add).then_inc(s["post_v"], 1)
                dve.wait_ge(s["post_v"], 3)
                for j in range(4):
                    ve.scalar_tensor_tensor(SGt[:, j, :], HT[:, 4 + j, :], col("ev_lnx_w", j), ps[:, j, :], ALU.mult, ALU.mult)
                    ins = ve.scalar_tensor_tensor(Vt[:, j, :], Vt[:, j, :], col("ev_lnx_b", j), ps[:, j, :], ALU.add, ALU.mult)
                st.then(ins)
                dve.wait_ge(s["post_a"], 2)
                st.then(ve.tensor_tensor(HT[:, 4:8, :], SGt[:, :, :], At[:, :, :], ALU.mult))
                ve.tensor_tensor(HT[:, 4:8, :], HT[:, 4:8, :], Vt[:, :, :], ALU.add).then_inc(s["post_v"], 1)
                residual()

            def cross(L):
                norm(XT, HT, SEQ, "norm_xattn", 8 * L)
                if L == 0:
                    norm(memT, memN, MEM, "mem_norm", 0)
                off = 4 * (L + 1)

                def find_max(t):
                    q, p = slice(4 * (t % 2), 4 * (t % 2) + 4), 4 + 2 * (t % 2)
                    dve.wait_ge(s["sm_scored"], off + t + 1)
                    st.then(ve.tensor_reduce(smx[:, q], ps[:, p:p + 2, :].rearrange("p b (h k) -> p (b h) k", h=2), AX.X, ALU.max))
                    ve.tensor_scalar(snm[:, q], smx[:, q], -(P ** -0.5), None, ALU.mult).then_inc(s["sm_max"], 1)

                find_max(0)
                for t in range(TT):
                    if t + 1 < TT:
                        find_max(t + 1)
                    q = slice(4 * (t % 2), 4 * (t % 2) + 4)
                    dve.wait_ge(s["sm_exp"], off + t + 1)
                    st.then(ve.reciprocal(srec[:, q], sden[:, q]))
                    ve.tensor_tensor(xp[:, t % 2, :, :], xp[:, t % 2, :, :], bcast(srec[:, q].unsqueeze(2), [P, 4, MEM]), ALU.mult).then_inc(s["sm_norm"], 1)
                residual()

            def odd():
                norm(XT, HT, SEQ, "norm_mix", 8)
                dve.wait_ge(s["proj_taken"], 59)
                st.then(ve.tensor_scalar(gz[:, :, :], gl[:, :, :], 0.0, None, ALU.min))
                dve.wait_ge(s["pre_a"], 8)
                st.then(ve.tensor_tensor(gl[:, :, :], gz[:, :, :], ge[:, :, :], ALU.subtract))
                for c in range(NCH):
                    for j in range(4):
                        ins = ve.tensor_tensor_scan(gcs[:, j, c * CH:c * CH + CH], ones[:, :], gl[:, j, c * CH:c * CH + CH], 0.0, ALU.mult, ALU.add)
                st.then(ins)
                cs = gcs[:, :, :].rearrange("p h (c t) -> p (h c) t", t=CH)
                mids = gmid[:, :, :].rearrange("p h c -> p (h c)").unsqueeze(2)
                st.then(ve.tensor_copy(mids, cs[:, :, CH // 2 - 1:CH // 2]))
                ve.tensor_tensor(cs, cs, bcast(mids, [P, 4 * NCH, CH]), ALU.subtract).then_inc(s["g_cs"], 1)
                dve.wait_ge(s["g_exp"], 1)
                ve.memset(gnext[:, :, :], 1.0)
                ve.scalar_tensor_tensor(gq[:, :, :], gq[:, :, :], P ** -0.5, gep[:, :, :], ALU.mult, ALU.mult)
                st.then(ve.tensor_copy(gmid[:, :, :], gep[:, :, :].rearrange("p h (c t) -> p h c t", t=CH)[:, :, :, CH - 1]))
                st.then(ve.tensor_tensor(gnext[:, :, 0:NCH - 1], gmid[:, :, 0:NCH - 1], gfirst[:, :, 1:NCH], ALU.mult))
                ve.tensor_tensor(gk[:, :, :], gk[:, :, :], gem[:, :, :], ALU.mult).then_inc(s["g_scaled"], 1)
                ve.memset(gsn[:, :, :], 0.0).then_inc(s["g_state"], 1)
                for j in range(KD):
                    dve.wait_ge(s["proj_taken"], 60 + j)
                    ins = ve.tensor_scalar(og[:, j, :], og[:, j, :], col("od_onorm", j % 2), None, ALU.mult)
                dve.wait_ge(s["g_state"], 1)
                with dve.Fori(0, NCH) as c:
                    st.enter(c, 1)
                    dve.wait_ge(s["g_mat"], c + 1)
                    ve.tensor_tensor(gat[:, :, :], ps[:, 1, :].rearrange("p (h t) -> p h t", h=4),
                                     bcast(tri[:, 1, :].unsqueeze(1), [P, 4, CH]), ALU.mult).then_inc(s["g_masked"], 1)
                    dve.wait_ge(s["g_added"], c + 3)
                    st.then(ve.tensor_tensor(gsn[:, :, :], ps[:, 4:6, :].rearrange("p b (h v) -> p (b h) v", h=2), gsn[:, :, :], ALU.add))
                    ve.tensor_tensor(gsn[:, :, :], gsn[:, :, :], bcast(gnext[:, :, bass.ds(c, 1)], [P, 4, 256]), ALU.mult).then_inc(s["g_state"], 1)
                    st.leave(NCH)
                residual()

            def moe(L, pairs):
                norm(XT, HT, SEQ, "norm_moe", 8 * L)
                dve.wait_ge(s["plan_g"], L + 1)
                dve.wait_ge(s["plan_p"], 3 * L + 1)
                o = 8 + NR * L
                st.then(ve.memset(glp[:, :, :], NEG))
                st.then(ve.tensor_tensor(lg[:, :, :], ps[:, 4, 0:256].rearrange("p (t n) -> p t n", t=TT)[:, :, 0:NR],
                                         bcast(bc[:, o:o + NR].unsqueeze(1), [P, TT, NR]), ALU.add))
                st.then(ve.tensor_copy(glp[:, :, 0:NG], lg[:, :, 0:NG]))
                for t in range(TT):
                    ins = ve.max(g8[:, t, :], glp[:, t, :])
                st.then(ins)
                for t in range(TT):
                    ins = ve.max_index(gi8[:, t, :], g8[:, t, :], glp[:, t, :])
                st.then(ins)
                ve.tensor_tensor(gex[:, :, :], lg[:, :, 0:NG], bcast(g8[:, :, 0:1], [P, TT, NG]), ALU.subtract).then_inc(s["plan_v"], 1)
                st.then(ve.tensor_copy(gidx[:, :].unsqueeze(2), gi8[:, :, 0:1]))
                st.then(ve.tensor_tensor(ogh[:, :, :], bcast(io[:, 0:NG].unsqueeze(1), [P, TT, NG]),
                                         bcast(gidx[:, :].unsqueeze(2), [P, TT, NG]), ALU.is_equal))
                prod = cmp[:, 0:TT * NX].rearrange("p (t e g) -> p t e g", t=TT, e=NE)
                for g in range(NG):
                    ins = ve.tensor_tensor(prod[:, :, :, g], lg[:, :, NG + NE * g:NG + NE * g + NE], bcast(ogh[:, :, g:g + 1], [P, TT, NE]), ALU.mult)
                st.then(ins)
                st.then(ve.tensor_reduce(ein[:, :, :], prod, AX.X, ALU.add))
                for t in range(TT):
                    ins = ve.max(e8[:, t, :], ein[:, t, :])
                st.then(ins)
                for t in range(TT):
                    ins = ve.max_index(ei8[:, t, :], e8[:, t, :], ein[:, t, :])
                st.then(ins)
                ve.tensor_tensor(dv[:, :].unsqueeze(2), e8[:, :, 1:2], e8[:, :, 0:1], ALU.subtract).then_inc(s["plan_v"], 1)
                st.then(ve.tensor_copy(eid[:, :, :], ei8[:, :, 0:2]))
                st.then(ve.scalar_tensor_tensor(eid[:, :, :], bcast(gidx[:, :].unsqueeze(2), [P, TT, 2]), float(NE), eid[:, :, :], ALU.mult, ALU.add))
                st.then(ve.tensor_tensor(oh[:, :, :, :].rearrange("p t c e -> p (t c) e"), bcast(io[:, 0:NX].unsqueeze(1), [P, 8, NX]),
                                         bcast(eid[:, :, :].rearrange("p t c -> p (t c)").unsqueeze(2), [P, 8, NX]), ALU.is_equal))
                ve.tensor_tensor(msk[:, :, :], oh[:, :, 0, :], oh[:, :, 1, :], ALU.add).then_inc(s["plan_v"], 1)
                dve.wait_ge(s["plan_p"], 3 * L + 2)
                ve.tensor_copy(rk[:, :, :], ps[:, 5, 0:P].rearrange("p (t e) -> p t e", t=TT))
                st.then(ve.tensor_copy(cn[:, :], ps[:, 5, P:P + NX]))
                c8 = cmp[:, 0:NX * 8].rearrange("p (e k) -> p e k", k=8)
                st.then(ve.tensor_tensor(c8, bcast(cn[:, :].unsqueeze(2), [P, NX, 8]), bcast(io64[:, :].unsqueeze(1), [P, NX, 8]), ALU.is_gt))
                st.then(ve.tensor_reduce(nb[:, :], c8, AX.X, ALU.add))
                st.then(ve.tensor_scalar(nb[:, 0:1], nb[:, 0:1], 1.0, None, ALU.max))
                st.then(ve.tensor_tensor_scan(pend[:, :], ones[:, 0:NX], nb[:, :], 0.0, ALU.mult, ALU.add))
                st.then(ve.tensor_tensor(pst[:, :], pend[:, :], nb[:, :], ALU.subtract))

                def experts_of(lo, hi):
                    ce = cmp[:, 0:(hi - lo) * NX].rearrange("p (b e) -> p b e", e=NX)
                    st.then(ve.tensor_tensor(ce, bcast(pend[:, :].unsqueeze(1), [P, hi - lo, NX]),
                                             bcast(io[:, lo:hi].unsqueeze(2), [P, hi - lo, NX]), ALU.is_le))
                    st.then(ve.tensor_reduce(bef[:, lo:hi], ce, AX.X, ALU.add))
                    st.then(ve.tensor_scalar(bef[:, lo:hi], bef[:, lo:hi], float(NX - 1), None, ALU.min))
                    st.then(ve.tensor_copy(bei[:, lo:hi], bef[:, lo:hi]))

                experts_of(0, 2)
                dve.sem_inc(s["first_in"], 1)
                oh8 = oh[:, :, :, :].rearrange("p t c e -> p (t c) e")
                pe8 = cmp[:, 0:8 * NX].rearrange("p (i e) -> p i e", i=8)
                for ci in range(2):
                    ins = ve.tensor_tensor(cmp[:, 0:8 * NX].rearrange("p (t c e) -> p t c e", t=TT, c=2)[:, :, ci, :], oh[:, :, ci, :], rk[:, :, :], ALU.mult)
                st.then(ins)
                st.then(ve.tensor_reduce(selr[:, :], pe8, AX.X, ALU.add))
                st.then(ve.tensor_tensor(pe8, oh8, bcast(pst[:, :].unsqueeze(1), [P, 8, NX]), ALU.mult))
                st.then(ve.tensor_reduce(selp[:, :], pe8, AX.X, ALU.add))
                r8 = cmp[:, 0:64].rearrange("p (i k) -> p i k", k=8)
                st.then(ve.tensor_tensor(r8, bcast(selr[:, :].unsqueeze(2), [P, 8, 8]), bcast(io64[:, :].unsqueeze(1), [P, 8, 8]), ALU.is_ge))
                st.then(ve.tensor_reduce(rq[:, :], r8, AX.X, ALU.add))
                st.then(ve.tensor_scalar(rq[:, :], rq[:, :], -1.0, None, ALU.add))
                st.then(ve.tensor_tensor(blk[:, :], selp[:, :], rq[:, :], ALU.add))
                st.then(ve.scalar_tensor_tensor(brk[:, :], rq[:, :], -float(BLK), selr[:, :], ALU.mult, ALU.add))
                st.then(ve.tensor_tensor(rhot[:, :, :], bcast(io[:, 0:BLK].unsqueeze(1), [P, 8, BLK]), bcast(brk[:, :].unsqueeze(2), [P, 8, BLK]), ALU.is_equal))
                st.then(ve.tensor_tensor(bhot[:, :, :], bcast(io[:, 0:NBLK].unsqueeze(1), [P, 8, NBLK]), bcast(blk[:, :].unsqueeze(2), [P, 8, NBLK]), ALU.is_equal))
                dve.wait_ge(s["plan_a"], 2 * L + 2)
                st.then(ve.tensor_reduce(pg[:, :], gex[:, :, :], AX.X, ALU.add))
                st.then(ve.tensor_scalar(dv[:, :], ee[:, :], 1.0, None, ALU.add))
                st.then(ve.tensor_tensor(pg[:, :], pg[:, :], dv[:, :], ALU.mult))
                st.then(ve.reciprocal(gate[:, :, 0:1], pg[:, :].unsqueeze(2)))
                st.then(ve.tensor_tensor(gate[:, :, 1:2], gate[:, :, 0:1], ee[:, :].unsqueeze(2), ALU.mult))
                st.then(ve.tensor_tensor(bgate[:, :, :], bhot[:, :, :], bcast(gate[:, :, :].rearrange("p t c -> p (t c)").unsqueeze(2), [P, 8, NBLK]), ALU.mult))
                for t in range(TT):
                    ins = ve.tensor_scalar(bhot[:, 2 * t:2 * t + 2, :], bhot[:, 2 * t:2 * t + 2, :], tokid[:, t:t + 1], None, ALU.mult)
                ins.then_inc(s["plan_v"], 1)
                ve.memset(ysb[:, :], 0.0)
                ve.memset(spread[:, :], 0.0).then_inc(s["spread_in"], 1)
                dve.wait_ge(s["plan_p"], 3 * L + 3)
                st.then(ve.tensor_copy(slot_gate[:, :], ps[:, 6, 32:32 + NPAIR]))
                st.then(ve.tensor_copy(idx[:, :], ps[:, 6, 0:NPAIR]))
                ve.tensor_copy(slot_tok[:, :], idx[:, :]).then_inc(s["slots_in"], 1)
                experts_of(2, NBLK)
                st.then(ve.tensor_scalar(cmp[:, 0:NBLK // 2], io[:, 0:NBLK // 2], 2.0, pend[:, NX - 1:NX], ALU.mult, ALU.is_lt))
                st.then(ve.tensor_reduce(nitf[:, 0:1], cmp[:, 0:NBLK // 2], AX.X, ALU.add))
                ve.tensor_copy(nit[:, 0:1], nitf[:, 0:1]).then_inc(s["plan_v"], 1)
                dve.wait_ge(s["plan_v"], PLAN_V * (L + 1))
                trips = dve.value_load(nit[0:1, 0:1], min_val=MIN_TRIPS, max_val=MAX_TRIPS)
                dve.wait_ge(s["spread_in"], pairs + (L + 1))

                def take_rows(turned):
                    dve.wait_ge(s["xg_turned"], turned)
                    ve.tensor_copy(xgT[:, :, :], ps[:, 0:2, :].rearrange("p b (k c) -> p (b k) c", k=4)).then_inc(s["xgT_in"], 1)

                take_rows(pairs + (L + 2))
                with dve.Fori(0, trips) as i:
                    for k in range(KD):
                        dve.wait_ge(s["added"], i * 8 + (pairs * 8 + (8 * L + k + 1)))
                        ve.tensor_tensor(XT[:, k, :], ps[:, (5, 7)[k % 2], :], XT[:, k, :], ALU.add).then_inc(s["add_in"], 1)
                    ve.tensor_scalar(spread[:, :], io[:, :], slot_tok[:, bass.ds(i, 1)], slot_gate[:, bass.ds(i, 1)],
                                     ALU.is_equal, ALU.mult).then_inc(s["spread_in"], 1)
                    for b in range(2):
                        if b == 1:
                            take_rows(i + (pairs + (L + 3)))
                        dve.wait_ge(s["sl_in"], i * 2 + (pairs * 2 + (b + 1)))
                        ve.tensor_tensor(act_[b][:, :, :], ps[:, 4, :].rearrange("p (f c) -> p f c", f=4)[:, :, BLK:2 * BLK],
                                         sl[b][:, :, :], ALU.mult).then_inc(s["act_in"], 1)
                dve.wait_ge(s["add_in"], (trips + pairs) * 8 + 2)
                for k in range(KD):
                    dve.wait_ge(s["added"], (trips + pairs) * 8 + (8 * L + k + 1))
                    ve.tensor_tensor(XT[:, k, :], ps[:, (5, 7)[k % 2], :], XT[:, k, :], ALU.add).then_inc(s["xt_ready"], 1)
                return trips

            even()
            cross(0)
            pairs = moe(0, 0)
            odd()
            cross(1)
            moe(1, pairs)
            norm(XT, HT, SEQ, "norm_final", 0)


_INS = ["x", "mem", "norm_mix", "norm_xattn", "norm_moe", "norm_final", "ev_w_in", "ev_sinks", "ev_mu", "ev_w0", "ev_w2",
        "ev_a0", "ev_a2", "ev_g2", "ev_k_k", "ev_k_a", "ev_r_k", "ev_lnx_w", "ev_lnx_b", "ev_w_out", "od_w_in",
        "od_gate_up", "od_gate_b", "od_onorm", "od_w_out", "mem_norm", "mem_wk", "mem_wv", "xa_wq", "xa_wo",
        "moe_w_group", "moe_b_group", "moe_w_expert", "moe_b_expert", "moe_w1", "moe_w3", "moe_w2"]


def kernel(**inputs):
    import numpy as _np
    import concourse.bacc as _bacc
    from concourse import mybir as _mybir
    from concourse.bass_utils import run_bass_kernel_spmd as _run

    nc = _bacc.Bacc("TRN2", target_bir_lowering=False, num_devices=1)
    arrays, args = {}, {}
    for name in _INS:
        arr = _np.ascontiguousarray(inputs[name])
        arrays[f"in_{name}"] = arr
        args[name] = nc.dram_tensor(f"in_{name}", arr.shape, _mybir.dt.from_np(arr.dtype), kind="ExternalInput").ap()
    hrows = nc.dram_tensor("hrows", (SEQ, D), F32, kind="Internal").ap()
    out = nc.dram_tensor("out_0", (1, SEQ, D), F32, kind="ExternalOutput").ap()
    trunk(nc, args, hrows, out)
    r = _run(nc, [arrays], core_ids=[0])
    return r.results[0]["out_0"]
```
